# Optimizing a Trainium2 kernel written in Bass

```python
import jax, jax.numpy as jnp
from jax import lax
import numpy as np

D_MODEL = 1024
BATCH = 1
SEQ = 256
DEPTH = 2

GRID_W = 64
CTX_LEN = 256
HEAD_DIM = 64
BLOCK = 128
MLP_GROUPS = 4
MLP_WIDTH = MLP_GROUPS * HEAD_DIM
WIN_HEADS = 4
WIN_KV = 2
WINDOW = 128
GLB_HEADS = 4
GLB_KV = 2
RET_HEADS = 4
RET_VDIM = HEAD_DIM
N_BRANCH = 4
BRANCH_W = 256
ROPE_BASE = 10000.0
D_FF = 2816
N_EXPERTS = 8
TOP_K = 2
D_FF_EXPERT = 1792
N_DENSE = (DEPTH + 1) // 2
N_MOE = DEPTH // 2
EPS = 1e-6
NEG_INF = -1e30
IN_SPLITS = (2 * MLP_WIDTH,
             WIN_HEADS * HEAD_DIM, WIN_KV * HEAD_DIM, WIN_KV * HEAD_DIM,
             GLB_HEADS * HEAD_DIM, GLB_KV * HEAD_DIM, GLB_KV * HEAD_DIM,
             RET_HEADS * HEAD_DIM, RET_HEADS * HEAD_DIM, RET_HEADS * RET_VDIM, RET_HEADS * RET_VDIM,
             N_BRANCH * D_MODEL)
IN_WIDTH = sum(IN_SPLITS)

kernel_name = 'hybrid_parallel_mixer_dit'

def rms_norm(x, g):
    xf = x.astype(jnp.float32)
    y = xf * lax.rsqrt(jnp.mean(xf * xf, axis=-1, keepdims=True) + EPS)
    return (y * g.astype(jnp.float32)).astype(x.dtype)

def group_norm(x, g):
    xf = x.astype(jnp.float32)
    xc = xf - jnp.mean(xf, axis=-1, keepdims=True)
    var = jnp.mean(xc * xc, axis=-1, keepdims=True)
    return xc * lax.rsqrt(var + EPS) * g.astype(jnp.float32)

def heads(t, n, dh=HEAD_DIM):
    return t.reshape(t.shape[0], t.shape[1], n, dh)

def split_cols(p):
    parts = []
    off = 0
    for n in IN_SPLITS:
        parts.append(p[..., off:off + n])
        off += n
    return parts

def rope(x, tables):
    cos, sin = tables
    half = x.shape[-1] // 2
    x1 = x[..., :half].astype(jnp.float32)
    x2 = x[..., half:].astype(jnp.float32)
    c = cos[:, None, :]
    s = sin[:, None, :]
    return jnp.concatenate([x1 * c - x2 * s, x1 * s + x2 * c], axis=-1).astype(x.dtype)

def axial_rope_tables(n_rows):
    row = jnp.repeat(jnp.arange(n_rows, dtype=jnp.float32), GRID_W)
    col = jnp.tile(jnp.arange(GRID_W, dtype=jnp.float32), n_rows)
    n_freq = HEAD_DIM // 4
    inv = ROPE_BASE ** (-jnp.arange(n_freq, dtype=jnp.float32) / n_freq)
    ang = jnp.concatenate([row[:, None] * inv, col[:, None] * inv], axis=-1)
    return jnp.cos(ang), jnp.sin(ang)

def seq_rope_tables(pos):
    n_freq = HEAD_DIM // 2
    inv = ROPE_BASE ** (-jnp.arange(n_freq, dtype=jnp.float32) / n_freq)
    ang = pos[:, None] * inv
    return jnp.cos(ang), jnp.sin(ang)

def chunk_mlp(uv, w_s, b_s, g_v):
    Bn, N, _ = uv.shape
    u, v = jnp.split(uv, 2, axis=-1)
    v = rms_norm(heads(v, MLP_GROUPS), g_v)
    v = v.reshape(Bn, N // BLOCK, BLOCK, MLP_GROUPS, HEAD_DIM)
    mixed = jnp.einsum('gij,bcjgd->bcigd', w_s, v) + b_s.T[None, None, :, :, None]
    return u * mixed.reshape(Bn, N, MLP_WIDTH)

def dense_attn(q, k, v, sink):
    Bn, N, Hq, d = q.shape
    Hkv = k.shape[2]
    G = Hq // Hkv
    qg = q.reshape(Bn, N, Hkv, G, d)
    s = jnp.einsum('bqhgd,bkhd->bhgqk', qg, k).astype(jnp.float32) * (d ** -0.5)
    if sink is not None:
        sk = jnp.broadcast_to(sink.astype(jnp.float32).reshape(1, Hkv, G, 1, 1), s.shape[:-1] + (1,))
        p = jax.nn.softmax(jnp.concatenate([s, sk], axis=-1), axis=-1)[..., :-1]
    else:
        p = jax.nn.softmax(s, axis=-1)
    o = jnp.einsum('bhgqk,bkhd->bqhgd', p.astype(v.dtype), v)
    return o.reshape(Bn, N, Hq * d)

def window_attn_latent(q, k, v, k_c, v_c, sink):
    Bn, S, Hq, d = q.shape
    Hkv = k.shape[2]
    G = Hq // Hkv
    nb = S // BLOCK
    L = k_c.shape[1]
    scale = d ** -0.5
    qb = q.reshape(Bn, nb, BLOCK, Hkv, G, d)
    pad = jnp.zeros((Bn, BLOCK, Hkv, d), k.dtype)
    kp = jnp.concatenate([pad, k, pad], axis=1).reshape(Bn, nb + 2, BLOCK, Hkv, d)
    vp = jnp.concatenate([pad, v, pad], axis=1).reshape(Bn, nb + 2, BLOCK, Hkv, d)
    kw = jnp.concatenate([kp[:, :-2], kp[:, 1:-1], kp[:, 2:]], axis=2)
    vw = jnp.concatenate([vp[:, :-2], vp[:, 1:-1], vp[:, 2:]], axis=2)
    qpos = jnp.arange(nb)[:, None] * BLOCK + jnp.arange(BLOCK)[None, :]
    kpos = jnp.arange(nb)[:, None] * BLOCK - BLOCK + jnp.arange(3 * BLOCK)[None, :]
    valid = (jnp.abs(qpos[:, :, None] - kpos[:, None, :]) <= WINDOW) & (kpos[:, None, :] >= 0) & (kpos[:, None, :] < S)
    s_loc = jnp.einsum('bnqhgd,bnkhd->bnhgqk', qb, kw).astype(jnp.float32) * scale
    s_loc = jnp.where(valid[None, :, None, None], s_loc, NEG_INF)
    s_ctx = jnp.einsum('bnqhgd,bkhd->bnhgqk', qb, k_c).astype(jnp.float32) * scale
    s_sink = jnp.broadcast_to(sink.astype(jnp.float32).reshape(1, 1, Hkv, G, 1, 1), s_ctx.shape[:-1] + (1,))
    p = jax.nn.softmax(jnp.concatenate([s_ctx, s_loc, s_sink], axis=-1), axis=-1).astype(v.dtype)
    o = (jnp.einsum('bnhgqk,bkhd->bnqhgd', p[..., :L], v_c)
         + jnp.einsum('bnhgqk,bnkhd->bnqhgd', p[..., L:L + 3 * BLOCK], vw))
    return o.reshape(Bn, S, Hq * d)

def global_attn_latent(q, k_all, v_all):
    Bn, S, Hq, d = q.shape
    Hkv = k_all.shape[2]
    G = Hq // Hkv
    nb = S // BLOCK
    scale = d ** -0.5
    qb = q.reshape(Bn, nb, BLOCK, Hkv, G, d).transpose(1, 0, 2, 3, 4, 5)

    def one_block(qblk):
        s = jnp.einsum('bqhgd,bkhd->bhgqk', qblk, k_all).astype(jnp.float32) * scale
        p = jax.nn.softmax(s, axis=-1).astype(v_all.dtype)
        return jnp.einsum('bhgqk,bkhd->bqhgd', p, v_all)

    o = lax.map(one_block, qb)
    return o.transpose(1, 0, 2, 3, 4, 5).reshape(Bn, S, Hq * d)

def retention_scan(q, k, v, log_gamma, s0, shift):
    Bn, N, H, dk = q.shape
    dv = v.shape[-1]
    nc = N // BLOCK
    idx = jnp.arange(BLOCK, dtype=jnp.float32)
    rel = idx[:, None] - idx[None, :] - shift
    mask = rel >= 0
    decay_in = jnp.where(mask[None], jnp.exp(log_gamma[:, None, None] * jnp.where(mask, rel, 0.0)[None]), 0.0)
    q_dec = jnp.exp(log_gamma[:, None] * (idx + 1.0 - shift)[None, :])
    k_dec = jnp.exp(log_gamma[:, None] * (BLOCK - 1.0 - idx)[None, :])
    chunk_dec = jnp.exp(log_gamma * BLOCK)[None, :, None, None]

    def to_chunks(t):
        return t.astype(jnp.float32).reshape(Bn, nc, BLOCK, H, t.shape[-1]).transpose(1, 0, 3, 2, 4)

    def step(state, inp):
        qc, kc, vc = inp
        qk = jnp.einsum('bhqd,bhkd->bhqk', qc, kc) * decay_in
        o = jnp.einsum('bhqk,bhkv->bhqv', qk, vc) + jnp.einsum('bhqd,bhdv->bhqv', qc * q_dec[..., None], state)
        state = chunk_dec * state + jnp.einsum('bhkd,bhkv->bhdv', kc * k_dec[..., None], vc)
        return state, o

    state, o = lax.scan(step, s0, (to_chunks(q), to_chunks(k), to_chunks(v)))
    return o.transpose(1, 0, 3, 2, 4).reshape(Bn, N, H, dv), state

def retention_out(o, g, gate_cols):
    y = group_norm(o, g)
    y = y.reshape(o.shape[0], o.shape[1], -1) * jax.nn.silu(gate_cols.astype(jnp.float32))
    return y.astype(gate_cols.dtype)

def merge(branches, gate_cols, w_branch, w_out):
    gates = jax.nn.sigmoid(gate_cols.reshape(gate_cols.shape[:-1] + (N_BRANCH, D_MODEL)))
    acc = gates[..., 0, :] * (branches[0] @ w_branch[0])
    for i in range(1, N_BRANCH):
        acc = acc + gates[..., i, :] * (branches[i] @ w_branch[i])
    return acc @ w_out

def token_mixers(h_ctx, h_lat, w_in, mlp_g_v, mlp_w_s, mlp_b_s, win_q_norm, win_k_norm, win_sink,
                 glb_q_norm, glb_k_norm, ret_decay, ret_gn, w_branch, w_out, axial, rot_ctx, rot_lat, need_ctx):
    pl = split_cols(h_lat @ w_in)
    pc = split_cols(h_ctx @ w_in)
    a_lat = chunk_mlp(jax.nn.gelu(pl[0]), mlp_w_s, mlp_b_s, mlp_g_v)
    wk_c = rms_norm(heads(pc[2], WIN_KV), win_k_norm)
    wv_c = heads(pc[3], WIN_KV)
    wq_l = rope(rms_norm(heads(pl[1], WIN_HEADS), win_q_norm), axial)
    wk_l = rope(rms_norm(heads(pl[2], WIN_KV), win_k_norm), axial)
    b_lat = window_attn_latent(wq_l, wk_l, heads(pl[3], WIN_KV), wk_c, wv_c, win_sink)
    gk_c = rms_norm(heads(pc[5], GLB_KV), glb_k_norm)
    gv_c = heads(pc[6], GLB_KV)
    gq_l = rope(rms_norm(heads(pl[4], GLB_HEADS), glb_q_norm), axial)
    gk_l = rope(rms_norm(heads(pl[5], GLB_KV), glb_k_norm), axial)
    c_lat = global_attn_latent(gq_l, jnp.concatenate([gk_c, gk_l], axis=1),
                               jnp.concatenate([gv_c, heads(pl[6], GLB_KV)], axis=1))
    k_scale = HEAD_DIM ** -0.5
    rq_c = rope(heads(pc[7], RET_HEADS), rot_ctx)
    rk_c = rope(heads(pc[8], RET_HEADS), rot_ctx) * k_scale
    rv_c = heads(pc[9], RET_HEADS, RET_VDIM)
    rq_l = rope(heads(pl[7], RET_HEADS), rot_lat)
    rk_l = rope(heads(pl[8], RET_HEADS), rot_lat) * k_scale
    rv_l = heads(pl[9], RET_HEADS, RET_VDIM)
    log_g = jax.nn.log_sigmoid(ret_decay.astype(jnp.float32))
    s0 = jnp.zeros((h_lat.shape[0], RET_HEADS, HEAD_DIM, RET_VDIM), jnp.float32)
    flip = lambda t: jnp.flip(t, axis=1)
    oc_f, st_f = retention_scan(rq_c, rk_c, rv_c, log_g[0], s0, 0)
    oc_b, st_b = retention_scan(flip(rq_c), flip(rk_c), flip(rv_c), log_g[1], s0, 1)
    ol_f, _ = retention_scan(rq_l, rk_l, rv_l, log_g[0], st_f, 0)
    ol_b, _ = retention_scan(flip(rq_l), flip(rk_l), flip(rv_l), log_g[1], st_b, 1)
    d_lat = retention_out(ol_f + flip(ol_b), ret_gn, pl[10])
    m_lat = merge((a_lat, b_lat, c_lat, d_lat), pl[11], w_branch, w_out)
    if not need_ctx:
        return None, m_lat
    a_ctx = chunk_mlp(jax.nn.gelu(pc[0]), mlp_w_s, mlp_b_s, mlp_g_v)
    b_ctx = dense_attn(rms_norm(heads(pc[1], WIN_HEADS), win_q_norm), wk_c, wv_c, win_sink)
    c_ctx_out = dense_attn(rms_norm(heads(pc[4], GLB_HEADS), glb_q_norm), gk_c, gv_c, None)
    d_ctx = retention_out(oc_f + flip(oc_b), ret_gn, pc[10])
    m_ctx = merge((a_ctx, b_ctx, c_ctx_out, d_ctx), pc[11], w_branch, w_out)
    return m_ctx, m_lat

def swiglu(h, w1, w3, w2):
    return (jax.nn.silu(h @ w1) * (h @ w3)) @ w2

def moe_swiglu(h, router_w, router_b, w1, w3, w2):
    logits = (h @ router_w + router_b).astype(jnp.float32)
    top_v, top_i = lax.top_k(logits, TOP_K)
    p = jax.nn.softmax(top_v, axis=-1)
    combine = jnp.sum(jax.nn.one_hot(top_i, N_EXPERTS, dtype=jnp.float32) * p[..., None], axis=-2)
    out = combine[..., 0:1].astype(h.dtype) * swiglu(h, w1[0], w3[0], w2[0])
    for e in range(1, N_EXPERTS):
        out = out + combine[..., e:e + 1].astype(h.dtype) * swiglu(h, w1[e], w3[e], w2[e])
    return out

def channel_mixer(h, layer, ffn_w1, ffn_w3, ffn_w2, router_w, router_b, moe_w1, moe_w3, moe_w2):
    j = layer // 2
    if layer % 2 == 0:
        return swiglu(h, ffn_w1[j], ffn_w3[j], ffn_w2[j])
    return moe_swiglu(h, router_w[j], router_b[j], moe_w1[j], moe_w3[j], moe_w2[j])

def setup_inputs(seed: int = 0) -> dict:
    key = jax.random.key(seed)
    ks = jax.random.split(key, 32)
    D = D_MODEL

    def nrm(k, shape, s):
        return jax.random.normal(k, shape, jnp.float32) * s

    gam = 1.0 - 2.0 ** (-5.0 - jnp.arange(RET_HEADS, dtype=jnp.float32))
    decay_logit = jnp.log(gam) - jnp.log1p(-gam)
    return {
        'x': nrm(ks[0], (BATCH, SEQ, D), 1.0),
        'c': nrm(ks[1], (BATCH, D), 1.0),
        'ctx': nrm(ks[2], (BATCH, CTX_LEN, D), 1.0),
        'c_ctx': nrm(ks[3], (D,), 1.0),
        'w_mod': nrm(ks[4], (DEPTH, D, 6 * D), 0.5 * D ** -0.5),
        'b_mod': nrm(ks[5], (DEPTH, 6 * D), 0.02),
        'g_norm1': 1.0 + nrm(ks[6], (DEPTH, D), 0.02),
        'g_norm2': 1.0 + nrm(ks[7], (DEPTH, D), 0.02),
        'w_in': nrm(ks[8], (DEPTH, D, IN_WIDTH), D ** -0.5),
        'mlp_g_v': 1.0 + nrm(ks[9], (DEPTH, MLP_GROUPS, HEAD_DIM), 0.02),
        'mlp_w_s': nrm(ks[10], (DEPTH, MLP_GROUPS, BLOCK, BLOCK), BLOCK ** -0.5),
        'mlp_b_s': 1.0 + nrm(ks[11], (DEPTH, MLP_GROUPS, BLOCK), 0.1),
        'win_q_norm': 1.0 + nrm(ks[12], (DEPTH, HEAD_DIM), 0.02),
        'win_k_norm': 1.0 + nrm(ks[13], (DEPTH, HEAD_DIM), 0.02),
        'win_sink': nrm(ks[14], (DEPTH, WIN_HEADS), 0.5),
        'glb_q_norm': 1.0 + nrm(ks[15], (DEPTH, HEAD_DIM), 0.02),
        'glb_k_norm': 1.0 + nrm(ks[16], (DEPTH, HEAD_DIM), 0.02),
        'ret_decay': decay_logit[None, None, :] + nrm(ks[17], (DEPTH, 2, RET_HEADS), 0.1),
        'ret_gn': 1.0 + nrm(ks[18], (DEPTH, RET_HEADS, RET_VDIM), 0.02),
        'w_branch': nrm(ks[19], (DEPTH, N_BRANCH, BRANCH_W, D), BRANCH_W ** -0.5),
        'w_out': nrm(ks[20], (DEPTH, D, D), D ** -0.5),
        'ffn_w1': nrm(ks[21], (N_DENSE, D, D_FF), D ** -0.5),
        'ffn_w3': nrm(ks[22], (N_DENSE, D, D_FF), D ** -0.5),
        'ffn_w2': nrm(ks[23], (N_DENSE, D_FF, D), D_FF ** -0.5),
        'router_w': nrm(ks[24], (N_MOE, D, N_EXPERTS), D ** -0.5),
        'router_b': nrm(ks[25], (N_MOE, N_EXPERTS), 0.01),
        'moe_w1': nrm(ks[26], (N_MOE, N_EXPERTS, D, D_FF_EXPERT), D ** -0.5),
        'moe_w3': nrm(ks[27], (N_MOE, N_EXPERTS, D, D_FF_EXPERT), D ** -0.5),
        'moe_w2': nrm(ks[28], (N_MOE, N_EXPERTS, D_FF_EXPERT, D), D_FF_EXPERT ** -0.5),
    }

def reference(x, c, ctx, c_ctx, w_mod, b_mod, g_norm1, g_norm2, w_in, mlp_g_v, mlp_w_s, mlp_b_s,
              win_q_norm, win_k_norm, win_sink, glb_q_norm, glb_k_norm, ret_decay, ret_gn, w_branch, w_out,
              ffn_w1, ffn_w3, ffn_w2, router_w, router_b, moe_w1, moe_w3, moe_w2):
    S = x.shape[1]
    L = ctx.shape[1]
    n_rows = S // GRID_W
    axial = axial_rope_tables(n_rows)
    rot_ctx = seq_rope_tables(jnp.arange(L, dtype=jnp.float32))
    rot_lat = seq_rope_tables(L + jnp.arange(S, dtype=jnp.float32))
    silu_c = jax.nn.silu(c)
    silu_cc = jax.nn.silu(c_ctx)[None, :]
    for layer in range(DEPTH):
        need_ctx = layer < DEPTH - 1
        mod_l = (silu_c @ w_mod[layer] + b_mod[layer])[:, None, :]
        mod_c = (silu_cc @ w_mod[layer] + b_mod[layer])[:, None, :]
        sh1_l, sc1_l, g1_l, sh2_l, sc2_l, g2_l = jnp.split(mod_l, 6, axis=-1)
        sh1_c, sc1_c, g1_c, sh2_c, sc2_c, g2_c = jnp.split(mod_c, 6, axis=-1)
        h_l = rms_norm(x, g_norm1[layer]) * (1.0 + sc1_l) + sh1_l
        h_c = rms_norm(ctx, g_norm1[layer]) * (1.0 + sc1_c) + sh1_c
        m_c, m_l = token_mixers(h_c, h_l, w_in[layer], mlp_g_v[layer], mlp_w_s[layer], mlp_b_s[layer],
                                win_q_norm[layer], win_k_norm[layer], win_sink[layer],
                                glb_q_norm[layer], glb_k_norm[layer], ret_decay[layer], ret_gn[layer],
                                w_branch[layer], w_out[layer], axial, rot_ctx, rot_lat, need_ctx)
        x = x + g1_l * m_l
        h_l = rms_norm(x, g_norm2[layer]) * (1.0 + sc2_l) + sh2_l
        x = x + g2_l * channel_mixer(h_l, layer, ffn_w1, ffn_w3, ffn_w2, router_w, router_b, moe_w1, moe_w3, moe_w2)
        if need_ctx:
            ctx = ctx + g1_c * m_c
            h_c = rms_norm(ctx, g_norm2[layer]) * (1.0 + sc2_c) + sh2_c
            ctx = ctx + g2_c * channel_mixer(h_c, layer, ffn_w1, ffn_w3, ffn_w2, router_w, router_b, moe_w1, moe_w3, moe_w2)
    return x


_drawn_inputs = setup_inputs


def setup_inputs(seed=0):
    import zlib

    import numpy as np

    out = dict(_drawn_inputs(seed))
    spreads = {}
    factors = {'g_norm1': 3.313,
     'g_norm2': 3.001,
     'mlp_g_v': 7.361,
     'win_q_norm': 8.0,
     'win_k_norm': 8.0,
     'win_sink': 8.0,
     'glb_q_norm': 8.0,
     'glb_k_norm': 8.0,
     'ret_gn': 5.915,
     'router_b': 15.171}
    for name, (base, spread) in spreads.items():
        noise = np.random.default_rng([zlib.crc32(name.encode()), seed]).standard_normal(out[name].shape)
        drawn = base * np.exp(spread * noise) if base else spread * noise
        out[name] = __import__('jax').numpy.asarray(drawn.astype(out[name].dtype))
    for name, factor in factors.items():
        out[name] = (out[name] * factor).astype(out[name].dtype)
    return out
```

```python
from contextlib import ExitStack

import numpy as np

import concourse.bass as bass
from concourse import mybir

F32 = mybir.dt.float32
F32R = mybir.dt.float32r
ALU = mybir.AluOpType
ACT = mybir.ActivationFunctionType
AX_X = mybir.AxisListType.X

P = 128
D = 1024
KC = D // P
SEQ = 256
CTX = 256
TOK = SEQ + CTX
NBLK = TOK // P
LBLK = SEQ // P
HD = 64
NH = 4
DEPTH = 2
MIX_W = 2560
COL_U, COL_V = 0, 256
COL_WQ, COL_WK, COL_WV = 512, 768, 896
COL_GQ, COL_GK, COL_GV = 1024, 1280, 1408
COL_RQ, COL_RK, COL_RV, COL_RG = 1536, 1792, 2048, 2304
OUT_COLS = (COL_U, COL_WQ, COL_GQ, COL_RQ)
NBR = 4
DFF = 2816
DFE = 1792
NEXP = 8
EPS = 1e-6
SCALE = HD ** -0.5
BIG = 1e30
UNIT = 2048
UC = UNIT // KC
MIX_UNITS = MIX_W // UC
GROUPS = D // UC
GROUP_UNITS = NBR + 1
OUT_UNITS = D // UC
MOD_UNITS = DEPTH * 6 * D // UC
MOD_RING = 4
FFN_PARTS = (12, 10)
EXP_CHUNKS = DFE // P
EXP_UNITS = EXP_CHUNKS + KC
UNITS0 = MIX_UNITS + GROUPS * GROUP_UNITS + OUT_UNITS + sum(FFN_PARTS) + 2 * KC
SH1, SC1, G1, SH2, SC2, G2 = range(6)
ds = bass.ds


def blocks_of(layer):
    return NBLK if layer < DEPTH - 1 else LBLK


def attention_items(layer):
    return [(h, b, 0, TOK) if b < LBLK else (h, b, SEQ, CTX) for b in range(blocks_of(layer)) for h in range(NH)]


def build_program(nc, t):
    with ExitStack() as ctx:
        base = 16512
        top = 229344 - 32
        place = {"at": base}
        ctx.enter_context(nc.sbuf_tensor("arena", [P, (top - base) // 4], F32))

        def at(name, shape, dt, offset):
            return nc.alloc_sbuf_tensor_at(name, shape, dt, offset=offset)

        def sb(name, shape, dt=F32):
            size = 4 * int(np.prod(shape[1:]))
            here = place["at"]
            place["at"] = here + (size + 31) // 32 * 32
            assert place["at"] <= top, name
            return at(name, shape, dt, here)

        def sem(name):
            return ctx.enter_context(nc.semaphore(name))

        raw = sb("raw", [P, 2, UNIT])
        whi = sb("whi", [P, 2, UNIT], F32R)
        wlo = sb("wlo", [P, 2, UNIT], F32R)
        xT = sb("xT", [P, KC, TOK])
        hhi = sb("hhi", [P, KC, TOK], F32R)
        hlo = sb("hlo", [P, KC, TOK], F32R)
        region = place["at"]
        mix = sb("mix", [P, NBLK, MIX_W])
        headsT = sb("headsT", [HD, 8, TOK])
        acchi = at("acchi", [P, KC, TOK], F32R, region)
        acclo = at("acclo", [P, KC, TOK], F32R, region + 4 * KC * TOK)
        hidhi = at("hidhi", [P, 12 * TOK], F32R, region)
        hidlo = at("hidlo", [P, 12 * TOK], F32R, region + 4 * 12 * TOK)
        modring = at("modring", [P, MOD_RING, KC, UC], F32, region)
        gates = at("gates", [P, NBR, 2, TOK], F32, region + 4 * NBLK * MIX_W)
        region2 = place["at"]
        brhi = sb("brhi", [P, KC, TOK], F32R)
        brlo = sb("brlo", [P, KC, TOK], F32R)
        xrows = at("xrows", [P, NBLK, D], F32, region2)
        hf = at("hf", [P, KC, TOK], F32, region2)
        scrA = at("scrA", [P, 1536], F32, region2)
        scrB = at("scrB", [P, 1536], F32, region2 + 4 * 1536)
        expS = at("expS", [P, 2, TOK], F32, region2 + 4 * 3072)
        expT = at("expT", [P, 2, TOK], F32, region2 + 4 * 4096)
        kdec = at("kdec", [P, 2, NBLK, NH * HD], F32, region2 + 4 * 5120)
        wsrow = at("wsrow", [P, NH, P], F32, region2 + 4 * 7168)
        wsT = at("wsT", [P, NH, P], F32, region2 + 4 * 7680)
        stateF = at("stateF", [HD, 3, NH * HD], F32, region2 + 4 * 7168)
        moe = at("moe", [P, KC, SEQ], F32, region2)
        combB = at("combB", [P, NEXP, SEQ], F32, region2 + 4 * 2048)
        rel = at("rel", [P, 4, P], F32, region2 + 4 * 4096)
        pick = at("pick", [NEXP, NEXP, P], F32, region2 + 4 * 4096)
        rout = at("rout", [P, 12, LBLK, NEXP], F32, region2 + 4 * 5120)
        combT = at("combT", [NEXP, SEQ], F32, region2 + 4 * 5632)
        rw = at("rw", [P, KC, NEXP], F32, region2 + 4 * 6144)
        rb = at("rb", [P, NEXP], F32, region2 + 4 * 6400)
        eidx = at("eidx", [P, NEXP], F32, region2 + 4 * 6432)
        tmp = sb("tmp", [P, 2, TOK])
        stateB = at("stateB", [HD, 3, NH * HD], F32, place["at"] - 4 * 2 * TOK)
        decay = sb("decay", [P, DEPTH, NH, P])
        ident = sb("ident", [P, P])
        ones = sb("ones", [P, P])
        rows1 = at("rows1", [P, P], F32, region2 + 4 * 6656)
        rows2 = at("rows2", [24, P], F32, region2 + 4 * 6784)
        idx = at("idx", [P, 4], F32, region2 + 4 * 6912)
        lgx = at("lgx", [P, 3, 16], F32, region2 + 4 * 6944)
        vecT = sb("vecT", [P, P])
        rowsT = sb("rowsT", [P, 24])
        siluc = sb("siluc", [P, KC, 2])
        mod = sb("mod", [P, DEPTH, 6, KC, 2])
        gsc = sb("gsc", [P, DEPTH, 2, KC, 2])
        wmask = sb("wmask", [P, 2, P])
        axial = sb("axial", [P, 2, LBLK, 32])
        rot = sb("rot", [P, 2, NBLK, 32])
        qkw = sb("qkw", [P, DEPTH, 4, HD])
        gv = sb("gv", [P, DEPTH, NH * HD])
        gn = sb("gn", [P, DEPTH, NH * HD])
        sink = sb("sink", [P, DEPTH * NH])
        nsink = sb("nsink", [P, DEPTH * NH])
        expcol = sb("expcol", [P, 4, DEPTH, 2, NH])
        stat = sb("stat", [P, 3, 24])
        negmax = sb("negmax", [P, 16])
        rowsum = sb("rowsum", [P, 16])
        sinkexp = sb("sinkexp", [P, 16])

        psA = ctx.enter_context(nc.psum_tensor("psA", [P, 4, 512], F32))
        psB = ctx.enter_context(nc.psum_tensor("psB", [P, 4, 512], F32))

        inputs_landed = sem("inputs_landed")
        late_landed = sem("late_landed")
        router_landed = sem("router_landed")
        mod_landed = [sem(f"mod_landed{s}") for s in range(MOD_RING)]
        mod_used = sem("mod_used")
        ones_set = sem("ones_set")
        setup_turned = sem("setup_turned")
        setup_copied = sem("setup_copied")
        silu_ready = sem("silu_ready")
        lg_steps = sem("lg_steps")
        lg_ready = sem("lg_ready")
        decay_exp = sem("decay_exp")
        decay_used = sem("decay_used")
        x_turned = sem("x_turned")
        x_placed = sem("x_placed")
        raw_landed = [sem(f"raw_landed{s}") for s in range(2)]
        hi_ready = sem("hi_ready")
        lo_ready = sem("lo_ready")
        w_used = sem("w_used")
        dve_step = sem("dve_step")
        act_step = sem("act_step")
        out_stored = sem("out_stored")
        out_placed = sem("out_placed")
        out_turned = sem("out_turned")
        squares = sem("squares")
        meansq = sem("meansq")
        ms_ready = sem("ms_ready")
        root_ready = sem("root_ready")
        xn_ready = sem("xn_ready")
        h_ready = sem("h_ready")
        h_split = sem("h_split")
        L = range(DEPTH)
        mix_taken = [sem(f"mix_taken{l}") for l in L]
        ws_turned = sem("ws_turned")
        ws_copied = sem("ws_copied")
        v_normed = sem("v_normed")
        mlp_mixed = sem("mlp_mixed")
        mlp_done = sem("mlp_done")
        heads_ready = sem("heads_ready")
        head_turned = [[sem(f"head_turned{l}{m}") for m in range(3)] for l in L]
        head_placed = [[sem(f"head_placed{l}{m}") for m in range(3)] for l in L]
        scores_ready = [[sem(f"scores_ready{l}{m}") for m in range(2)] for l in L]
        max_ready = [[sem(f"max_ready{l}{m}") for m in range(2)] for l in L]
        exp_ready = [[sem(f"exp_ready{l}{m}") for m in range(2)] for l in L]
        probs_turned = [[sem(f"probs_turned{l}{m}") for m in range(2)] for l in L]
        probs_placed = [[sem(f"probs_placed{l}{m}") for m in range(2)] for l in L]
        values_ready = [[sem(f"values_ready{l}{m}") for m in range(2)] for l in L]
        attn_done = [[sem(f"attn_done{l}{m}") for m in range(2)] for l in L]
        kdec_ready = sem("kdec_ready")
        kv_ready = sem("kv_ready")
        states_ready = sem("states_ready")
        qk_ready = [sem(f"qk_ready{l}") for l in L]
        qk_decayed = [sem(f"qk_decayed{l}") for l in L]
        ret_ready = [sem(f"ret_ready{l}") for l in L]
        ret_taken = [sem(f"ret_taken{l}") for l in L]
        branches_ready = sem("branches_ready")
        br_turned = [sem(f"br_turned{l}") for l in L]
        br_hi = [sem(f"br_hi{l}") for l in L]
        br_lo = [sem(f"br_lo{l}") for l in L]
        gates_taken = [sem(f"gates_taken{l}") for l in L]
        gates_used = [sem(f"gates_used{l}") for l in L]
        proj_ready = [sem(f"proj_ready{l}") for l in L]
        proj_taken = [sem(f"proj_taken{l}") for l in L]
        acc_ready = [sem(f"acc_ready{l}") for l in L]
        out_taken = [sem(f"out_taken{l}") for l in L]
        up_silu = [sem(f"up_silu{k}") for k in range(3)]
        up_taken = [sem(f"up_taken{k}") for k in range(3)]
        down_ready = [sem(f"down_ready{k}") for k in range(3)]
        down_taken = [sem(f"down_taken{k}") for k in range(3)]
        router_ready = sem("router_ready")
        combine_ready = sem("combine_ready")
        combine_turned = sem("combine_turned")
        combine_copied = sem("combine_copied")
        comb_spread = sem("comb_spread")
        gap_ready = sem("gap_ready")
        gap_exp = sem("gap_exp")
        x_final = sem("x_final")
        mod_ready = sem("mod_ready")

        first_mix = [0, UNITS0]
        first_group = [u + MIX_UNITS for u in first_mix]
        first_out = [u + GROUPS * GROUP_UNITS for u in first_group]
        first_ffn = [u + OUT_UNITS for u in first_out]
        first_part = [first_ffn[0], first_ffn[0] + FFN_PARTS[0] + KC]
        first_exp = first_ffn[1]

        ROOTS = 6
        NORM1, ROOT_V, ROOT_W, ROOT_G, ROOT_GN, NORM2 = range(ROOTS)
        setup_loads = []

        block = ctx.enter_context(nc.Block())

        @block.sync
        def _(sp):
            def load(dst, src):
                setup_loads.append(1)
                sp.dma_start(dst, src).then_inc(inputs_landed, 16)

            load(rows1[0:96, :], t["b_mod"].rearrange("l (c p) -> (l c) p", p=P))
            load(rows1[96:112, :], t["g_norm1"].rearrange("l (c p) -> (l c) p", p=P))
            load(rows1[112:128, :], t["g_norm2"].rearrange("l (c p) -> (l c) p", p=P))
            load(rows2[0:8, :], t["c"].rearrange("b (c p) -> (b c) p", p=P))
            load(rows2[8:16, :], t["c_ctx"].rearrange("(c p) -> c p", p=P))
            load(rows2[16:24, :], t["mlp_b_s"].rearrange("l g p -> (l g) p"))
            load(ident[:], t["k_ident"])
            load(xrows[:, 0:LBLK, :], t["x"].rearrange("b (n p) d -> p (b n) d", p=P))
            load(xrows[:, LBLK:NBLK, :], t["ctx"].rearrange("b (n p) d -> p (b n) d", p=P))
            load(wmask[:], t["k_wmask"])
            load(axial[:], t["k_axial"])
            load(rot[:], t["k_rot"])
            load(rel[:], t["k_rel"])
            load(idx[:], t["k_idx"])
            load(lgx[:, 0, :], t["ret_decay"].rearrange("l d h -> (l d h)").unsqueeze(0).broadcast_to([P, 16]))
            for l in range(DEPTH):
                for k, name in enumerate(("win_q_norm", "win_k_norm", "glb_q_norm", "glb_k_norm")):
                    load(qkw[:, l, k, :], t[name][l:l + 1, :].broadcast_to([P, HD]))
                load(gv[:, l, :], t["mlp_g_v"][l:l + 1].rearrange("l g d -> l (g d)").broadcast_to([P, NH * HD]))
                load(gn[:, l, :], t["ret_gn"][l:l + 1].rearrange("l g d -> l (g d)").broadcast_to([P, NH * HD]))
            load(sink[:], t["win_sink"].rearrange("l h -> (l h)").unsqueeze(0).broadcast_to([P, DEPTH * NH]))

            per = MOD_UNITS // DEPTH
            for l in range(DEPTH):
                w = t["w_mod"][l].rearrange("(c p) n -> p c n", p=P)
                if l == 0:
                    for s in range(MOD_RING):
                        sp.dma_start(modring[:, s], w[:, :, s * UC:(s + 1) * UC]).then_inc(mod_landed[s], 16)
                with sp.Fori(1 if l == 0 else 0, per // MOD_RING) as i:
                    for s in range(MOD_RING):
                        sp.wait_ge(mod_used, i * MOD_RING + (l * per + s + 1 - MOD_RING))
                        sp.dma_start(modring[:, s], w[:, :, ds(i * (MOD_RING * UC) + s * UC, UC)]).then_inc(mod_landed[s], 16)

            def unit_loads(slot, first, second):
                for dst, src in (first, second):
                    sp.dma_start(dst, src).then_inc(raw_landed[slot], 16)

            def square(slot, w, col):
                dst = raw[:, slot].rearrange("p (c n) -> p c n", c=KC)
                src = w.rearrange("(c p) n -> p c n", p=P)
                half = KC // 2
                unit_loads(slot, (dst[:, half:KC], src[:, half:KC, ds(col, UC)]), (dst[:, 0:half], src[:, 0:half, ds(col, UC)]))

            def up(slot, w1, w3, col):
                dst = raw[:, slot].rearrange("p (w c n) -> p w c n", w=2, c=KC)
                unit_loads(slot, (dst[:, 0], w1[:, ds(col, P)].rearrange("(c p) n -> p c n", p=P)),
                           (dst[:, 1], w3[:, ds(col, P)].rearrange("(c p) n -> p c n", p=P)))

            def down(slot, w2, rows, col):
                dst = raw[:, slot, 0:rows * P].rearrange("p (c n) -> p c n", c=rows)
                src = w2.rearrange("(c p) n -> p c n", p=P)
                h = rows // 2
                unit_loads(slot, (dst[:, 0:h], src[:, 0:h, ds(col, P)]), (dst[:, h:rows], src[:, h:rows, ds(col, P)]))

            def slot_split(n):
                sp.wait_ge(lo_ready, n - 1)

            for l in range(DEPTH):
                w = t["w_in"][l]
                if l == 0:
                    square(0, w, 0)
                    square(1, w, UC)
                with sp.Fori(1 if l == 0 else 0, MIX_UNITS // 2) as i:
                    for s in range(2):
                        slot_split(i * 2 + (first_mix[l] + s))
                        square(s, w, i * (2 * UC) + s * UC)
                sp.wait_ge(h_split, 2 * l * KC + KC)
                sp.dma_start(wsrow[:], t["mlp_w_s"][l].rearrange("g i j -> i g j")).then_inc(late_landed, 16)
                with sp.Fori(0, GROUPS // 2) as i:
                    for j in range(2 * GROUP_UNITS):
                        slot_split(i * (2 * GROUP_UNITS) + (first_group[l] + j))
                        g, u = divmod(j, GROUP_UNITS)
                        if u < NBR:
                            square(j % 2, w, i * (2 * UC) + (MIX_W + u * D + g * UC))
                        else:
                            square(j % 2, t["w_branch"][l].rearrange("b r n -> (b r) n"), i * (2 * UC) + g * UC)
                with sp.Fori(0, OUT_UNITS // 2) as i:
                    for s in range(2):
                        slot_split(i * 2 + (first_out[l] + s))
                        square(s, t["w_out"][l], i * (2 * UC) + s * UC)
                if l == 0:
                    done = 0
                    for k, chunks in enumerate(FFN_PARTS):
                        w1 = t["ffn_w1"][0][:, done * P:(done + chunks) * P]
                        w3 = t["ffn_w3"][0][:, done * P:(done + chunks) * P]
                        w2 = t["ffn_w2"][0][done * P:(done + chunks) * P, :]
                        done += chunks
                        with sp.Fori(0, chunks // 2) as i:
                            for s in range(2):
                                slot_split(i * 2 + (first_part[k] + s))
                                up(s, w1, w3, i * (2 * P) + s * P)
                        with sp.Fori(0, KC // 2) as i:
                            for s in range(2):
                                slot_split(i * 2 + (first_part[k] + chunks + s))
                                down(s, w2, chunks, i * (2 * P) + s * P)
                else:
                    with sp.Fori(0, NEXP) as e:
                        w1, w3, w2 = (t[name][0][ds(e, 1)].rearrange("o r n -> (o r) n")
                                      for name in ("moe_w1", "moe_w3", "moe_w2"))
                        with sp.Fori(0, EXP_CHUNKS // 2) as i:
                            for s in range(2):
                                slot_split(e * EXP_UNITS + i * 2 + (first_exp + s))
                                up(s, w1, w3, i * (2 * P) + s * P)
                        with sp.Fori(0, KC // 2) as i:
                            for s in range(2):
                                slot_split(e * EXP_UNITS + i * 2 + (first_exp + EXP_CHUNKS + s))
                                down(s, w2, EXP_CHUNKS, i * (2 * P) + s * P)

            sp.wait_ge(out_placed, KC)
            sp.dma_start(t["out"].rearrange("b (n p) d -> p (b n) d", p=P), xrows[:, 0:LBLK, :]).then_inc(out_stored, 16)
            sp.wait_ge(out_stored, 16)

        loaded = 16 * len(setup_loads)

        class Steps:

            def __init__(self, eng, semaphore):
                self.eng, self.semaphore, self.base, self.n = eng, semaphore, None, 0

            def __call__(self, ins):
                self.n += 1
                ins.then_inc(self.semaphore, 1)
                self.eng.wait_ge(self.semaphore, self.n if self.base is None else self.base + self.n)

            def loop(self, done, per):
                self.base, self.start = done * per, self.n

            def end(self, turns, per):
                assert self.n - self.start == per, (self.n - self.start, per)
                self.base, self.n = None, self.start + turns * per

        @block.tensor
        def _(pe):
            def mm(out, lhsT, rhs, start=True, stop=True):
                return nc.tensor.matmul(out, lhsT, rhs, start=start, stop=stop)

            def mm3(out, a, b, start, stop):
                mm(out, a[0], b[0], start, False)
                mm(out, a[0], b[1], False, False)
                return mm(out, a[1], b[0], False, stop)

            def w(slot, col, n):
                return whi[:, slot, col:col + n], wlo[:, slot, col:col + n]

            def h(k, a, b):
                return hhi[:, k, a:b], hlo[:, k, a:b]

            pe.wait_ge(inputs_landed, loaded)
            pe.wait_ge(ones_set, 1)
            nc.tensor.transpose(psB[:, 0, 0:P], rows1[:], ident[:])
            nc.tensor.transpose(psB[:, 0, P:P + 24], rows2[:], ident[0:24, 0:24]).then_inc(setup_turned, 1)
            for c in range(KC):
                if c >= 4:
                    pe.wait_ge(x_placed, c - 3)
                for b in range(NBLK):
                    last = nc.tensor.transpose(psA[:, c % 4, b * P:(b + 1) * P], xrows[:, b, c * P:(c + 1) * P], ident[:])
                last.then_inc(x_turned, 1)
            pe.wait_ge(silu_ready, 1)
            with pe.Fori(0, MOD_UNITS // MOD_RING) as i:
                for s in range(MOD_RING):
                    pe.wait_ge(mod_landed[s], i * 16 + 16)
                    for j in range(UC // P):
                        col = (s * (UC // P) + j) * 2
                        for k in range(KC):
                            last = mm(psB[:, 3, ds(i * (MOD_RING * UC // P * 2) + col, 2)],
                                      modring[:, s, k, j * P:(j + 1) * P], siluc[:, k, :], k == 0, k == KC - 1)
                    last.then_inc(mod_used, 1)

            def norm(k, T):
                pe.wait_ge(squares, k * KC + KC)
                if k == 0:
                    pe.wait_ge(setup_copied, 1)
                for c in range(KC):
                    last = mm(psB[:, 0, 0:T], ones[:], hf[:, c, 0:T], c == 0, c == KC - 1)
                last.then_inc(meansq, 1)
                pe.wait_ge(h_split, k * KC + KC)

            def arrived(n):
                pe.wait_ge(lo_ready, n + 1)

            def two_chunks(slot, pair, b, T):
                for j in range(2):
                    for k in range(KC):
                        last = mm3(psA[:, 2 * pair + j, 0:T], w(slot, k * UC + j * P, P), b(k), k == 0, k == KC - 1)
                return last

            def turn_heads(l, m, heads, col):
                pe.wait_ge(heads_ready, 3 * l + m + 1)
                for j in range(heads):
                    if j >= 4:
                        pe.wait_ge(head_placed[l][m], j - 3)
                    for b in range(NBLK):
                        last = nc.tensor.transpose(psA[0:HD, j % 4, b * P:(b + 1) * P],
                                                   mix[:, b, col + j * HD:col + (j + 1) * HD], ident[:])
                    last.then_inc(head_turned[l][m], 1)
                pe.wait_ge(head_placed[l][m], heads)

            def attention(l, m, vcol):
                items = attention_items(l)
                n = len(items)
                for step in range(n + 2):
                    if step < n:
                        i = step
                        hd, b, k0, nk = items[i]
                        if i >= 2:
                            pe.wait_ge(exp_ready[l][m], i - 1)
                        mm(psB[:, i % 2, 0:nk], headsT[:, hd, b * P:(b + 1) * P],
                           headsT[:, NH + hd // 2, k0:k0 + nk]).then_inc(scores_ready[l][m], 1)
                    if 1 <= step <= n:
                        i = step - 1
                        hd, b, k0, nk = items[i]
                        pe.wait_ge(exp_ready[l][m], i + 1)
                        if i >= 2:
                            pe.wait_ge(probs_placed[l][m], i - 1)
                        for y in range(nk // P):
                            last = nc.tensor.transpose(psA[:, i % 2, y * P:(y + 1) * P],
                                                       expS[:, i % 2, y * P:(y + 1) * P], ident[:])
                        last.then_inc(probs_turned[l][m], 1)
                    if step >= 2:
                        i = step - 2
                        hd, b, k0, nk = items[i]
                        pe.wait_ge(probs_placed[l][m], i + 1)
                        if i >= 2:
                            pe.wait_ge(attn_done[l][m], i - 1)
                        v = vcol + (hd // 2) * HD
                        for y in range(nk // P):
                            last = mm(psB[:, 2 + i % 2, 0:HD], expT[:, i % 2, y * P:(y + 1) * P],
                                      mix[:, k0 // P + y, v:v + HD], y == 0, y == nk // P - 1)
                        last.then_inc(values_ready[l][m], 1)
                pe.wait_ge(attn_done[l][m], n)

            def retention(l):
                pe.wait_ge(kdec_ready, l + 1)
                for d, order in enumerate(((2, 3, 0), (3, 2, 1))):
                    for step, b in enumerate(order):
                        for hd in range(NH):
                            last = mm(psB[0:HD, 2 * d + step // 2, (step % 2) * 256 + hd * HD:(step % 2) * 256 + (hd + 1) * HD],
                                      kdec[:, d, b, hd * HD:(hd + 1) * HD], mix[:, b, COL_RV + hd * HD:COL_RV + (hd + 1) * HD])
                last.then_inc(kv_ready, 1)

                def qk(b):
                    if b >= 2:
                        pe.wait_ge(qk_decayed[l], b - 1)
                    for hd in range(NH):
                        last = mm(psA[:, b % 2, hd * P:(hd + 1) * P], headsT[:, NH + hd, b * P:(b + 1) * P],
                                  headsT[:, hd, b * P:(b + 1) * P])
                    last.then_inc(qk_ready[l], 1)

                before = ((1, 2), (2, 1), (None, 0), (0, None))
                qk(0)
                pe.wait_ge(states_ready, l + 1)
                for b in range(blocks_of(l)):
                    if b + 1 < blocks_of(l):
                        qk(b + 1)
                    pe.wait_ge(qk_decayed[l], b + 1)
                    if b >= 2:
                        pe.wait_ge(ret_taken[l], b - 1)
                    for hd in range(NH):
                        last = mm(psA[:, 2 + b % 2, hd * HD:(hd + 1) * HD], expS[:, b % 2, hd * P:(hd + 1) * P],
                                  mix[:, b, COL_RV + hd * HD:COL_RV + (hd + 1) * HD])
                    for d, state in enumerate((stateF, stateB)):
                        if before[b][d] is not None:
                            for hd in range(NH):
                                last = mm(psB[:, b % 2, d * 256 + hd * HD:d * 256 + (hd + 1) * HD],
                                          headsT[:, hd, b * P:(b + 1) * P], state[:, before[b][d], hd * HD:(hd + 1) * HD])
                    last.then_inc(ret_ready[l], 1)

            def feed_forward(k, chunks, T, at_unit, up_done, down_done):
                with pe.Fori(0, chunks // 2) as i:
                    for s in range(2):
                        if s == 0:
                            pe.wait_ge(down_taken[k], down_done + 2)
                        arrived(i * 2 + (at_unit + s))
                        pe.wait_ge(up_taken[k], i * 2 + (up_done + s + 1))
                        for j in range(2):
                            for c in range(KC):
                                last = mm3(psA[:, 2 * s + j, 0:T], w(s, (j * KC + c) * P, P), h(c, 0, T), c == 0, c == KC - 1)
                        last.then_inc(w_used, 1)
                with pe.Fori(0, KC // 2) as i:
                    for s in range(2):
                        if s == 0:
                            pe.wait_ge(up_taken[k], up_done + (chunks + 2))
                        arrived(i * 2 + (at_unit + (chunks + s)))
                        pe.wait_ge(down_taken[k], i * 2 + (down_done + s + 1))
                        for c in range(chunks):
                            last = mm3(psA[:, 2 * s, 0:T], w(s, c * P, P),
                                       (hidhi[:, c * T:(c + 1) * T], hidlo[:, c * T:(c + 1) * T]), c == 0, c == chunks - 1)
                        last.then_inc(w_used, 1)

            for l in range(DEPTH):
                T = blocks_of(l) * P
                norm(2 * l, TOK)
                with pe.Fori(0, MIX_UNITS // 2) as i:
                    for s in range(2):
                        arrived(i * 2 + (first_mix[l] + s))
                        pe.wait_ge(mix_taken[l], i * 2 + (s + 1))
                        for b in range(NBLK):
                            for k in range(KC):
                                last = mm3(psA[:, 2 * s + b // 2, (b % 2) * UC:(b % 2 + 1) * UC],
                                           h(k, b * P, (b + 1) * P), w(s, k * UC, UC), k == 0, k == KC - 1)
                        last.then_inc(w_used, 1)
                pe.wait_ge(mix_taken[l], MIX_UNITS + 2)
                pe.wait_ge(late_landed, 16 * (l + 1))
                for g in range(NH):
                    last = nc.tensor.transpose(psB[:, 0, g * P:(g + 1) * P], wsrow[:, g, :], ident[:])
                last.then_inc(ws_turned, 1)
                pe.wait_ge(ws_copied, l + 1)
                pe.wait_ge(v_normed, l + 1)
                for g in range(NH):
                    last = mm(psB[:, 1 + g // 2, (g % 2) * 256:(g % 2 + 1) * 256], wsT[:, g, :],
                              mix[:, :, COL_V + g * HD:COL_V + (g + 1) * HD])
                last.then_inc(mlp_mixed, 1)
                turn_heads(l, 0, 6, COL_WQ)
                pe.wait_ge(mlp_done, l + 1)
                attention(l, 0, COL_WV)
                turn_heads(l, 1, 6, COL_GQ)
                attention(l, 1, COL_GV)
                turn_heads(l, 2, 8, COL_RQ)
                retention(l)
                pe.wait_ge(branches_ready, l + 1)
                for c in range(KC):
                    if c >= 4:
                        pe.wait_ge(br_lo[l], c - 3)
                    col = OUT_COLS[c // 2] + (c % 2) * P
                    for b in range(T // P):
                        last = nc.tensor.transpose(psA[:, c % 4, b * P:(b + 1) * P], mix[:, b, col:col + P], ident[:])
                    last.then_inc(br_turned[l], 1)
                pe.wait_ge(br_lo[l], KC)
                with pe.Fori(0, GROUPS // 2) as i:
                    for j in range(2 * GROUP_UNITS):
                        g, u = divmod(j, GROUP_UNITS)
                        arrived(i * (2 * GROUP_UNITS) + (first_group[l] + j))
                        if u < NBR:
                            pe.wait_ge(gates_taken[l], i * (2 * NBR) + (g * NBR + u + 1))
                            last = two_chunks(j % 2, u % 2, lambda k: h(k, 0, T), T)
                        else:
                            for c in range(2):
                                for br in range(NBR):
                                    pe.wait_ge(proj_taken[l], i * (4 * NBR) + ((2 * g + c) * NBR + br + 1))
                                    for k in (2 * br, 2 * br + 1):
                                        last = mm3(psB[:, br, 0:T], w(j % 2, k * UC + c * P, P),
                                                   (brhi[:, k, 0:T], brlo[:, k, 0:T]), k == 2 * br, k == 2 * br + 1)
                                    if (c, br) != (1, NBR - 1):
                                        last.then_inc(proj_ready[l], 1)
                        last.then_inc(w_used, 1)
                pe.wait_ge(gates_taken[l], GROUPS * NBR + 2)
                pe.wait_ge(acc_ready[l], KC)
                with pe.Fori(0, OUT_UNITS // 2) as i:
                    for s in range(2):
                        arrived(i * 2 + (first_out[l] + s))
                        pe.wait_ge(out_taken[l], i * 2 + (s + 1))
                        two_chunks(s, s, lambda k: (acchi[:, k, 0:T], acclo[:, k, 0:T]), T).then_inc(w_used, 1)
                norm(2 * l + 1, T)
                if l == 0:
                    for k, chunks in enumerate(FFN_PARTS):
                        if k:
                            pe.wait_ge(down_taken[k - 1], KC + 2)
                        feed_forward(k, chunks, T, first_part[k], 0, 0)
                else:
                    pe.wait_ge(router_landed, 64)
                    for b in range(LBLK):
                        for k in range(KC):
                            for half, part in enumerate((hhi, hlo)):
                                last = mm(psB[:, 1, b * NEXP:(b + 1) * NEXP], part[:, k, b * P:(b + 1) * P].bitcast(F32),
                                          rw[:, k, :], k == 0 and half == 0, k == KC - 1 and half == 1)
                    last.then_inc(router_ready, 1)
                    pe.wait_ge(combine_ready, 1)
                    for b in range(LBLK):
                        last = nc.tensor.transpose(psB[0:NEXP, 2, b * P:(b + 1) * P], rout[:, 0, b, :], ident[:])
                    last.then_inc(combine_turned, 1)
                    pe.wait_ge(combine_copied, 1)
                    pe.wait_ge(out_taken[l], OUT_UNITS + 2)
                    for e in range(NEXP):
                        last = mm(psA[:, e // 2, (e % 2) * SEQ:(e % 2 + 1) * SEQ], pick[:, e, :], combT[:])
                    last.then_inc(comb_spread, 1)
                    pe.wait_ge(comb_spread, 2)
                    with pe.Fori(0, NEXP) as e:
                        feed_forward(2, EXP_CHUNKS, T, e * EXP_UNITS + first_exp, e * EXP_CHUNKS, e * KC)
            pe.wait_ge(x_final, KC)
            for c in range(KC):
                if c >= 4:
                    pe.wait_ge(out_placed, c - 3)
                for b in range(LBLK):
                    last = nc.tensor.transpose(psA[:, c % 4, b * P:(b + 1) * P], xT[:, c, b * P:(b + 1) * P], ident[:])
                last.then_inc(out_turned, 1)

        @block.scalar
        def _(act):
            step = Steps(act, act_step)

            def f(out, in_, func, **k):
                return nc.scalar.activation(out, in_, func, **k)

            def hi_part(n, slot):
                act.wait_ge(raw_landed[slot], 16 * n + (32 - 16 * slot))
                f(whi[:, slot], raw[:, slot], ACT.Copy).then_inc(hi_ready, 1)

            def next_hi(n, slot):
                act.wait_ge(w_used, n + 1)
                hi_part(n + 2, slot)

            for l in range(DEPTH):
                act.sem_inc(mix_taken[l], 2)
                act.sem_inc(gates_taken[l], 2)

            act.wait_ge(setup_copied, 1)
            f(siluc[:], rowsT[:, 0:16].rearrange("p (w c) -> p c w", w=2), ACT.Silu).then_inc(silu_ready, 1)
            act.wait_ge(lg_ready, 1)
            step(f(lgx[:, 1, :], lgx[:, 1, :], ACT.Exp, scale=-1.0))
            f(lgx[:, 1, :], lgx[:, 1, :], ACT.Ln, bias=1.0).then_inc(lg_steps, 1)
            act.wait_ge(lg_ready, 2)
            for k in range(4):
                last = f(expcol[:, k].rearrange("p l d h -> p (l d h)"), lgx[:, 2, :], ACT.Exp, scale=idx[:, k:k + 1])
            last.then_inc(lg_steps, 1)
            for l in range(DEPTH):
                for hd in range(NH):
                    n = l * NH + hd
                    if n >= 2:
                        act.wait_ge(decay_used, n - 1)
                    for d in range(2):
                        col = (l * 2 + d) * NH + hd
                        last = f(tmp[:, n % 2, d * P:(d + 1) * P], rel[:, d, :], ACT.Exp, scale=lgx[:, 2, col:col + 1])
                    last.then_inc(decay_exp, 1)

            def root(k, ap):
                act.wait_ge(ms_ready, k + 1)
                f(ap, ap, ACT.Sqrt).then_inc(root_ready, 1)

            def norm(k, T):
                for c in range(KC):
                    last = f(hf[:, c, 0:T], xT[:, c, 0:T], ACT.Square)
                    last.then_inc(squares, 1)
                l, second = divmod(k, 2)
                root(l * ROOTS + (NORM2 if second else NORM1), tmp[:, 0, 0:T])
                sh = SH2 if second else SH1
                for c in range(KC):
                    act.wait_ge(xn_ready, k * KC + c + 1)
                    for w in range(T // SEQ):
                        part = hf[:, c, w * SEQ:(w + 1) * SEQ]
                        last = f(part, part, ACT.Identity, scale=gsc[:, l, second, c, w:w + 1], bias=mod[:, l, sh, c, w:w + 1])
                    last.then_inc(h_ready, 1)

            def place_heads(l, m, heads):
                for j in range(heads):
                    act.wait_ge(head_turned[l][m], j + 1)
                    f(headsT[:, j, :], psA[0:HD, j % 4, :], ACT.Copy).then_inc(head_placed[l][m], 1)

            def attention(l, m):
                items = attention_items(l)
                n = len(items)
                for t_ in range(n + 1):
                    if t_ < n:
                        i = t_
                        hd, b, k0, nk = items[i]
                        act.wait_ge(max_ready[l][m], i + 1)
                        if i >= 2:
                            act.wait_ge(probs_turned[l][m], i - 1)
                        if m == 0:
                            f(sinkexp[:, i:i + 1], negmax[:, i:i + 1], ACT.Exp, bias=sink[:, l * NH + hd:l * NH + hd + 1])
                        f(expS[:, i % 2, 0:nk], psB[:, i % 2, 0:nk], ACT.Exp, scale=SCALE, bias=negmax[:, i:i + 1],
                          accum_out=rowsum[:, i:i + 1]).then_inc(exp_ready[l][m], 1)
                    if t_ >= 1:
                        i = t_ - 1
                        hd, b, k0, nk = items[i]
                        act.wait_ge(probs_turned[l][m], i + 1)
                        if i >= 2:
                            act.wait_ge(values_ready[l][m], i - 1)
                        f(expT[:, i % 2, 0:nk], psA[:, i % 2, 0:nk], ACT.Copy).then_inc(probs_placed[l][m], 1)

            def feed_forward(k, chunks, T, at_unit, up_done):
                with act.Fori(0, chunks // 2) as i:
                    for s in range(2):
                        next_hi(i * 2 + (at_unit + s), s)
                        act.wait_ge(up_taken[k], i * 2 + (up_done + (s + 1)))
                        f(tmp[:, s, 0:T], psA[:, 2 * s, 0:T], ACT.Silu).then_inc(up_silu[k], 1)

            def down_his(chunks, at_unit, turns):
                with act.Fori(0, turns) as i:
                    for s in range(2):
                        next_hi(i * 2 + (at_unit + (chunks + s)), s)

            for l in range(DEPTH):
                T = blocks_of(l) * P
                if l == 0:
                    act.wait_ge(x_placed, KC)
                    act.wait_ge(mod_ready, 1)
                else:
                    act.wait_ge(down_taken[1], KC + 2)
                norm(2 * l, TOK)
                if l == 0:
                    hi_part(0, 0)
                    hi_part(1, 1)
                for u in range(MIX_UNITS):
                    s = u % 2
                    next_hi(first_mix[l] + u, s)
                    func = ACT.Gelu_apprx_tanh if u < 2 else ACT.Silu if u * UC == COL_RG else ACT.Copy
                    f(mix[:, :, u * UC:(u + 1) * UC], psA[:, 2 * s:2 * s + 2, :].rearrange("p a (b n) -> p (a b) n", n=UC),
                      func).then_inc(mix_taken[l], 1)
                root(l * ROOTS + ROOT_V, stat[:, 0, 0:NBLK * NH])
                root(l * ROOTS + ROOT_W, stat[:, 0, 0:NBLK * 6])
                place_heads(l, 0, 6)
                attention(l, 0)
                root(l * ROOTS + ROOT_G, stat[:, 0, 0:NBLK * 6])
                place_heads(l, 1, 6)
                attention(l, 1)
                place_heads(l, 2, 8)
                root(l * ROOTS + ROOT_GN, stat[:, 0, 0:T // P * NH])
                for c in range(KC):
                    act.wait_ge(br_turned[l], c + 1)
                    f(brhi[:, c, 0:T], psA[:, c % 4, 0:T], ACT.Copy).then_inc(br_hi[l], 1)
                with act.Fori(0, GROUPS // 2) as i:
                    for j in range(2 * GROUP_UNITS):
                        g, u = divmod(j, GROUP_UNITS)
                        next_hi(i * (2 * GROUP_UNITS) + (first_group[l] + j), j % 2)
                        if u == 0:
                            act.wait_ge(gates_used[l], i * 2 + (g + 1))
                        if u < NBR:
                            f(gates[:, u, :, 0:T], psA[:, 2 * (u % 2):2 * (u % 2) + 2, 0:T], ACT.Sigmoid).then_inc(gates_taken[l], 1)
                with act.Fori(0, OUT_UNITS // 2) as i:
                    for s in range(2):
                        next_hi(i * 2 + (first_out[l] + s), s)
                act.wait_ge(out_taken[l], OUT_UNITS + 2)
                norm(2 * l + 1, T)
                if l == 0:
                    for k, chunks in enumerate(FFN_PARTS):
                        feed_forward(k, chunks, T, first_part[k], 0)
                        down_his(chunks, first_part[k], KC // 2)
                else:
                    act.wait_ge(h_split, 3 * KC + KC)
                    act.dma_start(rw[:], t["router_w"][0].rearrange("(c p) e -> p c e", p=P)).then_inc(router_landed, 16)
                    act.dma_start(rb[:], t["router_b"].broadcast_to([P, NEXP])).then_inc(router_landed, 16)
                    act.dma_start(eidx[:], t["k_eidx"]).then_inc(router_landed, 16)
                    act.dma_start(pick[:], t["k_pick"]).then_inc(router_landed, 16)
                    act.wait_ge(gap_ready, 1)
                    f(stat[:, 0, 4:6], stat[:, 0, 2:4], ACT.Exp).then_inc(gap_exp, 1)
                    act.wait_ge(comb_spread, 1)
                    f(combB[:].rearrange("p e n -> p (e n)"), psA[:].rearrange("p a n -> p (a n)"), ACT.Copy).then_inc(comb_spread, 1)
                    with act.Fori(0, NEXP - 1) as e:
                        feed_forward(2, EXP_CHUNKS, T, e * EXP_UNITS + first_exp, e * EXP_CHUNKS)
                        down_his(EXP_CHUNKS, e * EXP_UNITS + first_exp, KC // 2)
                    e = NEXP - 1
                    feed_forward(2, EXP_CHUNKS, T, e * EXP_UNITS + first_exp, e * EXP_CHUNKS)
                    down_his(EXP_CHUNKS, e * EXP_UNITS + first_exp, KC // 2 - 1)

        @block.vector
        def _(dve):
            step = Steps(dve, dve_step)
            V = nc.vector

            def tt(out, a, b, op):
                return V.tensor_tensor(out, a, b, op)

            def lo_part(n, slot):
                dve.wait_ge(hi_ready, n + 1)
                tt(wlo[:, slot], raw[:, slot], whi[:, slot].bitcast(F32), ALU.subtract).then_inc(lo_ready, 1)

            def split(hi, lo, x):
                step(V.tensor_copy(hi, x))
                return tt(lo, x, hi.bitcast(F32), ALU.subtract)

            V.memset(ones[:], 1.0 / D).then_inc(ones_set, 1)
            for l in range(DEPTH):
                dve.sem_inc(gates_used[l], 1)
                dve.sem_inc(proj_taken[l], NBR)
                dve.sem_inc(out_taken[l], 2)
            for k in range(3):
                dve.sem_inc(up_taken[k], 2)
                dve.sem_inc(down_taken[k], 2)
            dve.wait_ge(inputs_landed, loaded)
            step(V.tensor_scalar(lgx[:, 1, :], lgx[:, 0, :], -1.0, None, ALU.mult))
            tt(lgx[:, 1, :], lgx[:, 0, :], lgx[:, 1, :], ALU.max).then_inc(lg_ready, 1)
            V.tensor_scalar(nsink[:], sink[:], -1.0, None, ALU.mult)
            dve.wait_ge(setup_turned, 1)
            V.tensor_copy(rowsT[:], psB[:, 0, P:P + 24])
            V.tensor_copy(vecT[:], psB[:, 0, 0:P]).then_inc(setup_copied, 1)
            dve.wait_ge(lg_steps, 1)
            step(V.tensor_scalar(lgx[:, 0, :], lgx[:, 0, :], 0.0, None, ALU.min))
            tt(lgx[:, 2, :], lgx[:, 0, :], lgx[:, 1, :], ALU.subtract).then_inc(lg_ready, 1)
            for c in range(KC):
                dve.wait_ge(x_turned, c + 1)
                V.tensor_copy(xT[:, c, :], psA[:, c % 4, :]).then_inc(x_placed, 1)
            for n in range(DEPTH * NH):
                l, hd = divmod(n, NH)
                dve.wait_ge(decay_exp, n + 1)
                step(tt(tmp[:, n % 2, 0:2 * P].rearrange("p (d n) -> p d n", d=2), tmp[:, n % 2, 0:2 * P].rearrange("p (d n) -> p d n", d=2),
                        rel[:, 2:4, :], ALU.mult))
                tt(decay[:, l, hd, :], tmp[:, n % 2, 0:P], tmp[:, n % 2, P:2 * P], ALU.add).then_inc(decay_used, 1)
            dve.wait_ge(lg_steps, 2)
            for k, d in ((1, 0), (2, 1)):
                for l in range(DEPTH):
                    step(V.tensor_scalar(expcol[:, k, l, d, :], expcol[:, k, l, d, :], SCALE, None, ALU.mult))
            dve.wait_ge(mod_used, MOD_UNITS)
            cols = DEPTH * 6 * KC
            dve.wait_ge(setup_copied, 1)
            m = mod[:].rearrange("p l s c w -> p (l s c) w")
            step(tt(m, psB[:, 3, 0:2 * cols].rearrange("p (n w) -> p n w", w=2),
                    vecT[:, 0:cols].unsqueeze(2).broadcast_to([P, cols, 2]), ALU.add))
            for l in range(DEPTH):
                for k, sc in enumerate((SC1, SC2)):
                    g = vecT[:, 96 + 16 * k + 8 * l:96 + 16 * k + 8 * l + 8].unsqueeze(2).broadcast_to([P, KC, 2])
                    step(V.tensor_scalar(gsc[:, l, k], mod[:, l, sc], 1.0, None, ALU.add))
                    step(tt(gsc[:, l, k], gsc[:, l, k], g, ALU.mult))
            dve.sem_inc(mod_ready, 1)

            def norm(k, T):
                l, second = divmod(k, 2)
                dve.wait_ge(meansq, k + 1)
                V.tensor_scalar(tmp[:, 0, 0:T], psB[:, 0, 0:T], EPS, None, ALU.add).then_inc(ms_ready, 1)
                dve.wait_ge(root_ready, l * ROOTS + (NORM2 if second else NORM1) + 1)
                step(V.reciprocal(tmp[:, 0, 0:T], tmp[:, 0, 0:T]))
                for c in range(KC):
                    tt(hf[:, c, 0:T], xT[:, c, 0:T], tmp[:, 0, 0:T], ALU.mult).then_inc(xn_ready, 1)
                for c in range(KC):
                    dve.wait_ge(h_ready, k * KC + c + 1)
                    split(hhi[:, c, 0:T], hlo[:, c, 0:T], hf[:, c, 0:T]).then_inc(h_split, 1)

            def heads_view(col, heads, nb=NBLK):
                return mix[:, 0:nb, col:col + heads * HD].rearrange("p b (h d) -> p b h d", d=HD)

            def per_head(a, nb, heads, n=HD):
                if a.shape[1] == heads and nb * heads != heads:
                    return a.unsqueeze(1).unsqueeze(3).broadcast_to([P, nb, heads, n])
                return a.rearrange("p (b h) -> p b h", b=nb).unsqueeze(3).broadcast_to([P, nb, heads, n])

            def rms(col, heads, root):
                x, n = heads_view(col, heads), NBLK * heads
                sq = scrA[:, 0:n * HD].rearrange("p (b h d) -> p b h d", b=NBLK, d=HD)
                step(tt(sq, x, x, ALU.mult))
                step(V.tensor_reduce(stat[:, 0, 0:n], scrA[:, 0:n * HD].rearrange("p (n d) -> p n d", d=HD), AX_X, ALU.add))
                V.tensor_scalar(stat[:, 0, 0:n], stat[:, 0, 0:n], 1.0 / HD, EPS, ALU.mult, ALU.add).then_inc(ms_ready, 1)
                dve.wait_ge(root_ready, root + 1)
                step(V.reciprocal(stat[:, 0, 0:n], stat[:, 0, 0:n]))
                step(tt(x, x, per_head(stat[:, 0, 0:n], NBLK, heads), ALU.mult))

            def rope(col, heads, table, nb):
                x = mix[:, 0:nb, col:col + heads * HD].rearrange("p b (h t d) -> p b h t d", t=2, d=HD // 2)
                x1, x2 = x[:, :, :, 0, :], x[:, :, :, 1, :]
                cos, sin = (table[:, k, 0:nb, :].unsqueeze(2).broadcast_to([P, nb, heads, HD // 2]) for k in range(2))
                n = nb * heads * HD // 2
                a, b = (s[:, 0:n].rearrange("p (b h d) -> p b h d", b=nb, h=heads) for s in (scrA, scrB))
                tt(a, x1, sin, ALU.mult)
                step(tt(b, x2, sin, ALU.mult))
                tt(x1, x1, cos, ALU.mult)
                step(tt(x2, x2, cos, ALU.mult))
                tt(x1, x1, b, ALU.subtract)
                return tt(x2, x2, a, ALU.add)

            def attention_heads(l, m, col, root):
                rms(col, 6, l * ROOTS + root)
                for k, (c, heads) in enumerate(((col, NH), (col + NH * HD, 2))):
                    x = heads_view(c, heads)
                    wt = qkw[:, l, 2 * m + k, :].unsqueeze(1).unsqueeze(1).broadcast_to([P, NBLK, heads, HD])
                    last = tt(x, x, wt, ALU.mult)
                step(last)
                rope(col, 6, axial, LBLK).then_inc(heads_ready, 1)

            def attention(l, m):
                items = attention_items(l)
                n = len(items)
                for t_ in range(n + 2):
                    if t_ < n:
                        i = t_
                        hd, b, k0, nk = items[i]
                        dve.wait_ge(scores_ready[l][m], i + 1)
                        s = psB[:, i % 2, 0:nk]
                        if m == 0 and b < LBLK:
                            other = psB[:, i % 2, (1 - b) * P:(2 - b) * P]
                            step(tt(other, other, wmask[:, b, :], ALU.add))
                        step(V.tensor_reduce(negmax[:, i:i + 1], s, AX_X, ALU.max))
                        if m == 0:
                            V.tensor_scalar(negmax[:, i:i + 1], negmax[:, i:i + 1], -SCALE, nsink[:, l * NH + hd:l * NH + hd + 1],
                                            ALU.mult, ALU.min).then_inc(max_ready[l][m], 1)
                        else:
                            V.tensor_scalar(negmax[:, i:i + 1], negmax[:, i:i + 1], -SCALE, None, ALU.mult).then_inc(max_ready[l][m], 1)
                    if t_ >= 2:
                        i = t_ - 2
                        hd, b, k0, nk = items[i]
                        dve.wait_ge(values_ready[l][m], i + 1)
                        if m == 0:
                            step(tt(rowsum[:, i:i + 1], rowsum[:, i:i + 1], sinkexp[:, i:i + 1], ALU.add))
                        step(V.reciprocal(rowsum[:, i:i + 1], rowsum[:, i:i + 1]))
                        col = OUT_COLS[m + 1] + hd * HD
                        V.tensor_scalar(mix[:, b, col:col + HD], psB[:, 2 + i % 2, 0:HD], rowsum[:, i:i + 1], None,
                                        ALU.mult).then_inc(attn_done[l][m], 1)

            def retention(l):
                nb = blocks_of(l)
                k = heads_view(COL_RK, NH)
                for d, e in enumerate((1, 2)):
                    kd = kdec[:, d].rearrange("p b (h d) -> p b h d", d=HD)
                    last = tt(kd, k, per_head(expcol[:, e, l, d, :], NBLK, NH), ALU.mult)
                last.then_inc(kdec_ready, 1)
                dve.wait_ge(kv_ready, l + 1)
                for d, state in enumerate((stateF, stateB)):
                    cd = expcol[0:HD, 3, l, d, :].unsqueeze(2).broadcast_to([HD, NH, HD])
                    kv = psB[0:HD, 2 * d:2 * d + 2, :].rearrange("p a (b n) -> p (a b) n", b=2)
                    step(V.tensor_copy(state[:, 0, :], kv[:, 0, :]))
                    for n in (1, 2):
                        new, old = (state[:, x, :].rearrange("p (h d) -> p h d", h=NH) for x in (n, n - 1))
                        step(tt(new, old, cd, ALU.mult))
                        step(tt(state[:, n, :], state[:, n, :], kv[:, n, :], ALU.add))
                dve.sem_inc(states_ready, 1)

                def decayed(b):
                    dve.wait_ge(qk_ready[l], b + 1)
                    if b >= 2:
                        dve.wait_ge(ret_ready[l], b - 1)
                    tt(expS[:, b % 2, :], psA[:, b % 2, :], decay[:, l].rearrange("p h n -> p (h n)"), ALU.mult).then_inc(qk_decayed[l], 1)

                decayed(0)
                for b in range(nb):
                    if b + 1 < nb:
                        decayed(b + 1)
                    dve.wait_ge(ret_ready[l], b + 1)
                    inter = [psB[:, b % 2, d * 256:(d + 1) * 256].rearrange("p (h d) -> p h d", h=NH) for d in range(2)]
                    o = mix[:, b, COL_RQ:COL_RQ + 256]
                    terms = [psA[:, 2 + b % 2, 0:256]]
                    for d, skip in enumerate((2, 3)):
                        if b != skip:
                            scr = (scrA, scrB)[d][:, (b % 3) * 256:(b % 3 + 1) * 256]
                            last = tt(scr.rearrange("p (h d) -> p h d", h=NH), inter[d],
                                      expcol[:, d, l, d, :].unsqueeze(2).broadcast_to([P, NH, HD]), ALU.mult)
                            terms.append(scr)
                    step(last)
                    last = tt(o, terms[0], terms[1], ALU.add)
                    if len(terms) > 2:
                        step(last)
                        last = tt(o, o, terms[2], ALU.add)
                    last.then_inc(ret_taken[l], 1)
                dve.wait_ge(ret_taken[l], nb)
                x, n = heads_view(COL_RQ, NH, nb), nb * NH
                flat = mix[:, 0:nb, COL_RQ:COL_RQ + NH * HD]
                sq = scrA[:, 0:n * HD].rearrange("p (b h d) -> p b h d", b=nb, d=HD)
                step(V.tensor_reduce(stat[:, 1, 0:n].rearrange("p (b h) -> p b h", b=nb), x, AX_X, ALU.add))
                step(V.tensor_scalar(stat[:, 1, 0:n], stat[:, 1, 0:n], 1.0 / HD, None, ALU.mult))
                step(tt(x, x, per_head(stat[:, 1, 0:n], nb, NH), ALU.subtract))
                step(tt(sq, x, x, ALU.mult))
                step(V.tensor_reduce(stat[:, 0, 0:n], scrA[:, 0:n * HD].rearrange("p (n d) -> p n d", d=HD), AX_X, ALU.add))
                V.tensor_scalar(stat[:, 0, 0:n], stat[:, 0, 0:n], 1.0 / HD, EPS, ALU.mult, ALU.add).then_inc(ms_ready, 1)
                dve.wait_ge(root_ready, l * ROOTS + ROOT_GN + 1)
                step(V.reciprocal(stat[:, 0, 0:n], stat[:, 0, 0:n]))
                step(tt(x, x, per_head(stat[:, 0, 0:n], nb, NH), ALU.mult))
                step(tt(flat, flat, gn[:, l, :].unsqueeze(1).broadcast_to([P, nb, NH * HD]), ALU.mult))
                tt(flat, flat, mix[:, 0:nb, COL_RG:COL_RG + NH * HD], ALU.mult).then_inc(branches_ready, 1)

            def add_to_x(l, gate, oc, bank, T):
                for w in range(T // SEQ):
                    x = xT[:, oc, w * SEQ:(w + 1) * SEQ] if isinstance(oc, int) else \
                        xT[:, ds(oc, 1), w * SEQ:(w + 1) * SEQ].rearrange("p o n -> p (o n)")
                    g = mod[:, l, gate, oc, w:w + 1] if isinstance(oc, int) else \
                        mod[:, l, gate, ds(oc, 1), w:w + 1].rearrange("p o n -> p (o n)")
                    last = V.scalar_tensor_tensor(out=x, in0=bank[:, w * SEQ:(w + 1) * SEQ], scalar=g, in1=x,
                                                  op0=ALU.mult, op1=ALU.add)
                return last

            def next_lo(n, slot):
                lo_part(n + 2, slot)

            UP_STEPS = 2

            def ups(k, chunks, T, at_unit, up_done, turns_done):
                with dve.Fori(0, chunks // 2) as i:
                    step.loop(turns_done + i, 2 * UP_STEPS)
                    for s in range(2):
                        next_lo(i * 2 + (at_unit + s), s)
                        dve.wait_ge(up_silu[k], i * 2 + (up_done + (s + 1)))
                        x = tmp[:, s, 0:T]
                        step(tt(x, x, psA[:, 2 * s + 1, 0:T], ALU.mult))
                        split(hidhi[:, ds(i * (2 * T) + s * T, T)], hidlo[:, ds(i * (2 * T) + s * T, T)], x).then_inc(up_taken[k], 1)

            for l in range(DEPTH):
                T = blocks_of(l) * P
                norm(2 * l, TOK)
                if l == 0:
                    lo_part(0, 0)
                    lo_part(1, 1)
                with dve.Fori(0, MIX_UNITS // 2) as i:
                    for s in range(2):
                        next_lo(i * 2 + (first_mix[l] + s), s)
                dve.wait_ge(mix_taken[l], MIX_UNITS + 2)
                dve.wait_ge(ws_turned, l + 1)
                V.tensor_copy(wsT[:].rearrange("p g n -> p (g n)"), psB[:, 0, :]).then_inc(ws_copied, 1)
                rms(COL_V, NH, l * ROOTS + ROOT_V)
                v = mix[:, :, COL_V:COL_V + NH * HD]
                tt(v, v, gv[:, l, :].unsqueeze(1).broadcast_to([P, NBLK, NH * HD]), ALU.mult).then_inc(v_normed, 1)
                attention_heads(l, 0, COL_WQ, ROOT_W)
                dve.wait_ge(mlp_mixed, l + 1)
                for g in range(NH):
                    u = mix[:, :, COL_U + g * HD:COL_U + (g + 1) * HD]
                    mixed = psB[:, 1 + g // 2, (g % 2) * 256:(g % 2 + 1) * 256].rearrange("p (b d) -> p b d", d=HD)
                    last = V.scalar_tensor_tensor(out=u, in0=mixed, scalar=rowsT[:, 16 + l * NH + g:17 + l * NH + g], in1=u,
                                                  op0=ALU.add, op1=ALU.mult)
                last.then_inc(mlp_done, 1)
                attention(l, 0)
                attention_heads(l, 1, COL_GQ, ROOT_G)
                attention(l, 1)
                dve.wait_ge(attn_done[l][1], len(attention_items(l)))
                step(rope(COL_RQ, NH, rot, NBLK))
                rope(COL_RK, NH, rot, NBLK).then_inc(heads_ready, 1)
                dve.wait_ge(heads_ready, 3 * l + 3)
                retention(l)
                for c in range(KC):
                    dve.wait_ge(br_hi[l], c + 1)
                    tt(brlo[:, c, 0:T], psA[:, c % 4, 0:T], brhi[:, c, 0:T].bitcast(F32), ALU.subtract).then_inc(br_lo[l], 1)
                STEPS = 4 * NBR
                READY = 2 * NBR - 1
                total, new = tmp[:, 0, 0:T], tmp[:, 1, 0:T]
                with dve.Fori(0, GROUPS // 2) as i:
                    step.loop(i, STEPS)
                    for j in range(2 * GROUP_UNITS):
                        g, u = divmod(j, GROUP_UNITS)
                        n = i * (2 * GROUP_UNITS) + (first_group[l] + j)
                        if u < NBR:
                            next_lo(n, j % 2)
                            continue
                        for c in range(2):
                            for br in range(NBR):
                                if (c, br) == (1, NBR - 1):
                                    dve.wait_ge(w_used, n + 1)
                                else:
                                    dve.wait_ge(proj_ready[l], i * (2 * READY) + (g * READY + c * NBR + br + 1))
                                if (c, br) == (0, 0):
                                    dve.wait_ge(gates_taken[l], i * (2 * NBR) + ((g + 1) * NBR + 2))
                                out = total if br == 0 else new
                                ins = tt(out, psB[:, br, 0:T], gates[:, br, c, 0:T], ALU.mult)
                                ins.then_inc(proj_taken[l], 1)
                                dve.wait_ge(proj_taken[l], i * (4 * NBR) + ((2 * g + c) * NBR + br + 1 + NBR))
                                if br:
                                    step(tt(total, total, new, ALU.add))
                            oc = i * (2 * UC // P) + (g * 2 + c)
                            hi, lo = (a[:, ds(oc, 1), 0:T].rearrange("p o n -> p (o n)") for a in (acchi, acclo))
                            step(V.tensor_copy(hi, total))
                            tt(lo, total, hi.bitcast(F32), ALU.subtract).then_inc(acc_ready[l], 1)
                            dve.wait_ge(acc_ready[l], i * (2 * UC // P) + (g * 2 + c + 1))
                        dve.sem_inc(gates_used[l], 1)
                        next_lo(n, j % 2)
                step.end(GROUPS // 2, STEPS)
                with dve.Fori(0, OUT_UNITS // 2) as i:
                    for s in range(2):
                        n = i * 2 + (first_out[l] + s)
                        next_lo(n, s)
                        dve.wait_ge(w_used, n + 1)
                        for j in range(2):
                            last = add_to_x(l, G1, i * 4 + (2 * s + j), psA[:, 2 * s + j], T)
                        last.then_inc(out_taken[l], 1)
                norm(2 * l + 1, T)
                if l == 0:
                    for k, chunks in enumerate(FFN_PARTS):
                        ups(k, chunks, T, first_part[k], 0, 0)
                        step.end(chunks // 2, 2 * UP_STEPS)
                        with dve.Fori(0, KC // 2) as i:
                            for s in range(2):
                                n = i * 2 + (first_part[k] + chunks + s)
                                next_lo(n, s)
                                dve.wait_ge(w_used, n + 1)
                                add_to_x(0, G2, i * 2 + s, psA[:, 2 * s], T).then_inc(down_taken[k], 1)
                        dve.wait_ge(down_taken[k], KC + 2)
                    continue
                dve.wait_ge(h_split, 3 * KC + KC)
                step(V.memset(moe[:].rearrange("p c n -> p (c n)"), 0.0))
                dve.wait_ge(router_landed, 64)
                dve.wait_ge(router_ready, 1)
                R = [rout[:, k] for k in range(12)]
                spread = [P, LBLK, NEXP]
                def over(col):
                    return stat[:, 0, col:col + LBLK].unsqueeze(2).broadcast_to(spread)
                step(tt(R[1], psB[:, 1, 0:LBLK * NEXP].rearrange("p (b e) -> p b e", b=LBLK),
                        rb[:].unsqueeze(1).broadcast_to(spread), ALU.add))
                for n, logits in enumerate((R[1], R[5])):
                    top = (8, 10)[n]
                    step(V.tensor_reduce(stat[:, 0, top:top + LBLK], logits, AX_X, ALU.max))
                    step(tt(R[2], logits, over(top), ALU.is_equal))
                    step(V.scalar_tensor_tensor(out=R[3], in0=R[2], scalar=-float(NEXP), in1=eidx[:].unsqueeze(1).broadcast_to(spread),
                                                op0=ALU.mult, op1=ALU.add))
                    step(V.tensor_reduce(stat[:, 0, 12:14], R[3], AX_X, ALU.min))
                    step(tt(R[6 + n], R[3], over(12), ALU.is_equal))
                    if n == 0:
                        step(V.scalar_tensor_tensor(out=R[5], in0=R[6], scalar=-BIG, in1=R[1], op0=ALU.mult, op1=ALU.add))
                tt(stat[:, 0, 2:4], stat[:, 0, 10:12], stat[:, 0, 8:10], ALU.subtract).then_inc(gap_ready, 1)
                dve.wait_ge(gap_exp, 1)
                step(V.tensor_scalar(stat[:, 0, 6:8], stat[:, 0, 4:6], 1.0, None, ALU.add))
                step(V.reciprocal(stat[:, 0, 6:8], stat[:, 0, 6:8]))
                step(tt(R[0], R[7], over(4), ALU.mult))
                step(tt(R[0], R[0], R[6], ALU.add))
                tt(R[0], R[0], over(6), ALU.mult).then_inc(combine_ready, 1)
                dve.wait_ge(combine_turned, 1)
                V.tensor_copy(combT[:], psB[0:NEXP, 2, 0:SEQ]).then_inc(combine_copied, 1)
                dve.wait_ge(comb_spread, 2)
                start = step.n

                def expert(e, last_turns):
                    at_unit = e * EXP_UNITS + first_exp
                    per = EXP_CHUNKS * UP_STEPS + KC
                    with dve.Fori(0, EXP_CHUNKS // 2) as i:
                        step.n, step.base = start, e * per + i * (2 * UP_STEPS)
                        for s in range(2):
                            next_lo(i * 2 + (at_unit + s), s)
                            dve.wait_ge(up_silu[2], i * 2 + (e * EXP_CHUNKS + (s + 1)))
                            x = tmp[:, s, 0:T]
                            step(tt(x, x, psA[:, 2 * s + 1, 0:T], ALU.mult))
                            split(hidhi[:, ds(i * (2 * T) + s * T, T)], hidlo[:, ds(i * (2 * T) + s * T, T)], x).then_inc(up_taken[2], 1)

                    def down_pair(i, more):
                        step.n, step.base = start, e * per + (i * 2 + EXP_CHUNKS * UP_STEPS)
                        for s in range(2):
                            n = i * 2 + (at_unit + (EXP_CHUNKS + s))
                            if more:
                                next_lo(n, s)
                            dve.wait_ge(w_used, n + 1)
                            x = tmp[:, s, SEQ:2 * SEQ]
                            c = combB[:, ds(e, 1), :].rearrange("p o n -> p (o n)")
                            m = moe[:, ds(i * 2 + s, 1), :].rearrange("p o n -> p (o n)")
                            step(tt(x, psA[:, 2 * s, 0:T], c, ALU.mult))
                            tt(m, m, x, ALU.add).then_inc(down_taken[2], 1)

                    with dve.Fori(0, last_turns) as i:
                        down_pair(i, True)
                    if last_turns < KC // 2:
                        down_pair(last_turns, False)

                with dve.Fori(0, NEXP - 1) as e:
                    expert(e, KC // 2)
                expert(NEXP - 1, KC // 2 - 1)
                dve.wait_ge(down_taken[2], NEXP * KC + 2)
                for c in range(KC):
                    V.scalar_tensor_tensor(out=xT[:, c, 0:T], in0=moe[:, c, :], scalar=mod[:, l, G2, c, 0:1], in1=xT[:, c, 0:T],
                                           op0=ALU.mult, op1=ALU.add).then_inc(x_final, 1)
            dve.wait_ge(x_final, KC)
            for c in range(KC):
                dve.wait_ge(out_turned, c + 1)
                V.tensor_copy(xrows[:, 0:LBLK, c * P:(c + 1) * P], psA[:, c % 4, 0:LBLK * P].rearrange("p (b n) -> p b n", n=P)).then_inc(out_placed, 1)


INPUTS = ("x", "c", "ctx", "c_ctx", "w_mod", "b_mod", "g_norm1", "g_norm2", "w_in", "mlp_g_v", "mlp_w_s", "mlp_b_s",
          "win_q_norm", "win_k_norm", "win_sink", "glb_q_norm", "glb_k_norm", "ret_decay", "ret_gn", "w_branch", "w_out",
          "ffn_w1", "ffn_w3", "ffn_w2", "router_w", "router_b", "moe_w1", "moe_w3", "moe_w2")
GRID_W = 64
ROPE_BASE = 10000.0


def shape_constants():
    f = np.float32
    i, j = np.arange(P, dtype=f)[:, None], np.arange(P, dtype=f)[None, :]
    wmask = np.stack([np.where(j <= i, f(0), f(-BIG)), np.where(j >= i, f(0), f(-BIG))], 1)
    rel = np.stack([np.maximum(j - i, 0), np.maximum(i - j - 1, 0), np.where(j >= i, SCALE, 0), np.where(i > j, SCALE, 0)], 1)
    idx = np.concatenate([i + 1, P - 1 - i, i, np.full_like(i, P)], 1)

    def by_block(ang):
        tab = np.stack([np.cos(ang), np.sin(ang)], 0).astype(f)
        return np.ascontiguousarray(tab.reshape(2, -1, P, HD // 2).transpose(2, 0, 1, 3))

    pos = np.arange(SEQ)
    inv = (ROPE_BASE ** (-np.arange(HD // 4, dtype=f) / f(HD // 4))).astype(f)
    axial = np.concatenate([(pos // GRID_W).astype(f)[:, None] * inv, (pos % GRID_W).astype(f)[:, None] * inv], 1)
    inv = (ROPE_BASE ** (-np.arange(HD // 2, dtype=f) / f(HD // 2))).astype(f)
    place = np.concatenate([CTX + np.arange(SEQ), np.arange(CTX)]).astype(f)
    pick = np.zeros((NEXP, NEXP, P), f)
    pick[np.arange(NEXP), np.arange(NEXP)] = 1
    return {"k_ident": np.eye(P, dtype=f), "k_wmask": wmask.astype(f), "k_rel": rel.astype(f), "k_idx": idx.astype(f),
            "k_axial": by_block(axial), "k_rot": by_block(place[:, None] * inv), "k_pick": pick,
            "k_eidx": np.tile(np.arange(NEXP, dtype=f), (P, 1))}


def kernel(**inputs):
    import concourse.bacc as bacc
    from concourse.bass_utils import run_bass_kernel_spmd

    nc = bacc.Bacc("TRN2", target_bir_lowering=False, num_devices=1)
    arrays = {name: np.ascontiguousarray(inputs[name]) for name in INPUTS}
    arrays.update(shape_constants())
    tensors = {name: nc.dram_tensor(name, a.shape, mybir.dt.from_np(a.dtype), kind="ExternalInput").ap()
               for name, a in arrays.items()}
    tensors["out"] = nc.dram_tensor("out", (1, SEQ, D), F32, kind="ExternalOutput").ap()
    build_program(nc, tensors)
    return run_bass_kernel_spmd(nc, [arrays], core_ids=[0]).results[0]["out"]
```

```python
from contextlib import ExitStack

import numpy as np

import concourse.bass as bass
from concourse import mybir

F32 = mybir.dt.float32
F32R = mybir.dt.float32r
ALU = mybir.AluOpType
ACT = mybir.ActivationFunctionType
AX_X = mybir.AxisListType.X

P = 128
D = 1024
KC = D // P
SEQ = 256
CTX = 256
TOK = SEQ + CTX
NBLK = TOK // P
LBLK = SEQ // P
HD = 64
NH = 4
DEPTH = 2
MIX_W = 2560
COL_U, COL_V = 0, 256
COL_WQ, COL_WK, COL_WV = 512, 768, 896
COL_GQ, COL_GK, COL_GV = 1024, 1280, 1408
COL_RQ, COL_RK, COL_RV, COL_RG = 1536, 1792, 2048, 2304
OUT_COLS = (COL_U, COL_WQ, COL_GQ, COL_RQ)
NBR = 4
DFF = 2816
DFE = 1792
NEXP = 8
EPS = 1e-6
SCALE = HD ** -0.5
BIG = 1e30
UNIT = 2048
UC = UNIT // KC
MIX_UNITS = MIX_W // UC
GROUPS = D // UC
GROUP_UNITS = NBR + 1
OUT_UNITS = D // UC
MG = 512
EARLY_GROUPS = 2 * D // MG
MOD_GROUPS = 6 * D // MG
EARLY_UNITS = 2 * D // UC
HALVES = 4 * D // P
MOD_RING = 4
FFN_PARTS = (12, 10)
EXP_CHUNKS = DFE // P
EXP_UNITS = EXP_CHUNKS + KC
UPS = DFE // UC
DOWNS = EXP_CHUNKS // 2
GU = 2 * UPS + DOWNS
HALF = UNIT // 2
UPPER_FIRST = (1, 0)
RING = 3
assert GU % RING == 0 and UNIT == 2 * D
UNITS0 = MIX_UNITS + GROUPS * GROUP_UNITS + OUT_UNITS + sum(FFN_PARTS) + 2 * KC
SH1, SC1, G1, SH2, SC2, G2 = range(6)
ds = bass.ds


def blocks_of(layer):
    return NBLK if layer < DEPTH - 1 else LBLK


def attention_items(layer):
    return [(h, b, 0, TOK) if b < LBLK else (h, b, SEQ, CTX) for b in range(blocks_of(layer)) for h in range(NH)]


def items_before(layer, mixer):
    return sum(2 * len(attention_items(x)) for x in range(layer)) + mixer * len(attention_items(layer))


def heads_before(layer, m):
    return layer * 20 + 6 * m


def build_program(nc, t):
    with ExitStack() as ctx:
        base = 16512
        top = 229344 - 32
        place = {"at": base}
        ctx.enter_context(nc.sbuf_tensor("arena", [P, (top - base) // 4], F32))

        def at(name, shape, dt, offset):
            return nc.alloc_sbuf_tensor_at(name, shape, dt, offset=offset)

        def sb(name, shape, dt=F32):
            size = 4 * int(np.prod(shape[1:]))
            here = place["at"]
            place["at"] = here + (size + 31) // 32 * 32
            assert place["at"] <= top, name
            return at(name, shape, dt, here)

        def sem(name):
            return ctx.enter_context(nc.semaphore(name))

        raw = sb("raw", [P, 2, UNIT])
        whi = sb("whi", [P, 2, UNIT], F32R)
        wlo = sb("wlo", [P, 2, UNIT], F32R)
        xT = sb("xT", [P, KC, TOK])
        hhi = sb("hhi", [P, KC, TOK], F32R)
        hlo = sb("hlo", [P, KC, TOK], F32R)
        region = place["at"]
        mix = sb("mix", [P, NBLK, MIX_W])
        headsT = sb("headsT", [HD, 8, TOK])
        acchi = at("acchi", [P, KC, TOK], F32R, region)
        acclo = at("acclo", [P, KC, TOK], F32R, region + 4 * KC * TOK)
        hidhi = at("hidhi", [P, 12 * TOK], F32R, region)
        hidlo = at("hidlo", [P, 12 * TOK], F32R, region + 4 * 12 * TOK)
        modring = at("modring", [P, MOD_RING, KC, UC], F32, region)
        gates = at("gates", [P, NBR, 2, TOK], F32, region + 4 * NBLK * MIX_W)
        region2 = place["at"]
        brhi = sb("brhi", [P, KC, TOK], F32R)
        brlo = sb("brlo", [P, KC, TOK], F32R)
        xrows = at("xrows", [P, NBLK, D], F32, region2)
        hf = at("hf", [P, KC, TOK], F32, region2)
        scrA = at("scrA", [P, 1536], F32, region2)
        scrB = at("scrB", [P, 1536], F32, region2 + 4 * 1536)
        expS = at("expS", [P, 2, TOK], F32, region2 + 4 * 3072)
        expT = at("expT", [P, 2, TOK], F32, region2 + 4 * 4096)
        kdec = at("kdec", [P, 2, NBLK, NH * HD], F32, region2 + 4 * 5120)
        wsrow = at("wsrow", [P, NH, P], F32, region2 + 4 * 7168)
        wsT = at("wsT", [P, NH, P], F32, region2 + 4 * 7680)
        modhalf = at("modhalf", [P, 2, KC, P], F32, region2 + 4 * 5120)
        modfull = at("modfull", [P, 2, KC, UC], F32, region2)
        modrows = [at("modrow_start", [2, 2, MG], F32, base + 24 * UNIT + 4 * KC * TOK),
                   at("modrow_attn", [2, 2, MG], F32, region2 + 4 * 7168),
                   at("modrow_ffn", [2, 2, MG], F32, region2 + 4 * 4096)]
        stateF = at("stateF", [HD, 3, NH * HD], F32, region2 + 4 * 7168)
        moe = at("moe", [P, KC, SEQ], F32, region2)
        eraw = at("eraw", [P, 3, UNIT], F32, base)
        ehi = at("ehi", [P, 3, UNIT], F32R, base + 12 * UNIT)
        elo = at("elo", [P, 3, UNIT], F32R, region)
        ghi = at("ghi", [P, KC, P], F32R, region + 12 * UNIT)
        glo = at("glo", [P, KC, P], F32R, region + 12 * UNIT + 4 * D)
        tokhi = at("tokhi", [P, LBLK, D], F32R, region + 12 * UNIT + 8 * D)
        toklo = at("toklo", [P, LBLK, D], F32R, region + 12 * UNIT + 8 * D + 4 * LBLK * D)
        hregion = base + 24 * UNIT + 4 * KC * TOK
        eupT_hi = at("eupT_hi", [P, EXP_CHUNKS, P], F32R, hregion)
        eupT_lo = at("eupT_lo", [P, EXP_CHUNKS, P], F32R, hregion + 4 * DFE)
        yhi = at("yhi", [P, D], F32R, hregion + 8 * DFE)
        ylo = at("ylo", [P, D], F32R, hregion + 8 * DFE + 4 * D)
        eup = at("eup", [P, 2, UC], F32, hregion + 8 * DFE + 8 * D)
        gat = at("gat", [P, LBLK, P], F32R, hregion + 8 * DFE + 8 * D + 8 * UC)
        sca = at("sca", [P, SEQ], F32R, hregion + 8 * DFE + 8 * D + 8 * UC + 4 * SEQ)
        combB = at("combB", [P, NEXP, SEQ], F32, region2 + 4 * 2048)
        rel = at("rel", [P, 4, P], F32, region2 + 4 * 4096)
        pick = at("pick", [NEXP, NEXP, P], F32, region2 + 4 * 4096)
        rout = at("rout", [P, 12, LBLK, NEXP], F32, region2 + 4 * 5120)
        posB = at("posB", [P, NEXP, SEQ], F32, region2 + 4 * 2048)
        before = at("before", [P, 2, P], F32, region2 + 4 * 6464)
        slots = at("slots", [P, P], F32, region2 + 4 * 6720)
        slot_of = at("slot_of", [P, 4], F32, region2 + 4 * 6848)
        cw = at("cw", [P, NEXP], F32, region2 + 4 * 6856)
        most = at("most", [P, 1], F32, region2 + 4 * 6864)
        most_i = at("most_i", [P, 1], mybir.dt.int32, region2 + 4 * 6872)
        combT = at("combT", [NEXP, SEQ], F32, region2 + 4 * 5632)
        rw = at("rw", [P, KC, NEXP], F32, region2 + 4 * 6144)
        rb = at("rb", [P, NEXP], F32, region2 + 4 * 6400)
        eidx = at("eidx", [P, NEXP], F32, region2 + 4 * 6432)
        tmp = sb("tmp", [P, 2, TOK])
        stateB = at("stateB", [HD, 3, NH * HD], F32, place["at"] - 4 * 2 * TOK)
        decay = sb("decay", [P, DEPTH, NH, P])
        ident = sb("ident", [P, P])
        ones = sb("ones", [P, P])
        rows1 = at("rows1", [P, P], F32, region2 + 4 * 6656)
        rows2 = at("rows2", [24, P], F32, region2 + 4 * 6784)
        idx = at("idx", [P, 4], F32, region2 + 4 * 6912)
        lgx = at("lgx", [P, 3, 16], F32, region2 + 4 * 6944)
        vecT = sb("vecT", [P, P])
        rowsT = sb("rowsT", [P, 24])
        siluc = sb("siluc", [P, KC, 2])
        mod = sb("mod", [P, DEPTH, 6, KC, 2])
        gsc = sb("gsc", [P, DEPTH, 2, KC, 2])
        wmask = sb("wmask", [P, 2, P])
        axial = sb("axial", [P, 2, LBLK, 32])
        rot = sb("rot", [P, 2, NBLK, 32])
        qkw = sb("qkw", [P, DEPTH, 4, HD])
        gv = sb("gv", [P, DEPTH, NH * HD])
        gn = sb("gn", [P, DEPTH, NH * HD])
        sink = sb("sink", [P, DEPTH * NH])
        nsink = sb("nsink", [P, DEPTH * NH])
        expcol = sb("expcol", [P, 4, DEPTH, 2, NH])
        stat = sb("stat", [P, 3, 24])
        negmax = sb("negmax", [P, 16])
        rowsum = sb("rowsum", [P, 16])
        sinkexp = sb("sinkexp", [P, 16])

        psA = ctx.enter_context(nc.psum_tensor("psA", [P, 4, 512], F32))
        psB = ctx.enter_context(nc.psum_tensor("psB", [P, 4, 512], F32))

        inputs_landed = sem("inputs_landed")
        late_landed = sem("late_landed")
        router_landed = sem("router_landed")
        mod_landed = [sem(f"mod_landed{s}") for s in range(MOD_RING)]
        mod_used = sem("mod_used")
        modh_landed = [sem(f"modh_landed{s}") for s in range(2)]
        modh_used = sem("modh_used")
        modf_landed = [sem(f"modf_landed{s}") for s in range(2)]
        modf_used = sem("modf_used")
        mod_copied = sem("mod_copied")
        mod_turned = sem("mod_turned")
        mod_added = sem("mod_added")
        ones_set = sem("ones_set")
        setup_turned = sem("setup_turned")
        setup_copied = sem("setup_copied")
        silu_ready = sem("silu_ready")
        lg_steps = sem("lg_steps")
        lg_ready = sem("lg_ready")
        decay_exp = sem("decay_exp")
        decay_used = sem("decay_used")
        x_turned = sem("x_turned")
        x_placed = sem("x_placed")
        raw_landed = [[sem(f"raw_landed{s}{h}") for h in range(2)] for s in range(2)]
        hi_ready = sem("hi_ready")
        lo_ready = sem("lo_ready")
        w_used = sem("w_used")
        dve_step = sem("dve_step")
        act_step = sem("act_step")
        out_stored = sem("out_stored")
        out_placed = sem("out_placed")
        out_turned = sem("out_turned")
        squares = sem("squares")
        meansq = sem("meansq")
        ms_ready = sem("ms_ready")
        root_ready = sem("root_ready")
        xn_ready = sem("xn_ready")
        h_ready = sem("h_ready")
        h_split = sem("h_split")
        L = range(DEPTH)
        mix_taken = [sem(f"mix_taken{l}") for l in L]
        ws_turned = sem("ws_turned")
        ws_copied = sem("ws_copied")
        v_normed = sem("v_normed")
        mlp_mixed = sem("mlp_mixed")
        mlp_done = sem("mlp_done")
        heads_ready = sem("heads_ready")
        head_turned = sem("head_turned")
        head_placed = sem("head_placed")
        scores_ready = sem("scores_ready")
        max_ready = sem("max_ready")
        exp_ready = sem("exp_ready")
        probs_turned = sem("probs_turned")
        probs_placed = sem("probs_placed")
        values_ready = sem("values_ready")
        attn_done = sem("attn_done")
        kdec_ready = sem("kdec_ready")
        kv_ready = sem("kv_ready")
        states_ready = sem("states_ready")
        qk_ready = [sem(f"qk_ready{l}") for l in L]
        qk_decayed = [sem(f"qk_decayed{l}") for l in L]
        ret_ready = [sem(f"ret_ready{l}") for l in L]
        ret_taken = [sem(f"ret_taken{l}") for l in L]
        branches_ready = sem("branches_ready")
        br_turned = [sem(f"br_turned{l}") for l in L]
        br_hi = [sem(f"br_hi{l}") for l in L]
        br_lo = [sem(f"br_lo{l}") for l in L]
        gates_taken = [sem(f"gates_taken{l}") for l in L]
        gates_used = [sem(f"gates_used{l}") for l in L]
        proj_ready = [sem(f"proj_ready{l}") for l in L]
        proj_taken = [sem(f"proj_taken{l}") for l in L]
        acc_ready = [sem(f"acc_ready{l}") for l in L]
        out_taken = [sem(f"out_taken{l}") for l in L]
        up_silu = [sem(f"up_silu{k}") for k in range(3)]
        up_taken = [sem(f"up_taken{k}") for k in range(3)]
        down_ready = [sem(f"down_ready{k}") for k in range(3)]
        down_taken = [sem(f"down_taken{k}") for k in range(3)]
        router_ready = sem("router_ready")
        combine_ready = sem("combine_ready")
        combine_turned = sem("combine_turned")
        combine_copied = sem("combine_copied")
        comb_spread = sem("comb_spread")
        gap_ready = sem("gap_ready")
        gap_exp = sem("gap_exp")
        mask_ready = sem("mask_ready")
        counted = sem("counted")
        most_ready = sem("most_ready")
        eraw_landed = [[sem(f"eraw_landed{s}{h}") for h in range(2)] for s in range(RING)]
        ehi_ready = sem("ehi_ready")
        elo_ready = sem("elo_ready")
        ew_used = sem("ew_used")
        tok_turned = sem("tok_turned")
        tok_hi = sem("tok_hi")
        tok_lo = sem("tok_lo")
        pos_turned = sem("pos_turned")
        pos_copied = sem("pos_copied")
        pos_spread = sem("pos_spread")
        pos_placed = sem("pos_placed")
        gat_ready = sem("gat_ready")
        gathered = sem("gathered")
        gathered_placed = sem("gathered_placed")
        cw_ready = sem("cw_ready")
        cw_placed = sem("cw_placed")
        eup_silu = sem("eup_silu")
        eup_ready = sem("eup_ready")
        eup_turned = sem("eup_turned")
        eupT_hi_ready = sem("eupT_hi_ready")
        eupT_lo_ready = sem("eupT_lo_ready")
        sca_ready = sem("sca_ready")
        scattered = sem("scattered")
        scattered_added = sem("scattered_added")
        y_hi_ready = sem("y_hi_ready")
        y_lo_ready = sem("y_lo_ready")
        moe_step = sem("moe_step")
        x_final = sem("x_final")
        mod_ready = sem("mod_ready")

        first_mix = [0, UNITS0]
        first_group = [u + MIX_UNITS for u in first_mix]
        first_out = [u + GROUPS * GROUP_UNITS for u in first_group]
        first_ffn = [u + OUT_UNITS for u in first_out]
        first_part = [first_ffn[0], first_ffn[0] + FFN_PARTS[0] + KC]
        first_exp = first_ffn[1]

        ROOTS = 6
        NORM1, ROOT_V, ROOT_W, ROOT_G, ROOT_GN, NORM2 = range(ROOTS)
        setup_loads = []

        block = ctx.enter_context(nc.Block())

        @block.sync
        def _(sp):
            def load(dst, src):
                setup_loads.append(1)
                sp.dma_start(dst, src).then_inc(inputs_landed, 16)

            load(rows1[0:96, :], t["b_mod"].rearrange("l (c p) -> (l c) p", p=P))
            load(rows1[96:112, :], t["g_norm1"].rearrange("l (c p) -> (l c) p", p=P))
            load(rows1[112:128, :], t["g_norm2"].rearrange("l (c p) -> (l c) p", p=P))
            load(rows2[0:8, :], t["c"].rearrange("b (c p) -> (b c) p", p=P))
            load(rows2[8:16, :], t["c_ctx"].rearrange("(c p) -> c p", p=P))
            load(rows2[16:24, :], t["mlp_b_s"].rearrange("l g p -> (l g) p"))
            load(ident[:], t["k_ident"])
            w = t["w_mod"][0].rearrange("(c p) n -> p c n", p=P)
            for u in range(MOD_RING):
                sp.dma_start(modring[:, u], w[:, :, u * UC:(u + 1) * UC]).then_inc(mod_landed[u], 16)
            load(xrows[:, 0:LBLK, :], t["x"].rearrange("b (n p) d -> p (b n) d", p=P))
            load(xrows[:, LBLK:NBLK, :], t["ctx"].rearrange("b (n p) d -> p (b n) d", p=P))
            load(wmask[:], t["k_wmask"])
            load(axial[:], t["k_axial"])
            load(rot[:], t["k_rot"])
            load(rel[:], t["k_rel"])
            load(idx[:], t["k_idx"])
            load(lgx[:, 0, :], t["ret_decay"].rearrange("l d h -> (l d h)").unsqueeze(0).broadcast_to([P, 16]))
            for l in range(DEPTH):
                for k, name in enumerate(("win_q_norm", "win_k_norm", "glb_q_norm", "glb_k_norm")):
                    load(qkw[:, l, k, :], t[name][l:l + 1, :].broadcast_to([P, HD]))
                load(gv[:, l, :], t["mlp_g_v"][l:l + 1].rearrange("l g d -> l (g d)").broadcast_to([P, NH * HD]))
                load(gn[:, l, :], t["ret_gn"][l:l + 1].rearrange("l g d -> l (g d)").broadcast_to([P, NH * HD]))
            load(sink[:], t["win_sink"].rearrange("l h -> (l h)").unsqueeze(0).broadcast_to([P, DEPTH * NH]))

            for u in range(MOD_RING, EARLY_UNITS):
                sp.wait_ge(mod_used, u + 1 - MOD_RING)
                sp.dma_start(modring[:, u % MOD_RING], w[:, :, u * UC:(u + 1) * UC]).then_inc(mod_landed[u % MOD_RING], 16)

            def unit_loads(n, slot, upper, lower, at_zero=False):
                for k, (dst, src) in enumerate((upper, lower)):
                    if n is not None and not (at_zero and k):
                        sp.wait_ge(lo_ready, n * 2 + (2 if at_zero else k + 1) - 4)
                    sp.dma_start(dst, src).then_inc(raw_landed[slot][UPPER_FIRST[k]], 16)

            def square(n, slot, w, col, at_zero=False):
                dst = raw[:, slot].rearrange("p (c n) -> p c n", c=KC)
                src = w.rearrange("(c p) n -> p c n", p=P)
                half = KC // 2
                unit_loads(n, slot, (dst[:, half:KC], src[:, half:KC, ds(col, UC)]), (dst[:, 0:half], src[:, 0:half, ds(col, UC)]),
                           at_zero)

            def up(n, slot, w1, w3, col):
                dst = raw[:, slot].rearrange("p (w c n) -> p w c n", w=2, c=KC)
                unit_loads(n, slot, (dst[:, 1], w3[:, ds(col, P)].rearrange("(c p) n -> p c n", p=P)),
                           (dst[:, 0], w1[:, ds(col, P)].rearrange("(c p) n -> p c n", p=P)), True)

            def down(n, slot, w2, rows, col):
                dst = raw[:, slot, 0:rows * P].rearrange("p (c n) -> p c n", c=rows)
                src = w2.rearrange("(c p) n -> p c n", p=P)
                unit_loads(n, slot, (dst[:, KC:rows], src[:, KC:rows, ds(col, P)]), (dst[:, 0:KC], src[:, 0:KC, ds(col, P)]), True)

            for l in range(DEPTH):
                w = t["w_in"][l]
                if l == 0:
                    square(None, 0, w, 0)
                    square(None, 1, w, UC)
                with sp.Fori(1 if l == 0 else 0, MIX_UNITS // 2) as i:
                    for s in range(2):
                        square(i * 2 + (first_mix[l] + s), s, w, i * (2 * UC) + s * UC, (l, s) == (0, 0))
                sp.wait_ge(h_split, 2 * l * KC + KC)
                sp.dma_start(wsrow[:], t["mlp_w_s"][l].rearrange("g i j -> i g j")).then_inc(late_landed, 16)
                with sp.Fori(0, GROUPS // 2) as i:
                    for j in range(2 * GROUP_UNITS):
                        n = i * (2 * GROUP_UNITS) + (first_group[l] + j)
                        g, u = divmod(j, GROUP_UNITS)
                        if u < NBR:
                            square(n, j % 2, w, i * (2 * UC) + (MIX_W + u * D + g * UC))
                        else:
                            square(n, j % 2, t["w_branch"][l].rearrange("b r n -> (b r) n"), i * (2 * UC) + g * UC, (l, g) == (0, 0))
                with sp.Fori(0, OUT_UNITS // 2) as i:
                    for s in range(2):
                        square(i * 2 + (first_out[l] + s), s, t["w_out"][l], i * (2 * UC) + s * UC, (l, s) == (0, 0))
                if l == 0:
                    done = 0
                    for k, chunks in enumerate(FFN_PARTS):
                        w1 = t["ffn_w1"][0][:, done * P:(done + chunks) * P]
                        w3 = t["ffn_w3"][0][:, done * P:(done + chunks) * P]
                        w2 = t["ffn_w2"][0][done * P:(done + chunks) * P, :]
                        done += chunks
                        with sp.Fori(0, chunks // 2) as i:
                            for s in range(2):
                                up(i * 2 + (first_part[k] + s), s, w1, w3, i * (2 * P) + s * P)
                        with sp.Fori(0, KC // 2) as i:
                            for s in range(2):
                                down(i * 2 + (first_part[k] + chunks + s), s, w2, chunks, i * (2 * P) + s * P)
                else:
                    def gathered_unit(e, u, first):
                        name = "moe_w2" if u >= 2 * UPS else ("moe_w1", "moe_w3")[u % 2]
                        w = t[name][0][ds(e, 1)].rearrange("o r n -> (o r) n") if not first else t[name][0][0]
                        src = w.rearrange("(c p) n -> p c n", p=P)
                        for k, half in enumerate(UPPER_FIRST):
                            at_zero = u in (0, 1, 2 * UPS)
                            if (not first or u >= RING) and not (at_zero and k):
                                sp.wait_ge(elo_ready, e * (2 * GU) + (2 * (u - RING) + (2 if at_zero else k + 1)))
                            if u < 2 * UPS:
                                dst = eraw[:, u % RING].rearrange("p (c n) -> p c n", c=KC)
                                col, c = (u // 2) * UC, half * (KC // 2)
                                dst, part = dst[:, c:c + KC // 2], src[:, c:c + KC // 2, col:col + UC]
                            else:
                                c = 2 * (u - 2 * UPS) + half
                                dst = eraw[:, u % RING].rearrange("p (c n) -> p c n", c=2)
                                dst, part = dst[:, half:half + 1], src[:, c:c + 1, :]
                            sp.dma_start(dst, part).then_inc(eraw_landed[u % RING][half], 16)

                    sp.wait_ge(w_used, first_exp)
                    for u in range(RING):
                        gathered_unit(0, u, True)
                    sp.wait_ge(most_ready, 1)
                    fullest = sp.value_load(most_i[0:1, 0:1], min_val=0, max_val=SEQ)
                    with sp.If(fullest < P + 1):
                        for u in range(RING, GU):
                            gathered_unit(0, u, True)
                        with sp.Fori(0, NEXP - 1) as e:
                            for u in range(GU):
                                gathered_unit(e + 1, u, False)
                    with sp.Else():
                        for s in range(RING):
                            for half in range(2):
                                sp.wait_ge(eraw_landed[s][half], 16)
                        with sp.Fori(0, NEXP) as e:
                            w1, w3, w2 = (t[name][0][ds(e, 1)].rearrange("o r n -> (o r) n")
                                          for name in ("moe_w1", "moe_w3", "moe_w2"))
                            with sp.Fori(0, EXP_CHUNKS // 2) as i:
                                for s in range(2):
                                    up(e * EXP_UNITS + i * 2 + (first_exp + s), s, w1, w3, i * (2 * P) + s * P)
                            with sp.Fori(0, KC // 2) as i:
                                for s in range(2):
                                    down(e * EXP_UNITS + i * 2 + (first_exp + EXP_CHUNKS + s), s, w2, EXP_CHUNKS, i * (2 * P) + s * P)

            sp.wait_ge(out_placed, KC)
            sp.dma_start(t["out"].rearrange("b (n p) d -> p (b n) d", p=P), xrows[:, 0:LBLK, :]).then_inc(out_stored, 16)
            sp.wait_ge(out_stored, 16)

        loaded = 16 * len(setup_loads)

        class Steps:

            def __init__(self, eng, semaphore):
                self.eng, self.semaphore, self.base, self.n = eng, semaphore, None, 0

            def __call__(self, ins):
                self.n += 1
                ins.then_inc(self.semaphore, 1)
                self.eng.wait_ge(self.semaphore, self.n if self.base is None else self.base + self.n)

            def loop(self, done, per):
                self.base, self.start = done * per, self.n

            def end(self, turns, per):
                assert self.n - self.start == per, (self.n - self.start, per)
                self.base, self.n = None, self.start + turns * per

        @block.tensor
        def _(pe):
            def mm(out, lhsT, rhs, start=True, stop=True):
                return nc.tensor.matmul(out, lhsT, rhs, start=start, stop=stop)

            def mm3(out, a, b, start, stop):
                mm(out, a[0], b[0], start, False)
                mm(out, a[0], b[1], False, False)
                return mm(out, a[1], b[0], False, stop)

            def w(slot, col, n):
                return whi[:, slot, col:col + n], wlo[:, slot, col:col + n]

            def h(k, a, b):
                return hhi[:, k, a:b], hlo[:, k, a:b]

            pe.wait_ge(inputs_landed, loaded)
            pe.wait_ge(ones_set, 1)
            nc.tensor.transpose(psB[:, 0, 0:P], rows1[:], ident[:])
            nc.tensor.transpose(psB[:, 0, P:P + 24], rows2[:], ident[0:24, 0:24]).then_inc(setup_turned, 1)
            for c in range(KC):
                if c >= 4:
                    pe.wait_ge(x_placed, c - 3)
                for b in range(NBLK):
                    last = nc.tensor.transpose(psA[:, c % 4, b * P:(b + 1) * P], xrows[:, b, c * P:(c + 1) * P], ident[:])
                last.then_inc(x_turned, 1)
            pe.wait_ge(silu_ready, 1)

            def mod_multiply(out, slot):
                for k in range(KC):
                    last = mm(out, siluc[:, k, :], slot[:, k, :], k == 0, k == KC - 1)
                return last

            def turn_rows(n, where, bank):
                pe.wait_ge(mod_copied, n + 1)
                if not (isinstance(n, int) and n == 0):
                    pe.wait_ge(mod_added, n + 0)
                for q in range(MG // P):
                    last = mm(bank[:, 2 * q:2 * q + 2],
                              modrows[where][:, n % 2 if isinstance(n, int) else 0, q * P:(q + 1) * P],
                              ident[0:2, 0:2], True, True)
                last.then_inc(mod_turned, 1)

            for g in range(EARLY_GROUPS):
                if g >= 2:
                    pe.wait_ge(mod_copied, g - 1)
                for x in range(2):
                    u = 2 * g + x
                    pe.wait_ge(mod_landed[u % MOD_RING], 16 * (u // MOD_RING + 1))
                    mod_multiply(psB[0:2, 2 + g % 2, x * UC:(x + 1) * UC], modring[:, u % MOD_RING]).then_inc(mod_used, 1)
                if g:
                    turn_rows(g - 1, 0, psB[:, 1])
            turn_rows(EARLY_GROUPS - 1, 0, psB[:, 1])

            def norm(k, T):
                pe.wait_ge(squares, k * KC + KC)
                if k == 0:
                    pe.wait_ge(setup_copied, 1)
                for c in range(KC):
                    last = mm(psB[:, 0, 0:T], ones[:], hf[:, c, 0:T], c == 0, c == KC - 1)
                last.then_inc(meansq, 1)
                pe.wait_ge(h_split, k * KC + KC)

            def arrived(n):
                pe.wait_ge(lo_ready, n * 2 + 2)

            def two_chunks(slot, pair, b, T):
                for j in range(2):
                    for k in range(KC):
                        last = mm3(psA[:, 2 * pair + j, 0:T], w(slot, k * UC + j * P, P), b(k), k == 0, k == KC - 1)
                return last

            def turn_heads(l, m, heads, col):
                pe.wait_ge(heads_ready, 3 * l + m + 1)
                for j in range(heads):
                    if j >= 4:
                        pe.wait_ge(head_placed, heads_before(l, m) + j - 3)
                    for b in range(NBLK):
                        last = nc.tensor.transpose(psA[0:HD, j % 4, b * P:(b + 1) * P],
                                                   mix[:, b, col + j * HD:col + (j + 1) * HD], ident[:])
                    last.then_inc(head_turned, 1)
                pe.wait_ge(head_placed, heads_before(l, m) + heads)

            def mod_half(l, x):
                n = l * MOD_GROUPS + EARLY_GROUPS + x // 4
                pe.wait_ge(modh_landed[x % 2], 16 * (l * HALVES // 2 + x // 2 + 1))
                if x % 4 == 0 and x:
                    pe.wait_ge(mod_copied, n)
                mod_multiply(psA[0:2, 2, (x % 4) * P:(x % 4 + 1) * P], modhalf[:, x % 2]).then_inc(modh_used, 1)
                if x % 4 == 1 and x % (HALVES // 2) != 1:
                    turn_rows(n - 1, 1, psA[:, 3])

            def attention(l, m, vcol):
                items = attention_items(l)
                n = len(items)
                per = HALVES // (2 * n)
                for step in range(n + 2):
                    if step < n:
                        i = step
                        hd, b, k0, nk = items[i]
                        if i >= 2:
                            pe.wait_ge(exp_ready, items_before(l, m) + i - 1)
                        mm(psB[:, i % 2, 0:nk], headsT[:, hd, b * P:(b + 1) * P],
                           headsT[:, NH + hd // 2, k0:k0 + nk]).then_inc(scores_ready, 1)
                    if 1 <= step <= n:
                        i = step - 1
                        hd, b, k0, nk = items[i]
                        pe.wait_ge(exp_ready, items_before(l, m) + i + 1)
                        if i >= 2:
                            pe.wait_ge(probs_placed, items_before(l, m) + i - 1)
                        for y in range(nk // P):
                            last = nc.tensor.transpose(psA[:, i % 2, y * P:(y + 1) * P],
                                                       expS[:, i % 2, y * P:(y + 1) * P], ident[:])
                        last.then_inc(probs_turned, 1)
                    if step >= 2:
                        i = step - 2
                        hd, b, k0, nk = items[i]
                        pe.wait_ge(probs_placed, items_before(l, m) + i + 1)
                        if i >= 2:
                            pe.wait_ge(attn_done, items_before(l, m) + i - 1)
                        v = vcol + (hd // 2) * HD
                        for y in range(nk // P):
                            last = mm(psB[:, 2 + i % 2, 0:HD], expT[:, i % 2, y * P:(y + 1) * P],
                                      mix[:, k0 // P + y, v:v + HD], y == 0, y == nk // P - 1)
                        last.then_inc(values_ready, 1)
                    if step < n:
                        for x in range(per):
                            mod_half(l, m * HALVES // 2 + step * per + x)
                last_group = l * MOD_GROUPS + EARLY_GROUPS + (m + 1) * HALVES // 8 - 1
                turn_rows(last_group, 1, psA[:, 3])
                pe.wait_ge(mod_added, last_group + 1)
                pe.wait_ge(attn_done, items_before(l, m) + n)

            def retention(l):
                pe.wait_ge(kdec_ready, l + 1)
                for d, order in enumerate(((2, 3, 0), (3, 2, 1))):
                    for step, b in enumerate(order):
                        for hd in range(NH):
                            last = mm(psB[0:HD, 2 * d + step // 2, (step % 2) * 256 + hd * HD:(step % 2) * 256 + (hd + 1) * HD],
                                      kdec[:, d, b, hd * HD:(hd + 1) * HD], mix[:, b, COL_RV + hd * HD:COL_RV + (hd + 1) * HD])
                last.then_inc(kv_ready, 1)

                def qk(b):
                    if b >= 2:
                        pe.wait_ge(qk_decayed[l], b - 1)
                    for hd in range(NH):
                        last = mm(psA[:, b % 2, hd * P:(hd + 1) * P], headsT[:, NH + hd, b * P:(b + 1) * P],
                                  headsT[:, hd, b * P:(b + 1) * P])
                    last.then_inc(qk_ready[l], 1)

                before = ((1, 2), (2, 1), (None, 0), (0, None))
                qk(0)
                pe.wait_ge(states_ready, l + 1)
                for b in range(blocks_of(l)):
                    if b + 1 < blocks_of(l):
                        qk(b + 1)
                    pe.wait_ge(qk_decayed[l], b + 1)
                    if b >= 2:
                        pe.wait_ge(ret_taken[l], b - 1)
                    for hd in range(NH):
                        last = mm(psA[:, 2 + b % 2, hd * HD:(hd + 1) * HD], expS[:, b % 2, hd * P:(hd + 1) * P],
                                  mix[:, b, COL_RV + hd * HD:COL_RV + (hd + 1) * HD])
                    for d, state in enumerate((stateF, stateB)):
                        if before[b][d] is not None:
                            for hd in range(NH):
                                last = mm(psB[:, b % 2, d * 256 + hd * HD:d * 256 + (hd + 1) * HD],
                                          headsT[:, hd, b * P:(b + 1) * P], state[:, before[b][d], hd * HD:(hd + 1) * HD])
                    last.then_inc(ret_ready[l], 1)

            def feed_forward(k, chunks, T, at_unit, up_done, down_done, beside=False):
                with pe.Fori(0, chunks // 2) as i:
                    for s in range(2):
                        if s == 0:
                            pe.wait_ge(down_taken[k], down_done + 2)
                        arrived(i * 2 + (at_unit + s))
                        pe.wait_ge(up_taken[k], i * 2 + (up_done + s + 1))
                        for j in range(2):
                            for c in range(KC):
                                last = mm3(psA[:, 2 * s + j, 0:T], w(s, (j * KC + c) * P, P), h(c, 0, T), c == 0, c == KC - 1)
                        last.then_inc(w_used, 1)
                with pe.Fori(0, KC // 2) as i:
                    for s in range(2):
                        if s == 0:
                            pe.wait_ge(up_taken[k], up_done + (chunks + 2))
                        arrived(i * 2 + (at_unit + (chunks + s)))
                        pe.wait_ge(down_taken[k], i * 2 + (down_done + s + 1))
                        for c in range(chunks):
                            last = mm3(psA[:, 2 * s, 0:T], w(s, c * P, P),
                                       (hidhi[:, c * T:(c + 1) * T], hidlo[:, c * T:(c + 1) * T]), c == 0, c == chunks - 1)
                        last.then_inc(w_used, 1)
                        if beside and s == 0:
                            for x in range(2):
                                pe.wait_ge(modf_landed[x], i * 16 + 16)
                                mod_multiply(psB[0:2, 2, x * UC:(x + 1) * UC], modfull[:, x]).then_inc(modf_used, 1)
                        elif beside:
                            turn_rows(i + MOD_GROUPS, 2, psB[:, 1])

            for l in range(DEPTH):
                T = blocks_of(l) * P
                norm(2 * l, TOK)
                with pe.Fori(0, MIX_UNITS // 2) as i:
                    for s in range(2):
                        arrived(i * 2 + (first_mix[l] + s))
                        pe.wait_ge(mix_taken[l], i * 2 + (s + 1))
                        for b in range(NBLK):
                            for k in range(KC):
                                last = mm3(psA[:, 2 * s + b // 2, (b % 2) * UC:(b % 2 + 1) * UC],
                                           h(k, b * P, (b + 1) * P), w(s, k * UC, UC), k == 0, k == KC - 1)
                        last.then_inc(w_used, 1)
                pe.wait_ge(mix_taken[l], MIX_UNITS + 2)
                pe.wait_ge(late_landed, 16 * (l + 1))
                for g in range(NH):
                    last = nc.tensor.transpose(psB[:, 0, g * P:(g + 1) * P], wsrow[:, g, :], ident[:])
                last.then_inc(ws_turned, 1)
                pe.wait_ge(ws_copied, l + 1)
                pe.wait_ge(v_normed, l + 1)
                for g in range(NH):
                    last = mm(psB[:, 1 + g // 2, (g % 2) * 256:(g % 2 + 1) * 256], wsT[:, g, :],
                              mix[:, :, COL_V + g * HD:COL_V + (g + 1) * HD])
                last.then_inc(mlp_mixed, 1)
                turn_heads(l, 0, 6, COL_WQ)
                pe.wait_ge(mlp_done, l + 1)
                attention(l, 0, COL_WV)
                turn_heads(l, 1, 6, COL_GQ)
                attention(l, 1, COL_GV)
                turn_heads(l, 2, 8, COL_RQ)
                retention(l)
                pe.wait_ge(branches_ready, l + 1)
                for c in range(KC):
                    if c >= 4:
                        pe.wait_ge(br_lo[l], c - 3)
                    col = OUT_COLS[c // 2] + (c % 2) * P
                    for b in range(T // P):
                        last = nc.tensor.transpose(psA[:, c % 4, b * P:(b + 1) * P], mix[:, b, col:col + P], ident[:])
                    last.then_inc(br_turned[l], 1)
                pe.wait_ge(br_lo[l], KC)
                with pe.Fori(0, GROUPS // 2) as i:
                    for j in range(2 * GROUP_UNITS):
                        g, u = divmod(j, GROUP_UNITS)
                        arrived(i * (2 * GROUP_UNITS) + (first_group[l] + j))
                        if u < NBR:
                            pe.wait_ge(gates_taken[l], i * (2 * NBR) + (g * NBR + u + 1))
                            last = two_chunks(j % 2, u % 2, lambda k: h(k, 0, T), T)
                        else:
                            for c in range(2):
                                for br in range(NBR):
                                    pe.wait_ge(proj_taken[l], i * (4 * NBR) + ((2 * g + c) * NBR + br + 1))
                                    for k in (2 * br, 2 * br + 1):
                                        last = mm3(psB[:, br, 0:T], w(j % 2, k * UC + c * P, P),
                                                   (brhi[:, k, 0:T], brlo[:, k, 0:T]), k == 2 * br, k == 2 * br + 1)
                                    if (c, br) != (1, NBR - 1):
                                        last.then_inc(proj_ready[l], 1)
                        last.then_inc(w_used, 1)
                pe.wait_ge(gates_taken[l], GROUPS * NBR + 2)
                pe.wait_ge(acc_ready[l], KC)
                with pe.Fori(0, OUT_UNITS // 2) as i:
                    for s in range(2):
                        arrived(i * 2 + (first_out[l] + s))
                        pe.wait_ge(out_taken[l], i * 2 + (s + 1))
                        two_chunks(s, s, lambda k: (acchi[:, k, 0:T], acclo[:, k, 0:T]), T).then_inc(w_used, 1)
                norm(2 * l + 1, T)
                if l == 0:
                    for k, chunks in enumerate(FFN_PARTS):
                        if k:
                            pe.wait_ge(down_taken[k - 1], KC + 2)
                        feed_forward(k, chunks, T, first_part[k], 0, 0, k == 0)
                else:
                    pe.wait_ge(router_landed, 16 * 7)
                    for b in range(LBLK):
                        for k in range(KC):
                            for half, part in enumerate((hhi, hlo)):
                                last = mm(psB[:, 1, b * NEXP:(b + 1) * NEXP], part[:, k, b * P:(b + 1) * P].bitcast(F32),
                                          rw[:, k, :], k == 0 and half == 0, k == KC - 1 and half == 1)
                    last.then_inc(router_ready, 1)
                    pe.wait_ge(mask_ready, 1)
                    for b in range(LBLK):
                        for y in range(b + 1):
                            mm(psB[:, 1, 16 + b * NEXP:16 + (b + 1) * NEXP], before[:, 0 if y == b else 1, :],
                               rout[:, 8, y, :], y == 0, y == b)
                    for b in range(LBLK):
                        last = mm(psB[:, 1, 32:32 + NEXP], before[:, 1, :], rout[:, 8, b, :], b == 0, b == LBLK - 1)
                    last.then_inc(counted, 1)
                    pe.wait_ge(out_taken[l], OUT_UNITS + 2)
                    for b in range(LBLK):
                        for c in range(KC):
                            last = nc.tensor.transpose(psA[:, 2 * b + c // 4, (c % 4) * P:(c % 4 + 1) * P],
                                                       hf[:, c, b * P:(b + 1) * P], ident[:])
                            if c % 4 == 3:
                                last.then_inc(tok_turned, 1)
                    pe.wait_ge(tok_lo, 2 * LBLK)
                    pe.wait_ge(most_ready, 1)
                    fullest = pe.value_load(most_i[0:1, 0:1], min_val=0, max_val=SEQ)

                    def spread_rows(rows, turned, copied, done):
                        for b in range(LBLK):
                            last = nc.tensor.transpose(psB[0:NEXP, 2, b * P:(b + 1) * P], rout[:, rows, b, :], ident[:])
                        last.then_inc(turned, 1)
                        pe.wait_ge(copied, 1)
                        for e in range(NEXP):
                            last = mm(psA[:, e // 2, (e % 2) * SEQ:(e % 2 + 1) * SEQ], pick[:, e, :], combT[:])
                        last.then_inc(done, 1)

                    def gather(half, n):
                        if half == 0:
                            pe.wait_ge(gat_ready, n + 1)
                        if half == 1:
                            pe.wait_ge(gathered_placed, n * 2 + 1)
                        part = (tokhi, toklo)[half]
                        for c in range(KC):
                            for b in range(LBLK):
                                last = mm(psB[:, c // 4, (c % 4) * P:(c % 4 + 1) * P], part[:, b, c * P:(c + 1) * P],
                                          gat[:, b, :], b == 0, b == LBLK - 1)
                        last.then_inc(gathered, 1)
                        if half == 1:
                            for b in range(LBLK):
                                w_ = rout[:, 0, b, ds(n, 1)] if not isinstance(n, int) else rout[:, 0, b, n:n + 1]
                                last = mm(psA[:, 3, 0:1], gat[:, b, :].bitcast(F32), w_, b == 0, b == LBLK - 1)
                            last.then_inc(cw_ready, 1)

                    def scatter(half, n):
                        if half == 0:
                            pe.wait_ge(y_lo_ready, n + 1)
                            pe.wait_ge(sca_ready, n + 1)
                        else:
                            pe.wait_ge(scattered_added, n * 2 + 1)
                        for c in range(4 * half, 4 * half + 4):
                            for k, y in enumerate((yhi, ylo)):
                                last = mm(psB[:, (c % 4) // 2, (c % 2) * SEQ:(c % 2 + 1) * SEQ], y[:, c * P:(c + 1) * P], sca[:],
                                          k == 0, k == 1)
                        last.then_inc(scattered, 1)

                    def arrived3(e, u):
                        pe.wait_ge(elo_ready, e * (2 * GU) + (2 * u + 2))

                    def turn_up(e, i):
                        pe.wait_ge(eup_ready, e * UPS + (i + 1))
                        if not (isinstance(e, int) and e == 0 and i == 0):
                            pe.wait_ge(eupT_lo_ready, e * UPS + i)
                        for y in range(2):
                            last = nc.tensor.transpose(psA[:, 2, y * P:(y + 1) * P], eup[:, i % 2, y * P:(y + 1) * P], ident[:])
                        last.then_inc(eup_turned, 1)

                    def gathered_expert(e):
                        first = isinstance(e, int) and e == 0
                        final = isinstance(e, int) and e == NEXP - 1
                        pe.wait_ge(gathered_placed, e * 2 + 2)
                        for u in range(2 * UPS):
                            i, which = divmod(u, 2)
                            arrived3(e, u)
                            if not (first and i == 0):
                                pe.wait_ge(eup_ready if which else eup_silu, e * UPS + i)
                            for k in range(KC):
                                last = mm3(psA[:, which, 0:UC], (ghi[:, k, :], glo[:, k, :]),
                                           (ehi[:, u % RING, k * UC:(k + 1) * UC], elo[:, u % RING, k * UC:(k + 1) * UC]),
                                           k == 0, k == KC - 1)
                            last.then_inc(ew_used, 1)
                            if which and i:
                                turn_up(e, i - 1)
                        if not first:
                            scatter(0, e - 1)
                        for j in range(DOWNS):
                            u = 2 * UPS + j
                            s_ = u % RING
                            arrived3(e, u)
                            pe.wait_ge(eupT_lo_ready, e * UPS + (j + 1))
                            if j == 0 and not first:
                                pe.wait_ge(y_lo_ready, e + 0)
                            for y in range(2):
                                for half in range(2):
                                    col = y * D + half * 512
                                    last = mm3(psB[:, 2 + half, :], (eupT_hi[:, 2 * j + y, :], eupT_lo[:, 2 * j + y, :]),
                                               (ehi[:, s_, col:col + 512], elo[:, s_, col:col + 512]),
                                               j == 0 and y == 0, j == DOWNS - 1 and y == 1)
                            last.then_inc(ew_used, 1)
                            if j == 0 and not first:
                                scatter(1, e - 1)
                            if j == 1:
                                turn_up(e, UPS - 1)
                            if j in (1, 2) and not final:
                                if j == 1 and not first:
                                    pe.wait_ge(scattered_added, e * 2)
                                gather(j - 1, e + 1)

                    with pe.If(fullest < P + 1):
                        spread_rows(9, pos_turned, pos_copied, pos_spread)
                        pe.wait_ge(pos_placed, 1)
                        gather(0, 0)
                        gather(1, 0)
                        gathered_expert(0)
                        with pe.Fori(1, NEXP - 1) as e:
                            gathered_expert(e)
                        gathered_expert(NEXP - 1)
                        for half in range(2):
                            scatter(half, NEXP - 1)
                    with pe.Else():
                        spread_rows(0, combine_turned, combine_copied, comb_spread)
                        pe.wait_ge(comb_spread, 2)
                        with pe.Fori(0, NEXP) as e:
                            feed_forward(2, EXP_CHUNKS, T, e * EXP_UNITS + first_exp, e * EXP_CHUNKS, e * KC)
            pe.wait_ge(x_final, KC)
            for c in range(KC):
                if c >= 4:
                    pe.wait_ge(out_placed, c - 3)
                for b in range(LBLK):
                    last = nc.tensor.transpose(psA[:, c % 4, b * P:(b + 1) * P], xT[:, c, b * P:(b + 1) * P], ident[:])
                last.then_inc(out_turned, 1)

        @block.gpsimd
        def _(pool):
            for l in range(DEPTH):
                w = t["w_mod"][l].rearrange("(c p) n -> p c n", p=P)

                def half_load(x, slot):
                    pool.dma_start(modhalf[:, slot], w[:, :, ds(x * P + 2 * D, P)]).then_inc(modh_landed[slot], 16)

                pool.wait_ge(h_split, 2 * l * KC + KC)
                half_load(0, 0)
                half_load(1, 1)
                with pool.Fori(1, HALVES // 2) as i:
                    for s in range(2):
                        pool.wait_ge(modh_used, i * 2 + (l * HALVES + s - 1))
                        half_load(i * 2 + s, s)
                if l == 0:
                    w = t["w_mod"][1].rearrange("(c p) n -> p c n", p=P)
                    pool.wait_ge(h_split, 2 * KC)
                    for s in range(2):
                        pool.dma_start(modfull[:, s], w[:, :, s * UC:(s + 1) * UC]).then_inc(modf_landed[s], 16)
                    with pool.Fori(1, EARLY_UNITS // 2) as i:
                        for s in range(2):
                            pool.wait_ge(modf_used, i * 2 + (s - 1))
                            pool.dma_start(modfull[:, s], w[:, :, ds(i * (2 * UC) + s * UC, UC)]).then_inc(modf_landed[s], 16)

        @block.scalar
        def _(act):
            step = Steps(act, act_step)

            def f(out, in_, func, **k):
                return nc.scalar.activation(out, in_, func, **k)

            def hi_part(n, slot):
                for h in UPPER_FIRST:
                    act.wait_ge(raw_landed[slot][h], 8 * n + (16 - 8 * slot))
                    part = slice(h * HALF, (h + 1) * HALF)
                    f(whi[:, slot, part], raw[:, slot, part], ACT.Copy).then_inc(hi_ready, 1)

            def next_hi(n, slot):
                act.wait_ge(w_used, n + 1)
                hi_part(n + 2, slot)

            for l in range(DEPTH):
                act.sem_inc(mix_taken[l], 2)
                act.sem_inc(gates_taken[l], 2)

            act.wait_ge(setup_copied, 1)
            f(siluc[:], rowsT[:, 0:16].rearrange("p (w c) -> p c w", w=2), ACT.Silu).then_inc(silu_ready, 1)
            act.wait_ge(lg_ready, 1)
            step(f(lgx[:, 1, :], lgx[:, 1, :], ACT.Exp, scale=-1.0))
            f(lgx[:, 1, :], lgx[:, 1, :], ACT.Ln, bias=1.0).then_inc(lg_steps, 1)
            act.wait_ge(lg_ready, 2)
            for k in range(4):
                last = f(expcol[:, k].rearrange("p l d h -> p (l d h)"), lgx[:, 2, :], ACT.Exp, scale=idx[:, k:k + 1])
            last.then_inc(lg_steps, 1)
            for l in range(DEPTH):
                for hd in range(NH):
                    n = l * NH + hd
                    if n >= 2:
                        act.wait_ge(decay_used, n - 1)
                    for d in range(2):
                        col = (l * 2 + d) * NH + hd
                        last = f(tmp[:, n % 2, d * P:(d + 1) * P], rel[:, d, :], ACT.Exp, scale=lgx[:, 2, col:col + 1])
                    last.then_inc(decay_exp, 1)

            def root(k, ap):
                act.wait_ge(ms_ready, k + 1)
                f(ap, ap, ACT.Sqrt).then_inc(root_ready, 1)

            def norm(k, T):
                for c in range(KC):
                    last = f(hf[:, c, 0:T], xT[:, c, 0:T], ACT.Square)
                    last.then_inc(squares, 1)
                l, second = divmod(k, 2)
                root(l * ROOTS + (NORM2 if second else NORM1), tmp[:, 0, 0:T])
                sh = SH2 if second else SH1
                for c in range(KC):
                    act.wait_ge(xn_ready, k * KC + c + 1)
                    for w in range(T // SEQ):
                        part = hf[:, c, w * SEQ:(w + 1) * SEQ]
                        last = f(part, part, ACT.Identity, scale=gsc[:, l, second, c, w:w + 1], bias=mod[:, l, sh, c, w:w + 1])
                    last.then_inc(h_ready, 1)

            def place_heads(l, m, heads):
                for j in range(heads):
                    act.wait_ge(head_turned, heads_before(l, m) + j + 1)
                    f(headsT[:, j, :], psA[0:HD, j % 4, :], ACT.Copy).then_inc(head_placed, 1)

            def attention(l, m):
                items = attention_items(l)
                n = len(items)
                for t_ in range(n + 1):
                    if t_ < n:
                        i = t_
                        hd, b, k0, nk = items[i]
                        act.wait_ge(max_ready, items_before(l, m) + i + 1)
                        if i >= 2:
                            act.wait_ge(probs_turned, items_before(l, m) + i - 1)
                        if m == 0:
                            f(sinkexp[:, i:i + 1], negmax[:, i:i + 1], ACT.Exp, bias=sink[:, l * NH + hd:l * NH + hd + 1])
                        f(expS[:, i % 2, 0:nk], psB[:, i % 2, 0:nk], ACT.Exp, scale=SCALE, bias=negmax[:, i:i + 1],
                          accum_out=rowsum[:, i:i + 1]).then_inc(exp_ready, 1)
                    if t_ >= 1:
                        i = t_ - 1
                        hd, b, k0, nk = items[i]
                        act.wait_ge(probs_turned, items_before(l, m) + i + 1)
                        if i >= 2:
                            act.wait_ge(values_ready, items_before(l, m) + i - 1)
                        f(expT[:, i % 2, 0:nk], psA[:, i % 2, 0:nk], ACT.Copy).then_inc(probs_placed, 1)

            def feed_forward(k, chunks, T, at_unit, up_done):
                with act.Fori(0, chunks // 2) as i:
                    for s in range(2):
                        next_hi(i * 2 + (at_unit + s), s)
                        act.wait_ge(up_taken[k], i * 2 + (up_done + (s + 1)))
                        f(tmp[:, s, 0:T], psA[:, 2 * s, 0:T], ACT.Silu).then_inc(up_silu[k], 1)

            def down_his(chunks, at_unit, turns):
                with act.Fori(0, turns) as i:
                    for s in range(2):
                        next_hi(i * 2 + (at_unit + (chunks + s)), s)

            for l in range(DEPTH):
                T = blocks_of(l) * P
                if l == 0:
                    act.wait_ge(x_placed, KC)
                    act.wait_ge(mod_ready, 1)
                else:
                    act.wait_ge(down_taken[1], KC + 2)
                norm(2 * l, TOK)
                if l == 0:
                    hi_part(0, 0)
                    hi_part(1, 1)
                for u in range(MIX_UNITS):
                    s = u % 2
                    next_hi(first_mix[l] + u, s)
                    func = ACT.Gelu_apprx_tanh if u < 2 else ACT.Silu if u * UC == COL_RG else ACT.Copy
                    f(mix[:, :, u * UC:(u + 1) * UC], psA[:, 2 * s:2 * s + 2, :].rearrange("p a (b n) -> p (a b) n", n=UC),
                      func).then_inc(mix_taken[l], 1)
                root(l * ROOTS + ROOT_V, stat[:, 0, 0:NBLK * NH])
                root(l * ROOTS + ROOT_W, stat[:, 0, 0:NBLK * 6])
                place_heads(l, 0, 6)
                attention(l, 0)
                root(l * ROOTS + ROOT_G, stat[:, 0, 0:NBLK * 6])
                place_heads(l, 1, 6)
                attention(l, 1)
                place_heads(l, 2, 8)
                root(l * ROOTS + ROOT_GN, stat[:, 0, 0:T // P * NH])
                for c in range(KC):
                    act.wait_ge(br_turned[l], c + 1)
                    f(brhi[:, c, 0:T], psA[:, c % 4, 0:T], ACT.Copy).then_inc(br_hi[l], 1)
                with act.Fori(0, GROUPS // 2) as i:
                    for j in range(2 * GROUP_UNITS):
                        g, u = divmod(j, GROUP_UNITS)
                        next_hi(i * (2 * GROUP_UNITS) + (first_group[l] + j), j % 2)
                        if u == 0:
                            act.wait_ge(gates_used[l], i * 2 + (g + 1))
                        if u < NBR:
                            f(gates[:, u, :, 0:T], psA[:, 2 * (u % 2):2 * (u % 2) + 2, 0:T], ACT.Sigmoid).then_inc(gates_taken[l], 1)
                with act.Fori(0, OUT_UNITS // 2 - l) as i:
                    for s in range(2):
                        next_hi(i * 2 + (first_out[l] + s), s)
                act.wait_ge(out_taken[l], OUT_UNITS + 2)
                norm(2 * l + 1, T)
                if l == 0:
                    for k, chunks in enumerate(FFN_PARTS):
                        feed_forward(k, chunks, T, first_part[k], 0)
                        down_his(chunks, first_part[k], KC // 2)
                else:
                    act.wait_ge(h_split, 3 * KC + KC)
                    act.dma_start(rw[:], t["router_w"][0].rearrange("(c p) e -> p c e", p=P)).then_inc(router_landed, 16)
                    act.dma_start(rb[:], t["router_b"].broadcast_to([P, NEXP])).then_inc(router_landed, 16)
                    act.dma_start(eidx[:], t["k_eidx"]).then_inc(router_landed, 16)
                    act.dma_start(pick[:], t["k_pick"]).then_inc(router_landed, 16)
                    act.dma_start(before[:], t["k_before"]).then_inc(router_landed, 16)
                    act.dma_start(slots[:], t["k_slots"]).then_inc(router_landed, 16)
                    act.dma_start(slot_of[:], t["k_idx"]).then_inc(router_landed, 16)
                    act.wait_ge(gap_ready, 1)
                    f(stat[:, 0, 4:6], stat[:, 0, 2:4], ACT.Exp).then_inc(gap_exp, 1)
                    for n in range(2 * LBLK):
                        act.wait_ge(tok_turned, n + 1)
                        f(tokhi[:, n // 2, (n % 2) * 512:(n % 2 + 1) * 512], psA[:, n, :], ACT.Copy).then_inc(tok_hi, 1)
                    act.wait_ge(most_ready, 1)
                    fullest = act.value_load(most_i[0:1, 0:1], min_val=0, max_val=SEQ)

                    def ehi_part(e, u):
                        s_ = u % RING
                        for h in UPPER_FIRST:
                            act.wait_ge(eraw_landed[s_][h], e * (16 * GU // RING) + 16 * (u // RING + 1))
                            part = slice(h * HALF, (h + 1) * HALF)
                            f(ehi[:, s_, part], eraw[:, s_, part], ACT.Copy).then_inc(ehi_ready, 1)

                    def place_up(e, i):
                        act.wait_ge(eup_turned, e * UPS + (i + 1))
                        f(eupT_hi[:, 2 * i:2 * i + 2, :].rearrange("p c n -> p (c n)"), psA[:, 2, 0:2 * P], ACT.Copy).then_inc(eupT_hi_ready, 1)

                    def place_gathered(half, n):
                        act.wait_ge(gathered, n * 2 + (half + 1))
                        f((ghi, glo)[half][:].rearrange("p c n -> p (c n)"), psB[:, 0:2, :].rearrange("p a n -> p (a n)"),
                          ACT.Copy).then_inc(gathered_placed, 1)

                    def gathered_expert(e):
                        first = isinstance(e, int) and e == 0
                        final = isinstance(e, int) and e == NEXP - 1
                        for u in range(GU):
                            i, which = divmod(u, 2)
                            act.wait_ge(ew_used, e * GU + (u + 1))
                            if u < 2 * UPS and not which:
                                if not (first and i < 2):
                                    act.wait_ge(eup_ready, e * UPS + (i - 1))
                                f(tmp[:, i % 2, 0:UC], psA[:, 0, 0:UC], ACT.Silu).then_inc(eup_silu, 1)
                            if not (final and u + RING >= GU):
                                ehi_part(e, u + RING)
                            if u < 2 * UPS and which and i:
                                place_up(e, i - 1)
                            if u == 2 * UPS + 1:
                                place_up(e, UPS - 1)
                            j = u - 2 * UPS
                            if j in (1, 2) and not final:
                                place_gathered(j - 1, e + 1)
                        act.wait_ge(cw_placed, e + 1)
                        c = cw[:, e:e + 1] if isinstance(e, int) else cw[:, ds(e, 1)]
                        f(yhi[:], psB[:, 2:4, :].rearrange("p a n -> p (a n)"), ACT.Copy, scale=c).then_inc(y_hi_ready, 1)

                    with act.If(fullest < P + 1):
                        act.wait_ge(pos_spread, 1)
                        f(posB[:].rearrange("p e n -> p (e n)"), psA[:].rearrange("p a n -> p (a n)"), ACT.Copy).then_inc(pos_placed, 1)
                        for u in range(RING):
                            ehi_part(0, u)
                        for half in range(2):
                            place_gathered(half, 0)
                        gathered_expert(0)
                        with act.Fori(1, NEXP - 1) as e:
                            gathered_expert(e)
                        gathered_expert(NEXP - 1)
                    with act.Else():
                        act.wait_ge(comb_spread, 1)
                        f(combB[:].rearrange("p e n -> p (e n)"), psA[:].rearrange("p a n -> p (a n)"), ACT.Copy).then_inc(comb_spread, 1)
                        for s in range(2):
                            hi_part(first_exp + s, s)
                        with act.Fori(0, NEXP - 1) as e:
                            feed_forward(2, EXP_CHUNKS, T, e * EXP_UNITS + first_exp, e * EXP_CHUNKS)
                            down_his(EXP_CHUNKS, e * EXP_UNITS + first_exp, KC // 2)
                        e = NEXP - 1
                        feed_forward(2, EXP_CHUNKS, T, e * EXP_UNITS + first_exp, e * EXP_CHUNKS)
                        down_his(EXP_CHUNKS, e * EXP_UNITS + first_exp, KC // 2 - 1)

        @block.vector
        def _(dve):
            step = Steps(dve, dve_step)
            V = nc.vector

            def tt(out, a, b, op):
                return V.tensor_tensor(out, a, b, op)

            def lo_part(n, slot):
                for k, h in enumerate(UPPER_FIRST):
                    dve.wait_ge(hi_ready, n * 2 + (k + 1))
                    part = slice(h * HALF, (h + 1) * HALF)
                    tt(wlo[:, slot, part], raw[:, slot, part], whi[:, slot, part].bitcast(F32), ALU.subtract).then_inc(lo_ready, 1)

            def split(hi, lo, x):
                step(V.tensor_copy(hi, x))
                return tt(lo, x, hi.bitcast(F32), ALU.subtract)

            V.memset(ones[:], 1.0 / D).then_inc(ones_set, 1)
            for l in range(DEPTH):
                dve.sem_inc(gates_used[l], 1)
                dve.sem_inc(proj_taken[l], NBR)
                dve.sem_inc(out_taken[l], 2)
            for k in range(3):
                dve.sem_inc(up_taken[k], 2)
                dve.sem_inc(down_taken[k], 2)
            dve.wait_ge(inputs_landed, loaded)
            step(V.tensor_scalar(lgx[:, 1, :], lgx[:, 0, :], -1.0, None, ALU.mult))
            tt(lgx[:, 1, :], lgx[:, 0, :], lgx[:, 1, :], ALU.max).then_inc(lg_ready, 1)
            V.tensor_scalar(nsink[:], sink[:], -1.0, None, ALU.mult)
            dve.wait_ge(setup_turned, 1)
            V.tensor_copy(rowsT[:], psB[:, 0, P:P + 24])
            V.tensor_copy(vecT[:], psB[:, 0, 0:P]).then_inc(setup_copied, 1)
            dve.wait_ge(lg_steps, 1)
            step(V.tensor_scalar(lgx[:, 0, :], lgx[:, 0, :], 0.0, None, ALU.min))
            tt(lgx[:, 2, :], lgx[:, 0, :], lgx[:, 1, :], ALU.subtract).then_inc(lg_ready, 1)
            for c in range(KC):
                dve.wait_ge(x_turned, c + 1)
                V.tensor_copy(xT[:, c, :], psA[:, c % 4, :]).then_inc(x_placed, 1)
            for n in range(DEPTH * NH):
                l, hd = divmod(n, NH)
                dve.wait_ge(decay_exp, n + 1)
                step(tt(tmp[:, n % 2, 0:2 * P].rearrange("p (d n) -> p d n", d=2), tmp[:, n % 2, 0:2 * P].rearrange("p (d n) -> p d n", d=2),
                        rel[:, 2:4, :], ALU.mult))
                tt(decay[:, l, hd, :], tmp[:, n % 2, 0:P], tmp[:, n % 2, P:2 * P], ALU.add).then_inc(decay_used, 1)
            dve.wait_ge(lg_steps, 2)
            for k, d in ((1, 0), (2, 1)):
                for l in range(DEPTH):
                    step(V.tensor_scalar(expcol[:, k, l, d, :], expcol[:, k, l, d, :], SCALE, None, ALU.mult))
            dve.wait_ge(setup_copied, 1)
            modcols = mod[:].rearrange("p l s c w -> p (l s c) w")

            def copy_rows(n, where, bank):
                V.tensor_copy(modrows[where][:, n % 2 if isinstance(n, int) else 0, :], bank).then_inc(mod_copied, 1)

            def add_bias(n, bank):
                dve.wait_ge(mod_turned, n + 1)
                part = slice(4 * n, 4 * n + 4) if isinstance(n, int) else ds(n * 4, 4)
                tt(modcols[:, part, :], bank[:, 0:8].rearrange("p (n w) -> p n w", w=2),
                   vecT[:, part].unsqueeze(2).broadcast_to([P, 4, 2]), ALU.add).then_inc(mod_added, 1)

            def scales(l, second):
                dve.wait_ge(mod_added, l * MOD_GROUPS + (MOD_GROUPS if second else EARLY_GROUPS))
                w = vecT[:, 96 + 16 * second + 8 * l:96 + 16 * second + 8 * l + 8].unsqueeze(2).broadcast_to([P, KC, 2])
                step(V.tensor_scalar(gsc[:, l, second], mod[:, l, SC2 if second else SC1], 1.0, None, ALU.add))
                step(tt(gsc[:, l, second], gsc[:, l, second], w, ALU.mult))

            for g in range(EARLY_GROUPS):
                dve.wait_ge(mod_used, 2 * g + 2)
                if g >= 2:
                    dve.wait_ge(mod_turned, g - 1)
                copy_rows(g, 0, psB[0:2, 2 + g % 2, :])
                if g:
                    add_bias(g - 1, psB[:, 1])
            add_bias(EARLY_GROUPS - 1, psB[:, 1])
            scales(0, 0)
            dve.sem_inc(mod_ready, 1)

            def norm(k, T):
                l, second = divmod(k, 2)
                dve.wait_ge(meansq, k + 1)
                V.tensor_scalar(tmp[:, 0, 0:T], psB[:, 0, 0:T], EPS, None, ALU.add).then_inc(ms_ready, 1)
                dve.wait_ge(root_ready, l * ROOTS + (NORM2 if second else NORM1) + 1)
                step(V.reciprocal(tmp[:, 0, 0:T], tmp[:, 0, 0:T]))
                for c in range(KC):
                    tt(hf[:, c, 0:T], xT[:, c, 0:T], tmp[:, 0, 0:T], ALU.mult).then_inc(xn_ready, 1)
                for c in range(KC):
                    dve.wait_ge(h_ready, k * KC + c + 1)
                    split(hhi[:, c, 0:T], hlo[:, c, 0:T], hf[:, c, 0:T]).then_inc(h_split, 1)

            def heads_view(col, heads, nb=NBLK):
                return mix[:, 0:nb, col:col + heads * HD].rearrange("p b (h d) -> p b h d", d=HD)

            def per_head(a, nb, heads, n=HD):
                if a.shape[1] == heads and nb * heads != heads:
                    return a.unsqueeze(1).unsqueeze(3).broadcast_to([P, nb, heads, n])
                return a.rearrange("p (b h) -> p b h", b=nb).unsqueeze(3).broadcast_to([P, nb, heads, n])

            def rms(col, heads, root):
                x, n = heads_view(col, heads), NBLK * heads
                sq = scrA[:, 0:n * HD].rearrange("p (b h d) -> p b h d", b=NBLK, d=HD)
                step(tt(sq, x, x, ALU.mult))
                step(V.tensor_reduce(stat[:, 0, 0:n], scrA[:, 0:n * HD].rearrange("p (n d) -> p n d", d=HD), AX_X, ALU.add))
                V.tensor_scalar(stat[:, 0, 0:n], stat[:, 0, 0:n], 1.0 / HD, EPS, ALU.mult, ALU.add).then_inc(ms_ready, 1)
                dve.wait_ge(root_ready, root + 1)
                step(V.reciprocal(stat[:, 0, 0:n], stat[:, 0, 0:n]))
                step(tt(x, x, per_head(stat[:, 0, 0:n], NBLK, heads), ALU.mult))

            def rope(col, heads, table, nb):
                x = mix[:, 0:nb, col:col + heads * HD].rearrange("p b (h t d) -> p b h t d", t=2, d=HD // 2)
                x1, x2 = x[:, :, :, 0, :], x[:, :, :, 1, :]
                cos, sin = (table[:, k, 0:nb, :].unsqueeze(2).broadcast_to([P, nb, heads, HD // 2]) for k in range(2))
                n = nb * heads * HD // 2
                a, b = (s[:, 0:n].rearrange("p (b h d) -> p b h d", b=nb, h=heads) for s in (scrA, scrB))
                tt(a, x1, sin, ALU.mult)
                step(tt(b, x2, sin, ALU.mult))
                tt(x1, x1, cos, ALU.mult)
                step(tt(x2, x2, cos, ALU.mult))
                tt(x1, x1, b, ALU.subtract)
                return tt(x2, x2, a, ALU.add)

            def attention_heads(l, m, col, root):
                rms(col, 6, l * ROOTS + root)
                for k, (c, heads) in enumerate(((col, NH), (col + NH * HD, 2))):
                    x = heads_view(c, heads)
                    wt = qkw[:, l, 2 * m + k, :].unsqueeze(1).unsqueeze(1).broadcast_to([P, NBLK, heads, HD])
                    last = tt(x, x, wt, ALU.mult)
                step(last)
                rope(col, 6, axial, LBLK).then_inc(heads_ready, 1)

            def attention(l, m):
                items = attention_items(l)
                n = len(items)
                per = HALVES // (2 * n)
                groups = l * MOD_GROUPS + EARLY_GROUPS + m * HALVES // 8
                for t_ in range(n + 2):
                    if t_ < n:
                        i = t_
                        hd, b, k0, nk = items[i]
                        dve.wait_ge(scores_ready, items_before(l, m) + i + 1)
                        s = psB[:, i % 2, 0:nk]
                        if m == 0 and b < LBLK:
                            other = psB[:, i % 2, (1 - b) * P:(2 - b) * P]
                            step(tt(other, other, wmask[:, b, :], ALU.add))
                        step(V.tensor_reduce(negmax[:, i:i + 1], s, AX_X, ALU.max))
                        if m == 0:
                            V.tensor_scalar(negmax[:, i:i + 1], negmax[:, i:i + 1], -SCALE, nsink[:, l * NH + hd:l * NH + hd + 1],
                                            ALU.mult, ALU.min).then_inc(max_ready, 1)
                        else:
                            V.tensor_scalar(negmax[:, i:i + 1], negmax[:, i:i + 1], -SCALE, None, ALU.mult).then_inc(max_ready, 1)
                    if t_ >= 2:
                        i = t_ - 2
                        hd, b, k0, nk = items[i]
                        dve.wait_ge(values_ready, items_before(l, m) + i + 1)
                        if m == 0:
                            step(tt(rowsum[:, i:i + 1], rowsum[:, i:i + 1], sinkexp[:, i:i + 1], ALU.add))
                        step(V.reciprocal(rowsum[:, i:i + 1], rowsum[:, i:i + 1]))
                        col = OUT_COLS[m + 1] + hd * HD
                        V.tensor_scalar(mix[:, b, col:col + HD], psB[:, 2 + i % 2, 0:HD], rowsum[:, i:i + 1], None,
                                        ALU.mult).then_inc(attn_done, 1)
                    done = (t_ + 1) * per
                    if t_ < n and done % 4 == 0:
                        g = groups + done // 4 - 1
                        if g > groups:
                            add_bias(g - 1, psA[:, 3])
                        dve.wait_ge(modh_used, l * HALVES + m * HALVES // 2 + done)
                        copy_rows(g, 1, psA[0:2, 2, :])
                add_bias(groups + HALVES // 8 - 1, psA[:, 3])

            def retention(l):
                nb = blocks_of(l)
                k = heads_view(COL_RK, NH)
                for d, e in enumerate((1, 2)):
                    kd = kdec[:, d].rearrange("p b (h d) -> p b h d", d=HD)
                    last = tt(kd, k, per_head(expcol[:, e, l, d, :], NBLK, NH), ALU.mult)
                last.then_inc(kdec_ready, 1)
                dve.wait_ge(kv_ready, l + 1)
                for d, state in enumerate((stateF, stateB)):
                    cd = expcol[0:HD, 3, l, d, :].unsqueeze(2).broadcast_to([HD, NH, HD])
                    kv = psB[0:HD, 2 * d:2 * d + 2, :].rearrange("p a (b n) -> p (a b) n", b=2)
                    step(V.tensor_copy(state[:, 0, :], kv[:, 0, :]))
                    for n in (1, 2):
                        new, old = (state[:, x, :].rearrange("p (h d) -> p h d", h=NH) for x in (n, n - 1))
                        step(tt(new, old, cd, ALU.mult))
                        step(tt(state[:, n, :], state[:, n, :], kv[:, n, :], ALU.add))
                dve.sem_inc(states_ready, 1)

                def decayed(b):
                    dve.wait_ge(qk_ready[l], b + 1)
                    if b >= 2:
                        dve.wait_ge(ret_ready[l], b - 1)
                    tt(expS[:, b % 2, :], psA[:, b % 2, :], decay[:, l].rearrange("p h n -> p (h n)"), ALU.mult).then_inc(qk_decayed[l], 1)

                decayed(0)
                for b in range(nb):
                    if b + 1 < nb:
                        decayed(b + 1)
                    dve.wait_ge(ret_ready[l], b + 1)
                    inter = [psB[:, b % 2, d * 256:(d + 1) * 256].rearrange("p (h d) -> p h d", h=NH) for d in range(2)]
                    o = mix[:, b, COL_RQ:COL_RQ + 256]
                    terms = [psA[:, 2 + b % 2, 0:256]]
                    for d, skip in enumerate((2, 3)):
                        if b != skip:
                            scr = (scrA, scrB)[d][:, (b % 3) * 256:(b % 3 + 1) * 256]
                            last = tt(scr.rearrange("p (h d) -> p h d", h=NH), inter[d],
                                      expcol[:, d, l, d, :].unsqueeze(2).broadcast_to([P, NH, HD]), ALU.mult)
                            terms.append(scr)
                    step(last)
                    last = tt(o, terms[0], terms[1], ALU.add)
                    if len(terms) > 2:
                        step(last)
                        last = tt(o, o, terms[2], ALU.add)
                    last.then_inc(ret_taken[l], 1)
                dve.wait_ge(ret_taken[l], nb)
                x, n = heads_view(COL_RQ, NH, nb), nb * NH
                flat = mix[:, 0:nb, COL_RQ:COL_RQ + NH * HD]
                sq = scrA[:, 0:n * HD].rearrange("p (b h d) -> p b h d", b=nb, d=HD)
                step(V.tensor_reduce(stat[:, 1, 0:n].rearrange("p (b h) -> p b h", b=nb), x, AX_X, ALU.add))
                step(V.tensor_scalar(stat[:, 1, 0:n], stat[:, 1, 0:n], 1.0 / HD, None, ALU.mult))
                step(tt(x, x, per_head(stat[:, 1, 0:n], nb, NH), ALU.subtract))
                step(tt(sq, x, x, ALU.mult))
                step(V.tensor_reduce(stat[:, 0, 0:n], scrA[:, 0:n * HD].rearrange("p (n d) -> p n d", d=HD), AX_X, ALU.add))
                V.tensor_scalar(stat[:, 0, 0:n], stat[:, 0, 0:n], 1.0 / HD, EPS, ALU.mult, ALU.add).then_inc(ms_ready, 1)
                dve.wait_ge(root_ready, l * ROOTS + ROOT_GN + 1)
                step(V.reciprocal(stat[:, 0, 0:n], stat[:, 0, 0:n]))
                step(tt(x, x, per_head(stat[:, 0, 0:n], nb, NH), ALU.mult))
                step(tt(flat, flat, gn[:, l, :].unsqueeze(1).broadcast_to([P, nb, NH * HD]), ALU.mult))
                tt(flat, flat, mix[:, 0:nb, COL_RG:COL_RG + NH * HD], ALU.mult).then_inc(branches_ready, 1)

            def add_to_x(l, gate, oc, bank, T):
                for w in range(T // SEQ):
                    x = xT[:, oc, w * SEQ:(w + 1) * SEQ] if isinstance(oc, int) else \
                        xT[:, ds(oc, 1), w * SEQ:(w + 1) * SEQ].rearrange("p o n -> p (o n)")
                    g = mod[:, l, gate, oc, w:w + 1] if isinstance(oc, int) else \
                        mod[:, l, gate, ds(oc, 1), w:w + 1].rearrange("p o n -> p (o n)")
                    last = V.scalar_tensor_tensor(out=x, in0=bank[:, w * SEQ:(w + 1) * SEQ], scalar=g, in1=x,
                                                  op0=ALU.mult, op1=ALU.add)
                return last

            def next_lo(n, slot):
                lo_part(n + 2, slot)

            UP_STEPS = 2

            def ups(k, chunks, T, at_unit, up_done, turns_done):
                with dve.Fori(0, chunks // 2) as i:
                    step.loop(turns_done + i, 2 * UP_STEPS)
                    for s in range(2):
                        next_lo(i * 2 + (at_unit + s), s)
                        dve.wait_ge(up_silu[k], i * 2 + (up_done + (s + 1)))
                        x = tmp[:, s, 0:T]
                        step(tt(x, x, psA[:, 2 * s + 1, 0:T], ALU.mult))
                        split(hidhi[:, ds(i * (2 * T) + s * T, T)], hidlo[:, ds(i * (2 * T) + s * T, T)], x).then_inc(up_taken[k], 1)

            for l in range(DEPTH):
                T = blocks_of(l) * P
                norm(2 * l, TOK)
                if l == 0:
                    lo_part(0, 0)
                    lo_part(1, 1)
                with dve.Fori(0, MIX_UNITS // 2) as i:
                    for s in range(2):
                        next_lo(i * 2 + (first_mix[l] + s), s)
                dve.wait_ge(mix_taken[l], MIX_UNITS + 2)
                dve.wait_ge(ws_turned, l + 1)
                V.tensor_copy(wsT[:].rearrange("p g n -> p (g n)"), psB[:, 0, :]).then_inc(ws_copied, 1)
                rms(COL_V, NH, l * ROOTS + ROOT_V)
                v = mix[:, :, COL_V:COL_V + NH * HD]
                tt(v, v, gv[:, l, :].unsqueeze(1).broadcast_to([P, NBLK, NH * HD]), ALU.mult).then_inc(v_normed, 1)
                attention_heads(l, 0, COL_WQ, ROOT_W)
                dve.wait_ge(mlp_mixed, l + 1)
                for g in range(NH):
                    u = mix[:, :, COL_U + g * HD:COL_U + (g + 1) * HD]
                    mixed = psB[:, 1 + g // 2, (g % 2) * 256:(g % 2 + 1) * 256].rearrange("p (b d) -> p b d", d=HD)
                    last = V.scalar_tensor_tensor(out=u, in0=mixed, scalar=rowsT[:, 16 + l * NH + g:17 + l * NH + g], in1=u,
                                                  op0=ALU.add, op1=ALU.mult)
                last.then_inc(mlp_done, 1)
                attention(l, 0)
                attention_heads(l, 1, COL_GQ, ROOT_G)
                attention(l, 1)
                scales(l, 1)
                dve.wait_ge(attn_done, items_before(l, 1) + len(attention_items(l)))
                step(rope(COL_RQ, NH, rot, NBLK))
                rope(COL_RK, NH, rot, NBLK).then_inc(heads_ready, 1)
                dve.wait_ge(heads_ready, 3 * l + 3)
                retention(l)
                for c in range(KC):
                    dve.wait_ge(br_hi[l], c + 1)
                    tt(brlo[:, c, 0:T], psA[:, c % 4, 0:T], brhi[:, c, 0:T].bitcast(F32), ALU.subtract).then_inc(br_lo[l], 1)
                STEPS = 4 * NBR
                READY = 2 * NBR - 1
                total, new = tmp[:, 0, 0:T], tmp[:, 1, 0:T]
                with dve.Fori(0, GROUPS // 2) as i:
                    step.loop(i, STEPS)
                    for j in range(2 * GROUP_UNITS):
                        g, u = divmod(j, GROUP_UNITS)
                        n = i * (2 * GROUP_UNITS) + (first_group[l] + j)
                        if u < NBR:
                            next_lo(n, j % 2)
                            continue
                        for c in range(2):
                            for br in range(NBR):
                                if (c, br) == (1, NBR - 1):
                                    dve.wait_ge(w_used, n + 1)
                                else:
                                    dve.wait_ge(proj_ready[l], i * (2 * READY) + (g * READY + c * NBR + br + 1))
                                if (c, br) == (0, 0):
                                    dve.wait_ge(gates_taken[l], i * (2 * NBR) + ((g + 1) * NBR + 2))
                                out = total if br == 0 else new
                                ins = tt(out, psB[:, br, 0:T], gates[:, br, c, 0:T], ALU.mult)
                                ins.then_inc(proj_taken[l], 1)
                                dve.wait_ge(proj_taken[l], i * (4 * NBR) + ((2 * g + c) * NBR + br + 1 + NBR))
                                if br:
                                    step(tt(total, total, new, ALU.add))
                            oc = i * (2 * UC // P) + (g * 2 + c)
                            hi, lo = (a[:, ds(oc, 1), 0:T].rearrange("p o n -> p (o n)") for a in (acchi, acclo))
                            step(V.tensor_copy(hi, total))
                            tt(lo, total, hi.bitcast(F32), ALU.subtract).then_inc(acc_ready[l], 1)
                            dve.wait_ge(acc_ready[l], i * (2 * UC // P) + (g * 2 + c + 1))
                        dve.sem_inc(gates_used[l], 1)
                        next_lo(n, j % 2)
                step.end(GROUPS // 2, STEPS)
                def out_pair(i, more):
                    for s in range(2):
                        n = i * 2 + (first_out[l] + s)
                        if more:
                            next_lo(n, s)
                        dve.wait_ge(w_used, n + 1)
                        for j in range(2):
                            last = add_to_x(l, G1, i * 4 + (2 * s + j), psA[:, 2 * s + j], T)
                        last.then_inc(out_taken[l], 1)

                with dve.Fori(0, OUT_UNITS // 2 - l) as i:
                    out_pair(i, True)
                if l:
                    out_pair(OUT_UNITS // 2 - 1, False)
                norm(2 * l + 1, T)
                if l == 0:
                    for k, chunks in enumerate(FFN_PARTS):
                        ups(k, chunks, T, first_part[k], 0, 0)
                        step.end(chunks // 2, 2 * UP_STEPS)
                        with dve.Fori(0, KC // 2) as i:
                            for s in range(2):
                                n = i * 2 + (first_part[k] + chunks + s)
                                next_lo(n, s)
                                dve.wait_ge(w_used, n + 1)
                                add_to_x(0, G2, i * 2 + s, psA[:, 2 * s], T).then_inc(down_taken[k], 1)
                                if k == 0 and s == 0:
                                    dve.wait_ge(modf_used, i * 2 + 2)
                                    copy_rows(i + MOD_GROUPS, 2, psB[0:2, 2, :])
                                elif k == 0:
                                    add_bias(i + MOD_GROUPS, psB[:, 1])
                        dve.wait_ge(down_taken[k], KC + 2)
                    scales(1, 0)
                    continue
                dve.wait_ge(router_landed, 16 * 7)
                dve.wait_ge(router_ready, 1)
                R = [rout[:, k] for k in range(12)]
                spread = [P, LBLK, NEXP]
                def over(col):
                    return stat[:, 0, col:col + LBLK].unsqueeze(2).broadcast_to(spread)
                step(tt(R[1], psB[:, 1, 0:LBLK * NEXP].rearrange("p (b e) -> p b e", b=LBLK),
                        rb[:].unsqueeze(1).broadcast_to(spread), ALU.add))
                for n, logits in enumerate((R[1], R[5])):
                    top = (8, 10)[n]
                    step(V.tensor_reduce(stat[:, 0, top:top + LBLK], logits, AX_X, ALU.max))
                    step(tt(R[2], logits, over(top), ALU.is_equal))
                    step(V.scalar_tensor_tensor(out=R[3], in0=R[2], scalar=-float(NEXP), in1=eidx[:].unsqueeze(1).broadcast_to(spread),
                                                op0=ALU.mult, op1=ALU.add))
                    step(V.tensor_reduce(stat[:, 0, 12:14], R[3], AX_X, ALU.min))
                    step(tt(R[6 + n], R[3], over(12), ALU.is_equal))
                    if n == 0:
                        step(V.scalar_tensor_tensor(out=R[5], in0=R[6], scalar=-BIG, in1=R[1], op0=ALU.mult, op1=ALU.add))
                tt(stat[:, 0, 2:4], stat[:, 0, 10:12], stat[:, 0, 8:10], ALU.subtract).then_inc(gap_ready, 1)
                dve.wait_ge(gap_exp, 1)
                step(V.tensor_scalar(stat[:, 0, 6:8], stat[:, 0, 4:6], 1.0, None, ALU.add))
                step(V.reciprocal(stat[:, 0, 6:8], stat[:, 0, 6:8]))
                step(tt(R[0], R[7], over(4), ALU.mult))
                step(tt(R[0], R[0], R[6], ALU.add))
                step(tt(R[0], R[0], over(6), ALU.mult))
                tt(R[8], R[6], R[7], ALU.add).then_inc(mask_ready, 1)
                dve.wait_ge(counted, 1)
                step(V.scalar_tensor_tensor(out=R[9], in0=psB[:, 1, 16:16 + LBLK * NEXP].rearrange("p (b e) -> p b e", b=LBLK),
                                            scalar=1.0, in1=R[8], op0=ALU.add, op1=ALU.mult))
                step(V.tensor_scalar(R[9], R[9], -1.0, None, ALU.add))
                step(V.tensor_reduce(most[:], psB[:, 1, 32:32 + NEXP], AX_X, ALU.max))
                V.tensor_copy(most_i[:], most[:]).then_inc(most_ready, 1)
                for n in range(2 * LBLK):
                    dve.wait_ge(tok_hi, n + 1)
                    part = slice((n % 2) * 512, (n % 2 + 1) * 512)
                    tt(toklo[:, n // 2, part], psA[:, n, :], tokhi[:, n // 2, part].bitcast(F32), ALU.subtract).then_inc(tok_lo, 1)
                dve.wait_ge(tok_lo, 2 * LBLK)
                step(V.memset(moe[:].rearrange("p c n -> p (c n)"), 0.0))
                dve.wait_ge(most_ready, 1)
                fullest = dve.value_load(most_i[0:1, 0:1], min_val=0, max_val=SEQ)

                def elo_part(e, u):
                    s_ = u % RING
                    for k, h in enumerate(UPPER_FIRST):
                        dve.wait_ge(ehi_ready, e * (2 * GU) + (2 * u + k + 1))
                        part = slice(h * HALF, (h + 1) * HALF)
                        tt(elo[:, s_, part], eraw[:, s_, part], ehi[:, s_, part].bitcast(F32), ALU.subtract).then_inc(elo_ready, 1)

                def build_gather(n):
                    for b in range(LBLK):
                        at_ = R[9][:, b, ds(n, 1)] if not isinstance(n, int) else R[9][:, b, n:n + 1]
                        last = V.tensor_scalar(gat[:, b, :], slots[:], at_, None, ALU.is_equal)
                    last.then_inc(gat_ready, 1)

                def place_up_lo(e, i):
                    dve.wait_ge(eupT_hi_ready, e * UPS + (i + 1))
                    hi, lo = (a[:, 2 * i:2 * i + 2, :].rearrange("p c n -> p (c n)") for a in (eupT_hi, eupT_lo))
                    tt(lo, psA[:, 2, 0:2 * P], hi.bitcast(F32), ALU.subtract).then_inc(eupT_lo_ready, 1)

                def add_scattered(half, n):
                    dve.wait_ge(scattered, n * 2 + (half + 1))
                    m = moe[:, 4 * half:4 * half + 4, :].rearrange("p c n -> p (c n)")
                    tt(m, m, psB[:, 0:2, :].rearrange("p a n -> p (a n)"), ALU.add).then_inc(scattered_added, 1)

                def weights_of_slots(n):
                    dve.wait_ge(cw_ready, n + 1)
                    c = cw[:, n:n + 1] if isinstance(n, int) else cw[:, ds(n, 1)]
                    V.tensor_copy(c, psA[:, 3, 0:1]).then_inc(cw_placed, 1)

                def gathered_expert(e):
                    first = isinstance(e, int) and e == 0
                    final = isinstance(e, int) and e == NEXP - 1
                    if not final:
                        dve.wait_ge(cw_ready, e + 1)
                        build_gather(e + 1)
                    for u in range(GU):
                        i, which = divmod(u, 2)
                        if u < 2 * UPS and which:
                            dve.wait_ge(eup_silu, e * UPS + (i + 1))
                            dve.wait_ge(ew_used, e * GU + (u + 1))
                            if not (first and i < 2):
                                dve.wait_ge(eup_turned, e * UPS + (i - 1))
                            tt(eup[:, i % 2, :], tmp[:, i % 2, 0:UC], psA[:, 1, 0:UC], ALU.mult).then_inc(eup_ready, 1)
                        if u == 2 * UPS - 1 and not first:
                            add_scattered(0, e - 1)
                        if u == 2 * UPS and not first:
                            add_scattered(1, e - 1)
                        if not (final and u + RING >= GU):
                            elo_part(e, u + RING)
                        if u < 2 * UPS and which and i:
                            place_up_lo(e, i - 1)
                        if u == 2 * UPS + 1:
                            place_up_lo(e, UPS - 1)
                        if u == 2 * UPS + 2 and not final:
                            weights_of_slots(e + 1)
                    dve.wait_ge(y_hi_ready, e + 1)
                    c = cw[:, e:e + 1] if isinstance(e, int) else cw[:, ds(e, 1)]
                    V.scalar_tensor_tensor(out=ylo[:], in0=psB[:, 2:4, :].rearrange("p a n -> p (a n)"), scalar=c,
                                           in1=yhi[:].bitcast(F32), op0=ALU.mult, op1=ALU.subtract).then_inc(y_lo_ready, 1)
                    at_ = posB[:, e, :] if isinstance(e, int) else posB[:, ds(e, 1), :].rearrange("p o n -> p (o n)")
                    V.tensor_scalar(sca[:], at_, slot_of[:, 2:3], None, ALU.is_equal).then_inc(sca_ready, 1)

                with dve.If(fullest < P + 1):
                    dve.wait_ge(pos_turned, 1)
                    V.tensor_copy(combT[:], psB[0:NEXP, 2, 0:SEQ]).then_inc(pos_copied, 1)
                    build_gather(0)
                    dve.wait_ge(pos_placed, 1)
                    for u in range(RING):
                        elo_part(0, u)
                    weights_of_slots(0)
                    gathered_expert(0)
                    with dve.Fori(1, NEXP - 1) as e:
                        gathered_expert(e)
                    gathered_expert(NEXP - 1)
                    for half in range(2):
                        add_scattered(half, NEXP - 1)
                    dve.wait_ge(scattered_added, 2 * NEXP)
                with dve.Else():
                    dve.wait_ge(combine_turned, 1)
                    V.tensor_copy(combT[:], psB[0:NEXP, 2, 0:SEQ]).then_inc(combine_copied, 1)
                    dve.wait_ge(comb_spread, 2)
                    for s in range(2):
                        lo_part(first_exp + s, s)
                    start = step.n

                    def expert(e, last_turns):
                        at_unit = e * EXP_UNITS + first_exp
                        per = EXP_CHUNKS * UP_STEPS + KC
                        with dve.Fori(0, EXP_CHUNKS // 2) as i:
                            step.n, step.base = start, e * per + i * (2 * UP_STEPS)
                            for s in range(2):
                                next_lo(i * 2 + (at_unit + s), s)
                                dve.wait_ge(up_silu[2], i * 2 + (e * EXP_CHUNKS + (s + 1)))
                                x = tmp[:, s, 0:T]
                                step(tt(x, x, psA[:, 2 * s + 1, 0:T], ALU.mult))
                                split(hidhi[:, ds(i * (2 * T) + s * T, T)], hidlo[:, ds(i * (2 * T) + s * T, T)], x).then_inc(up_taken[2], 1)

                        def down_pair(i, more):
                            step.n, step.base = start, e * per + (i * 2 + EXP_CHUNKS * UP_STEPS)
                            for s in range(2):
                                n = i * 2 + (at_unit + (EXP_CHUNKS + s))
                                if more:
                                    next_lo(n, s)
                                dve.wait_ge(w_used, n + 1)
                                x = tmp[:, s, SEQ:2 * SEQ]
                                c = combB[:, ds(e, 1), :].rearrange("p o n -> p (o n)")
                                m = moe[:, ds(i * 2 + s, 1), :].rearrange("p o n -> p (o n)")
                                step(tt(x, psA[:, 2 * s, 0:T], c, ALU.mult))
                                tt(m, m, x, ALU.add).then_inc(down_taken[2], 1)

                        with dve.Fori(0, last_turns) as i:
                            down_pair(i, True)
                        if last_turns < KC // 2:
                            down_pair(last_turns, False)

                    with dve.Fori(0, NEXP - 1) as e:
                        expert(e, KC // 2)
                    expert(NEXP - 1, KC // 2 - 1)
                    dve.wait_ge(down_taken[2], NEXP * KC + 2)
                for c in range(KC):
                    V.scalar_tensor_tensor(out=xT[:, c, 0:T], in0=moe[:, c, :], scalar=mod[:, l, G2, c, 0:1], in1=xT[:, c, 0:T],
                                           op0=ALU.mult, op1=ALU.add).then_inc(x_final, 1)
            dve.wait_ge(x_final, KC)
            for c in range(KC):
                dve.wait_ge(out_turned, c + 1)
                V.tensor_copy(xrows[:, 0:LBLK, c * P:(c + 1) * P], psA[:, c % 4, 0:LBLK * P].rearrange("p (b n) -> p b n", n=P)).then_inc(out_placed, 1)


INPUTS = ("x", "c", "ctx", "c_ctx", "w_mod", "b_mod", "g_norm1", "g_norm2", "w_in", "mlp_g_v", "mlp_w_s", "mlp_b_s",
          "win_q_norm", "win_k_norm", "win_sink", "glb_q_norm", "glb_k_norm", "ret_decay", "ret_gn", "w_branch", "w_out",
          "ffn_w1", "ffn_w3", "ffn_w2", "router_w", "router_b", "moe_w1", "moe_w3", "moe_w2")
GRID_W = 64
ROPE_BASE = 10000.0


def shape_constants():
    f = np.float32
    i, j = np.arange(P, dtype=f)[:, None], np.arange(P, dtype=f)[None, :]
    wmask = np.stack([np.where(j <= i, f(0), f(-BIG)), np.where(j >= i, f(0), f(-BIG))], 1)
    rel = np.stack([np.maximum(j - i, 0), np.maximum(i - j - 1, 0), np.where(j >= i, SCALE, 0), np.where(i > j, SCALE, 0)], 1)
    idx = np.concatenate([i + 1, P - 1 - i, i, np.full_like(i, P)], 1)

    def by_block(ang):
        tab = np.stack([np.cos(ang), np.sin(ang)], 0).astype(f)
        return np.ascontiguousarray(tab.reshape(2, -1, P, HD // 2).transpose(2, 0, 1, 3))

    pos = np.arange(SEQ)
    inv = (ROPE_BASE ** (-np.arange(HD // 4, dtype=f) / f(HD // 4))).astype(f)
    axial = np.concatenate([(pos // GRID_W).astype(f)[:, None] * inv, (pos % GRID_W).astype(f)[:, None] * inv], 1)
    inv = (ROPE_BASE ** (-np.arange(HD // 2, dtype=f) / f(HD // 2))).astype(f)
    place = np.concatenate([CTX + np.arange(SEQ), np.arange(CTX)]).astype(f)
    pick = np.zeros((NEXP, NEXP, P), f)
    pick[np.arange(NEXP), np.arange(NEXP)] = 1
    return {"k_ident": np.eye(P, dtype=f), "k_wmask": wmask.astype(f), "k_rel": rel.astype(f), "k_idx": idx.astype(f),
            "k_axial": by_block(axial), "k_rot": by_block(place[:, None] * inv), "k_pick": pick,
            "k_before": np.stack([(i < j), np.ones((P, P), bool)], 1).astype(f), "k_slots": np.tile(j, (P, 1)), "k_eidx": np.tile(np.arange(NEXP, dtype=f), (P, 1))}


def kernel(**inputs):
    import concourse.bacc as bacc
    from concourse.bass_utils import run_bass_kernel_spmd

    nc = bacc.Bacc("TRN2", target_bir_lowering=False, num_devices=1)
    arrays = {name: np.ascontiguousarray(inputs[name]) for name in INPUTS}
    arrays.update(shape_constants())
    tensors = {name: nc.dram_tensor(name, a.shape, mybir.dt.from_np(a.dtype), kind="ExternalInput").ap()
               for name, a in arrays.items()}
    tensors["out"] = nc.dram_tensor("out", (1, SEQ, D), F32, kind="ExternalOutput").ap()
    build_program(nc, tensors)
    return run_bass_kernel_spmd(nc, [arrays], core_ids=[0]).results[0]["out"]
```

```python
from contextlib import ExitStack

import numpy as np

import concourse.bass as bass
from concourse import mybir

F32 = mybir.dt.float32
F32R = mybir.dt.float32r
ALU = mybir.AluOpType
ACT = mybir.ActivationFunctionType
AX_X = mybir.AxisListType.X

P = 128
D = 1024
KC = D // P
SEQ = 256
CTX = 256
TOK = SEQ + CTX
NBLK = TOK // P
LBLK = SEQ // P
HD = 64
NH = 4
DEPTH = 2
MIX_W = 2560
COL_U, COL_V = 0, 256
COL_WQ, COL_WK, COL_WV = 512, 768, 896
COL_GQ, COL_GK, COL_GV = 1024, 1280, 1408
COL_RQ, COL_RK, COL_RV, COL_RG = 1536, 1792, 2048, 2304
OUT_COLS = (COL_U, COL_WQ, COL_GQ, COL_RQ)
NBR = 4
DFF = 2816
DFE = 1792
NEXP = 8
EPS = 1e-6
SCALE = HD ** -0.5
BIG = 1e30
UNIT = 2048
UC = UNIT // KC
MIX_UNITS = MIX_W // UC
GROUPS = D // UC
GROUP_UNITS = NBR + 1
OUT_UNITS = D // UC
MG = 512
EARLY_GROUPS = 2 * D // MG
GATES_FIRST = 2
MOD_GROUPS = 6 * D // MG
EARLY_UNITS = 2 * D // UC
HALVES = 2 * 4 * D // UC
HALF_RING = 4
MOD_RING = 4
FFN_PARTS = (12, 10)
EXP_CHUNKS = DFE // P
EXP_UNITS = EXP_CHUNKS + KC
UPS = DFE // UC
DOWNS = EXP_CHUNKS // 2
GU = 2 * UPS + DOWNS
HALF = UNIT // 2
UPPER_FIRST = (1, 0)
RING = 3
assert GU % RING == 0 and UNIT == 2 * D
UNITS0 = MIX_UNITS + GROUPS * GROUP_UNITS + OUT_UNITS + sum(FFN_PARTS) + 2 * KC
AFTER_V, AFTER_W, AFTER_G, AFTER_R = ((COL_V + 255) // UC, (COL_WK + 127) // UC, (COL_GK + 127) // UC, (COL_RK + 255) // UC)
SH1, SC1, G1, SH2, SC2, G2 = range(6)
ds = bass.ds


def blocks_of(layer):
    return NBLK if layer < DEPTH - 1 else LBLK


def mix_blocks(layer, unit):
    first = unit * UC
    keys_values = (COL_WK, COL_GK, COL_RK, COL_RV)
    return NBLK if layer < DEPTH - 1 or any(first <= c < first + UC for c in keys_values) else LBLK


def head_blocks(layer, j):
    return blocks_of(layer) if j < NH else NBLK


def attention_items(layer):
    return [(h, b, 0, TOK) if b < LBLK else (h, b, SEQ, CTX) for b in range(blocks_of(layer)) for h in range(NH)]


def items_before(layer, mixer):
    return sum(2 * len(attention_items(x)) for x in range(layer)) + mixer * len(attention_items(layer))


def high_ring(layer):
    return 2 if layer < DEPTH - 1 else 4


def halves_ahead(m, item, per):
    first = m * HALVES // 2 + item * per + 2
    return range(first, min(first + per, HALVES))


def heads_before(layer, m):
    return layer * 20 + 6 * m


def build_program(nc, t):
    with ExitStack() as ctx:
        base = 16512
        top = 229344 - 32
        place = {"at": base}
        ctx.enter_context(nc.sbuf_tensor("arena", [P, (top - base) // 4], F32))

        def at(name, shape, dt, offset):
            return nc.alloc_sbuf_tensor_at(name, shape, dt, offset=offset)

        def sb(name, shape, dt=F32):
            size = 4 * int(np.prod(shape[1:]))
            here = place["at"]
            place["at"] = here + (size + 31) // 32 * 32
            assert place["at"] <= top, name
            return at(name, shape, dt, here)

        def sem(name):
            return ctx.enter_context(nc.semaphore(name))

        raw = sb("raw", [P, 2, UNIT])
        whi = sb("whi", [P, 2, UNIT], F32R)
        wlo = sb("wlo", [P, 2, UNIT], F32R)
        xT = sb("xT", [P, KC, TOK])
        hhi = sb("hhi", [P, KC, TOK], F32R)
        hlo = sb("hlo", [P, KC, TOK], F32R)
        region = place["at"]
        mix = sb("mix", [P, NBLK, MIX_W])
        headsT = sb("headsT", [HD, 8, TOK])
        acchi = at("acchi", [P, KC, TOK], F32R, region)
        acclo = at("acclo", [P, KC, TOK], F32R, region + 4 * KC * TOK)
        hidhi = at("hidhi", [P, 12 * TOK], F32R, region)
        hidlo = at("hidlo", [P, 12 * TOK], F32R, region + 4 * 12 * TOK)
        modring = at("modring", [P, MOD_RING, KC, UC], F32, region)
        gates = at("gates", [P, NBR, 2, TOK], F32, region + 4 * NBLK * MIX_W)
        region2 = place["at"]
        brhi = sb("brhi", [P, KC, TOK], F32R)
        brlo = sb("brlo", [P, KC, TOK], F32R)
        xrows = at("xrows", [P, NBLK, D], F32, region2)
        hf = at("hf", [P, KC, TOK], F32, region2)
        sqr = at("sqr", [P, 2, TOK], F32, region2 + 4 * 5120)
        scrA = at("scrA", [P, 1536], F32, region2)
        scrB = at("scrB", [P, 1536], F32, region2 + 4 * 1536)
        expS = at("expS", [P, 2, TOK], F32, region2 + 4 * 3072)
        expT = at("expT", [P, 2, TOK], F32, region2 + 4 * 4096)
        kdec = at("kdec", [P, 2, NBLK, NH * HD], F32, region2 + 4 * 5120)
        wsrow = at("wsrow", [P, NH, P], F32, region2 + 4 * 7168)
        wsT = at("wsT", [P, NH, P], F32, region2 + 4 * 7680)
        half_at = [region2 + 4 * x for x in (5120, 6144, 7168, 2048)]
        half_raw = [at(f"half_raw{s}", [P, KC // 2, UC], F32, half_at[s]) for s in range(HALF_RING)]
        half_lo = [at(f"half_lo{s}", [P, KC // 2, UC], F32R, half_at[s]) for s in range(HALF_RING)]
        half_hi = at("half_hi", [P, 2, KC // 2, UC], F32R, region2)
        xT_parts = at("xT_parts", [P, KC, TOK], F32R, base + 24 * UNIT)
        modfull = at("modfull", [P, 2, KC, UC], F32, region2)
        modrows = [at("modrow_start", [2, 2, MG], F32, base + 24 * UNIT + 4 * KC * TOK),
                   at("modrow_attn", [4, 2, MG], F32, place["at"]),
                   at("modrow_ffn", [2, 2, MG], F32, region2 + 4 * 4096)]
        stateF = at("stateF", [HD, 3, NH * HD], F32, region2 + 4 * 7168)
        moe = at("moe", [P, KC, SEQ], F32, region2)
        eraw = at("eraw", [P, 3, UNIT], F32, base)
        ehi = at("ehi", [P, 3, UNIT], F32R, base + 12 * UNIT)
        elo = at("elo", [P, 3, UNIT], F32R, region)
        ghi = at("ghi", [P, KC, P], F32R, region + 12 * UNIT)
        glo = at("glo", [P, KC, P], F32R, region + 12 * UNIT + 4 * D)
        tokhi = at("tokhi", [P, LBLK, D], F32R, region + 12 * UNIT + 8 * D)
        toklo = at("toklo", [P, LBLK, D], F32R, region + 12 * UNIT + 8 * D + 4 * LBLK * D)
        hregion = base + 24 * UNIT + 4 * KC * TOK
        eupT_hi = at("eupT_hi", [P, EXP_CHUNKS, P], F32R, hregion)
        eupT_lo = at("eupT_lo", [P, EXP_CHUNKS, P], F32R, hregion + 4 * DFE)
        yhi = at("yhi", [P, D], F32R, hregion + 8 * DFE)
        ylo = at("ylo", [P, D], F32R, hregion + 8 * DFE + 4 * D)
        eup = at("eup", [P, 2, UC], F32, hregion + 8 * DFE + 8 * D)
        gat = at("gat", [P, LBLK, P], F32R, hregion + 8 * DFE + 8 * D + 8 * UC)
        sca = at("sca", [P, SEQ], F32R, hregion + 8 * DFE + 8 * D + 8 * UC + 4 * SEQ)
        combB = at("combB", [P, NEXP, SEQ], F32, region2 + 4 * 2048)
        rel = at("rel", [P, 4, P], F32, region2 + 4 * 4096)
        pick = at("pick", [NEXP, NEXP, P], F32, region2 + 4 * 4096)
        rout = at("rout", [P, 12, LBLK, NEXP], F32, region2 + 4 * 5120)
        posB = at("posB", [P, NEXP, SEQ], F32, region2 + 4 * 2048)
        before = at("before", [P, 2, P], F32, region2 + 4 * 6464)
        slots = at("slots", [P, P], F32, region2 + 4 * 6720)
        slot_of = at("slot_of", [P, 4], F32, region2 + 4 * 6848)
        cw = at("cw", [P, NEXP], F32, region2 + 4 * 6856)
        most = at("most", [P, 1], F32, region2 + 4 * 6864)
        most_i = at("most_i", [P, 1], mybir.dt.int32, region2 + 4 * 6872)
        combT = at("combT", [NEXP, SEQ], F32, region2 + 4 * 5632)
        rw = at("rw", [P, KC, NEXP], F32, region2 + 4 * 6144)
        rb = at("rb", [P, NEXP], F32, region2 + 4 * 6400)
        eidx = at("eidx", [P, NEXP], F32, region2 + 4 * 6432)
        tmp = sb("tmp", [P, 2, TOK])
        stateB = at("stateB", [HD, 3, NH * HD], F32, place["at"] - 4 * 2 * TOK)
        decay = sb("decay", [P, DEPTH, NH, P])
        ident = sb("ident", [P, P])
        ones = sb("ones", [P, P])
        rows1 = at("rows1", [P, P], F32, region2 + 4 * 6656)
        rows2 = at("rows2", [24, P], F32, region2 + 4 * 6784)
        idx = at("idx", [P, 4], F32, region2 + 4 * 6912)
        lgx = at("lgx", [P, 3, 16], F32, region2 + 4 * 6944)
        vecT = sb("vecT", [P, P])
        rowsT = sb("rowsT", [P, 24])
        siluc = sb("siluc", [P, KC, 2])
        siluc4 = sb("siluc4", [P, KC, 4], F32R)
        fold = sb("fold", [4, 2])
        mod = sb("mod", [P, DEPTH, 6, KC, 2])
        gsc = sb("gsc", [P, DEPTH, 2, KC, 2])
        wmask = sb("wmask", [P, 2, P])
        axial = sb("axial", [P, 2, LBLK, 32])
        rot = sb("rot", [P, 2, NBLK, 32])
        qkw = sb("qkw", [P, DEPTH, 4, HD])
        gv = sb("gv", [P, DEPTH, NH * HD])
        gn = sb("gn", [P, DEPTH, NH * HD])
        sink = sb("sink", [P, DEPTH * NH])
        nsink = sb("nsink", [P, DEPTH * NH])
        expcol = sb("expcol", [P, 4, DEPTH, 2, NH])
        stat = sb("stat", [P, 3, 24])
        negmax = sb("negmax", [P, 16])
        rowsum = sb("rowsum", [P, 16])
        sinkexp = sb("sinkexp", [P, 16])

        def high_place(l, x):
            place = x % high_ring(l)
            c = (place - 2) * (KC // 2)
            return half_hi[:, place] if place < 2 else xT_parts[:, c:c + KC // 2, SEQ:TOK]

        psA = ctx.enter_context(nc.psum_tensor("psA", [P, 4, 512], F32))
        psB = ctx.enter_context(nc.psum_tensor("psB", [P, 4, 512], F32))

        rows_landed = sem("rows_landed")
        x_landed = sem("x_landed")
        lg_landed = sem("lg_landed")
        inputs_landed = sem("inputs_landed")
        late_landed = sem("late_landed")
        router_landed = sem("router_landed")
        mod_landed = [sem(f"mod_landed{s}") for s in range(MOD_RING)]
        mod_used = sem("mod_used")
        modh_landed = [sem(f"modh_landed{s}") for s in range(HALF_RING)]
        modh_hi = sem("modh_hi")
        modh_lo = sem("modh_lo")
        modh_used = sem("modh_used")
        modf_landed = [sem(f"modf_landed{s}") for s in range(2)]
        modf_used = sem("modf_used")
        mod_copied = sem("mod_copied")
        mod_turned = sem("mod_turned")
        mod_added = sem("mod_added")
        ones_set = sem("ones_set")
        setup_turned = sem("setup_turned")
        setup_copied = sem("setup_copied")
        silu_ready = sem("silu_ready")
        lg_steps = sem("lg_steps")
        lg_ready = sem("lg_ready")
        decay_exp = sem("decay_exp")
        decay_used = sem("decay_used")
        x_turned = sem("x_turned")
        x_placed = sem("x_placed")
        raw_landed = [[sem(f"raw_landed{s}{h}") for h in range(2)] for s in range(2)]
        hi_ready = sem("hi_ready")
        lo_ready = sem("lo_ready")
        w_used = sem("w_used")
        dve_step = sem("dve_step")
        act_step = sem("act_step")
        out_stored = sem("out_stored")
        out_placed = sem("out_placed")
        out_turned = sem("out_turned")
        squares = sem("squares")
        meansq = sem("meansq")
        spread_ready = sem("spread_ready")
        rinv_spread = sem("rinv_spread")
        ms_ready = sem("ms_ready")
        root_ready = sem("root_ready")
        xn_ready = sem("xn_ready")
        h_ready = sem("h_ready")
        h_split = sem("h_split")
        L = range(DEPTH)
        mix_taken = [sem(f"mix_taken{l}") for l in L]
        ws_turned = sem("ws_turned")
        ws_copied = sem("ws_copied")
        v_normed = sem("v_normed")
        mlp_mixed = sem("mlp_mixed")
        mlp_done = sem("mlp_done")
        heads_ready = sem("heads_ready")
        head_turned = sem("head_turned")
        head_placed = sem("head_placed")
        scores_ready = sem("scores_ready")
        max_ready = sem("max_ready")
        exp_ready = sem("exp_ready")
        probs_turned = sem("probs_turned")
        probs_placed = sem("probs_placed")
        values_ready = sem("values_ready")
        attn_done = sem("attn_done")
        kdec_ready = sem("kdec_ready")
        kv_ready = sem("kv_ready")
        states_ready = sem("states_ready")
        qk_ready = [sem(f"qk_ready{l}") for l in L]
        qk_decayed = [sem(f"qk_decayed{l}") for l in L]
        ret_ready = [sem(f"ret_ready{l}") for l in L]
        ret_taken = [sem(f"ret_taken{l}") for l in L]
        branches_ready = sem("branches_ready")
        br_turned = [sem(f"br_turned{l}") for l in L]
        br_hi = [sem(f"br_hi{l}") for l in L]
        br_lo = [sem(f"br_lo{l}") for l in L]
        gates_taken = [sem(f"gates_taken{l}") for l in L]
        gates_used = [sem(f"gates_used{l}") for l in L]
        proj_ready = [sem(f"proj_ready{l}") for l in L]
        proj_taken = [sem(f"proj_taken{l}") for l in L]
        acc_ready = [sem(f"acc_ready{l}") for l in L]
        out_taken = [sem(f"out_taken{l}") for l in L]
        up_silu = [sem(f"up_silu{k}") for k in range(3)]
        up_taken = [sem(f"up_taken{k}") for k in range(3)]
        down_ready = [sem(f"down_ready{k}") for k in range(3)]
        down_taken = [sem(f"down_taken{k}") for k in range(3)]
        router_ready = sem("router_ready")
        combine_turned = sem("combine_turned")
        combine_copied = sem("combine_copied")
        comb_spread = sem("comb_spread")
        gap_ready = sem("gap_ready")
        gap_exp = sem("gap_exp")
        mask_ready = sem("mask_ready")
        counted = sem("counted")
        most_ready = sem("most_ready")
        eraw_landed = [[sem(f"eraw_landed{s}{h}") for h in range(2)] for s in range(RING)]
        ehi_ready = sem("ehi_ready")
        elo_ready = sem("elo_ready")
        ew_used = sem("ew_used")
        tok_turned = sem("tok_turned")
        tok_hi = sem("tok_hi")
        tok_lo = sem("tok_lo")
        pos_turned = sem("pos_turned")
        pos_copied = sem("pos_copied")
        pos_spread = sem("pos_spread")
        pos_placed = sem("pos_placed")
        gat_ready = sem("gat_ready")
        gathered = sem("gathered")
        gathered_placed = sem("gathered_placed")
        cw_ready = sem("cw_ready")
        cw_placed = sem("cw_placed")
        eup_silu = sem("eup_silu")
        eup_ready = sem("eup_ready")
        eup_turned = sem("eup_turned")
        eupT_hi_ready = sem("eupT_hi_ready")
        eupT_lo_ready = sem("eupT_lo_ready")
        sca_ready = sem("sca_ready")
        scattered = sem("scattered")
        scattered_added = sem("scattered_added")
        y_hi_ready = sem("y_hi_ready")
        y_lo_ready = sem("y_lo_ready")
        moe_zeroed = sem("moe_zeroed")
        x_final = sem("x_final")

        first_mix = [0, UNITS0]
        first_group = [u + MIX_UNITS for u in first_mix]
        first_out = [u + GROUPS * GROUP_UNITS for u in first_group]
        first_ffn = [u + OUT_UNITS for u in first_out]
        first_part = [first_ffn[0], first_ffn[0] + FFN_PARTS[0] + KC]
        first_exp = first_ffn[1]

        ROOTS = 6
        NORM1, ROOT_V, ROOT_W, ROOT_G, ROOT_GN, NORM2 = range(ROOTS)
        setup_loads = []

        block = ctx.enter_context(nc.Block())

        @block.sync
        def _(sp):
            def load(dst, src, landed=inputs_landed):
                setup_loads.append(landed)
                sp.dma_start(dst, src).then_inc(landed, 16)

            load(rows1[0:96, :], t["b_mod"].rearrange("l (c p) -> (l c) p", p=P), rows_landed)
            load(rows1[96:112, :], t["g_norm1"].rearrange("l (c p) -> (l c) p", p=P), rows_landed)
            load(rows1[112:128, :], t["g_norm2"].rearrange("l (c p) -> (l c) p", p=P), rows_landed)
            load(rows2[0:8, :], t["c"].rearrange("b (c p) -> (b c) p", p=P), rows_landed)
            load(rows2[8:16, :], t["c_ctx"].rearrange("(c p) -> c p", p=P), rows_landed)
            load(rows2[16:24, :], t["mlp_b_s"].rearrange("l g p -> (l g) p"), rows_landed)
            load(ident[:], t["k_ident"], rows_landed)
            w = t["w_mod"][0].rearrange("(c p) n -> p c n", p=P)
            for u in range(MOD_RING):
                sp.dma_start(modring[:, u], w[:, :, u * UC:(u + 1) * UC]).then_inc(mod_landed[u], 16)
            load(xrows[:, 0:LBLK, :], t["x"].rearrange("b (n p) d -> p (b n) d", p=P), x_landed)
            load(xrows[:, LBLK:NBLK, :], t["ctx"].rearrange("b (n p) d -> p (b n) d", p=P), x_landed)
            load(idx[:], t["k_idx"], lg_landed)
            load(lgx[:, 0, :], t["ret_decay"].rearrange("l d h -> (l d h)").unsqueeze(0).broadcast_to([P, 16]), lg_landed)
            load(rel[:], t["k_rel"], lg_landed)
            for u in range(MOD_RING, EARLY_UNITS):
                sp.wait_ge(mod_used, u + 1 - MOD_RING)
                sp.dma_start(modring[:, u % MOD_RING], w[:, :, u * UC:(u + 1) * UC]).then_inc(mod_landed[u % MOD_RING], 16)
            load(wmask[:], t["k_wmask"])
            load(axial[:], t["k_axial"])
            load(rot[:], t["k_rot"])
            for l in range(DEPTH):
                for k, name in enumerate(("win_q_norm", "win_k_norm", "glb_q_norm", "glb_k_norm")):
                    load(qkw[:, l, k, :], t[name][l:l + 1, :].broadcast_to([P, HD]))
                load(gv[:, l, :], t["mlp_g_v"][l:l + 1].rearrange("l g d -> l (g d)").broadcast_to([P, NH * HD]))
                load(gn[:, l, :], t["ret_gn"][l:l + 1].rearrange("l g d -> l (g d)").broadcast_to([P, NH * HD]))
            load(sink[:], t["win_sink"].rearrange("l h -> (l h)").unsqueeze(0).broadcast_to([P, DEPTH * NH]))

            def unit_loads(n, slot, upper, lower, at_zero=False):
                for k, (dst, src) in enumerate((upper, lower)):
                    if n is not None and not (at_zero and k):
                        sp.wait_ge(lo_ready, n * 2 + (2 if at_zero else k + 1) - 4)
                    sp.dma_start(dst, src).then_inc(raw_landed[slot][UPPER_FIRST[k]], 16)

            def square(n, slot, w, col, at_zero=False):
                dst = raw[:, slot].rearrange("p (c n) -> p c n", c=KC)
                src = w.rearrange("(c p) n -> p c n", p=P)
                half = KC // 2
                unit_loads(n, slot, (dst[:, half:KC], src[:, half:KC, ds(col, UC)]), (dst[:, 0:half], src[:, 0:half, ds(col, UC)]),
                           at_zero)

            def up(n, slot, w1, w3, col):
                dst = raw[:, slot].rearrange("p (w c n) -> p w c n", w=2, c=KC)
                unit_loads(n, slot, (dst[:, 1], w3[:, ds(col, P)].rearrange("(c p) n -> p c n", p=P)),
                           (dst[:, 0], w1[:, ds(col, P)].rearrange("(c p) n -> p c n", p=P)), True)

            def down(n, slot, w2, rows, col):
                dst = raw[:, slot, 0:rows * P].rearrange("p (c n) -> p c n", c=rows)
                src = w2.rearrange("(c p) n -> p c n", p=P)
                unit_loads(n, slot, (dst[:, KC:rows], src[:, KC:rows, ds(col, P)]), (dst[:, 0:KC], src[:, 0:KC, ds(col, P)]), True)

            for l in range(DEPTH):
                w = t["w_in"][l]
                if l == 0:
                    square(None, 0, w, 0)
                    square(None, 1, w, UC)
                with sp.Fori(1 if l == 0 else 0, MIX_UNITS // 2) as i:
                    for s in range(2):
                        square(i * 2 + (first_mix[l] + s), s, w, i * (2 * UC) + s * UC, (l, s) == (0, 0))
                with sp.Fori(0, GROUPS // 2) as i:
                    for j in range(2 * GROUP_UNITS):
                        n = i * (2 * GROUP_UNITS) + (first_group[l] + j)
                        g, u = divmod(j, GROUP_UNITS)
                        if u < NBR:
                            square(n, j % 2, w, i * (2 * UC) + (MIX_W + u * D + g * UC))
                        else:
                            square(n, j % 2, t["w_branch"][l].rearrange("b r n -> (b r) n"), i * (2 * UC) + g * UC, (l, g) == (0, 0))
                with sp.Fori(0, OUT_UNITS // 2) as i:
                    for s in range(2):
                        square(i * 2 + (first_out[l] + s), s, t["w_out"][l], i * (2 * UC) + s * UC, (l, s) == (0, 0))
                if l == 0:
                    done = 0
                    for k, chunks in enumerate(FFN_PARTS):
                        w1 = t["ffn_w1"][0][:, done * P:(done + chunks) * P]
                        w3 = t["ffn_w3"][0][:, done * P:(done + chunks) * P]
                        w2 = t["ffn_w2"][0][done * P:(done + chunks) * P, :]
                        done += chunks
                        with sp.Fori(0, chunks // 2) as i:
                            for s in range(2):
                                up(i * 2 + (first_part[k] + s), s, w1, w3, i * (2 * P) + s * P)
                        with sp.Fori(0, KC // 2) as i:
                            for s in range(2):
                                down(i * 2 + (first_part[k] + chunks + s), s, w2, chunks, i * (2 * P) + s * P)
                else:
                    def gathered_unit(e, u, first):
                        name = "moe_w2" if u >= 2 * UPS else ("moe_w1", "moe_w3")[u % 2]
                        w = t[name][0][ds(e, 1)].rearrange("o r n -> (o r) n") if not first else t[name][0][0]
                        src = w.rearrange("(c p) n -> p c n", p=P)
                        for k, half in enumerate(UPPER_FIRST):
                            at_zero = u in (0, 1, 2 * UPS)
                            if (not first or u >= RING) and not (at_zero and k):
                                sp.wait_ge(elo_ready, e * (2 * GU) + (2 * (u - RING) + (2 if at_zero else k + 1)))
                            if u < 2 * UPS:
                                dst = eraw[:, u % RING].rearrange("p (c n) -> p c n", c=KC)
                                col, c = (u // 2) * UC, half * (KC // 2)
                                dst, part = dst[:, c:c + KC // 2], src[:, c:c + KC // 2, col:col + UC]
                            else:
                                c = 2 * (u - 2 * UPS) + half
                                dst = eraw[:, u % RING].rearrange("p (c n) -> p c n", c=2)
                                dst, part = dst[:, half:half + 1], src[:, c:c + 1, :]
                            sp.dma_start(dst, part).then_inc(eraw_landed[u % RING][half], 16)

                    sp.wait_ge(w_used, first_exp)
                    for u in range(RING):
                        gathered_unit(0, u, True)
                    sp.wait_ge(most_ready, 1)
                    fullest = sp.value_load(most_i[0:1, 0:1], min_val=0, max_val=SEQ)
                    with sp.If(fullest < P + 1):
                        for u in range(RING, GU):
                            gathered_unit(0, u, True)
                        with sp.Fori(0, NEXP - 1) as e:
                            for u in range(GU):
                                gathered_unit(e + 1, u, False)
                    with sp.Else():
                        for s in range(RING):
                            for half in range(2):
                                sp.wait_ge(eraw_landed[s][half], 16)
                        sp.wait_ge(ehi_ready, 2 * RING)
                        with sp.Fori(0, NEXP) as e:
                            w1, w3, w2 = (t[name][0][ds(e, 1)].rearrange("o r n -> (o r) n")
                                          for name in ("moe_w1", "moe_w3", "moe_w2"))
                            with sp.Fori(0, EXP_CHUNKS // 2) as i:
                                for s in range(2):
                                    up(e * EXP_UNITS + i * 2 + (first_exp + s), s, w1, w3, i * (2 * P) + s * P)
                            with sp.Fori(0, KC // 2) as i:
                                for s in range(2):
                                    down(e * EXP_UNITS + i * 2 + (first_exp + EXP_CHUNKS + s), s, w2, EXP_CHUNKS, i * (2 * P) + s * P)

            for half in range(2):
                sp.wait_ge(out_placed, (half + 1) * KC // 2)
                cols = slice(half * D // 2, (half + 1) * D // 2)
                sp.dma_start(t["out"].rearrange("b (n p) d -> p (b n) d", p=P)[:, :, cols], xrows[:, 0:LBLK, cols]).then_inc(out_stored, 16)
            sp.wait_ge(out_stored, 32)

        def loaded(landed):
            return 16 * setup_loads.count(landed)

        class Steps:

            def __init__(self, eng, semaphore):
                self.eng, self.semaphore, self.base, self.n = eng, semaphore, None, 0

            def __call__(self, ins):
                self.n += 1
                ins.then_inc(self.semaphore, 1)
                self.eng.wait_ge(self.semaphore, self.n if self.base is None else self.base + self.n)

            def loop(self, done, per):
                self.base, self.start = done * per, self.n

            def end(self, turns, per):
                assert self.n - self.start == per, (self.n - self.start, per)
                self.base, self.n = None, self.start + turns * per

        @block.tensor
        def _(pe):
            def mm(out, lhsT, rhs, start=True, stop=True):
                return nc.tensor.matmul(out, lhsT, rhs, start=start, stop=stop)

            def mm3(out, a, b, start, stop):
                mm(out, a[0], b[0], start, False)
                mm(out, a[0], b[1], False, False)
                return mm(out, a[1], b[0], False, stop)

            def w(slot, col, n):
                return whi[:, slot, col:col + n], wlo[:, slot, col:col + n]

            def h(k, a, b):
                return hhi[:, k, a:b], hlo[:, k, a:b]

            pe.wait_ge(rows_landed, loaded(rows_landed))
            pe.wait_ge(ones_set, 1)
            nc.tensor.transpose(psB[:, 0, 0:P], rows1[:], ident[:])
            nc.tensor.transpose(psB[:, 0, P:P + 24], rows2[:], ident[0:24, 0:24]).then_inc(setup_turned, 1)
            pe.wait_ge(silu_ready, 1)

            def mod_multiply(out, slot):
                for k in range(KC):
                    last = mm(out, siluc[:, k, :], slot[:, k, :], k == 0, k == KC - 1)
                return last

            def turn_rows(n, where, bank):
                pe.wait_ge(mod_copied, n + 1)
                if not (isinstance(n, int) and n == 0):
                    pe.wait_ge(mod_added, n + 0)
                for q in range(MG // P):
                    last = mm(bank[:, 2 * q:2 * q + 2],
                              modrows[where][:, n % 2 if isinstance(n, int) else 0, q * P:(q + 1) * P],
                              fold[:] if where == 1 else ident[0:2, 0:2], True, True)
                last.then_inc(mod_turned, 1)

            def mean_square(k, c, slot, T, first, final):
                pe.wait_ge(squares, k * KC + (c + 1))
                for b in range(T // P):
                    last = mm(psB[:, 0, b:b + 1], sqr[:, slot, b * P:(b + 1) * P], ones[:, 0:1],
                              first and b == 0, final and b == T // P - 1)
                last.then_inc(meansq, 1)

            def mod_group(g):
                if g >= 2:
                    pe.wait_ge(mod_copied, g - 1)
                for x in range(2):
                    u = 2 * g + x
                    pe.wait_ge(mod_landed[u % MOD_RING], 16 * (u // MOD_RING + 1))
                    mod_multiply(psB[0:2, 2 + g % 2, x * UC:(x + 1) * UC], modring[:, u % MOD_RING]).then_inc(mod_used, 1)
                if g:
                    turn_rows(g - 1, 0, psB[:, 1])

            mod_group(0)
            mod_group(1)
            pe.wait_ge(x_landed, loaded(x_landed))
            for c in range(KC):
                if c >= 4:
                    pe.wait_ge(x_placed, c - 3)
                for b in range(NBLK):
                    last = nc.tensor.transpose(psA[:, c % 4, b * P:(b + 1) * P], xrows[:, b, c * P:(c + 1) * P], ident[:])
                last.then_inc(x_turned, 1)
            mod_group(2)
            for c in range(KC):
                mean_square(0, c, c % 2, TOK, c == 0, c == KC - 1)
            mod_group(3)
            turn_rows(EARLY_GROUPS - 1, 0, psB[:, 1])

            def norm(k, T):
                pe.wait_ge(spread_ready, k + 1)
                for b in range(T // P):
                    last = mm(psB[:, 1, b * P:(b + 1) * P], ones[:], tmp[:, 1, b * P:(b + 1) * P])
                last.then_inc(rinv_spread, 1)

            def h_arrived(k, c):
                pe.wait_ge(h_split, k * KC + c + 1)

            def arrived(n):
                pe.wait_ge(lo_ready, n * 2 + 2)

            def two_chunks(slot, pair, b, T):
                for j in range(2):
                    for k in range(KC):
                        last = mm3(psA[:, 2 * pair + j, 0:T], w(slot, k * UC + j * P, P), b(k), k == 0, k == KC - 1)
                return last

            def turn_heads(l, m, heads, col):
                pe.wait_ge(heads_ready, 3 * l + m + 1)
                for j in range(heads):
                    if j >= 4:
                        pe.wait_ge(head_placed, heads_before(l, m) + j - 3)
                    for b in range(head_blocks(l, j)):
                        last = nc.tensor.transpose(psA[0:HD, j % 4, b * P:(b + 1) * P],
                                                   mix[:, b, col + j * HD:col + (j + 1) * HD], ident[:])
                    last.then_inc(head_turned, 1)
                pe.wait_ge(head_placed, heads_before(l, m) + heads)

            def mod_half(l, x):
                n = l * MOD_GROUPS + EARLY_GROUPS + x // 4
                pe.wait_ge(modh_lo, l * HALVES + x + 1)
                if x % 4 == 0 and x:
                    pe.wait_ge(mod_copied, n)
                col, first = divmod(x % 4, 2)
                for k in range(KC // 2):
                    w4 = siluc4[:, first * (KC // 2) + k, :]
                    out = psA[0:4, 2, col * UC:(col + 1) * UC]
                    mm(out, w4, high_place(l, x)[:, k, :], first == 0 and k == 0, False)
                    last = mm(out, w4, half_lo[x % HALF_RING][:, k, :], False, first == 1 and k == KC // 2 - 1)
                last.then_inc(modh_used, 1)
                if x % 4 == 1 and x % (HALVES // 2) != 1:
                    turn_rows(n - 1, 1, psA[:, 3])

            def attention(l, m, vcol):
                items = attention_items(l)
                n = len(items)
                per = HALVES // (2 * n)

                def scores(i):
                    hd, b, k0, nk = items[i]
                    if i >= 2:
                        pe.wait_ge(exp_ready, items_before(l, m) + i - 1)
                    mm(psB[:, i % 2, 0:nk], headsT[:, hd, b * P:(b + 1) * P],
                       headsT[:, NH + hd // 2, k0:k0 + nk]).then_inc(scores_ready, 1)

                scores(0)
                for step in range(n + 2):
                    if 1 <= step <= n:
                        i = step - 1
                        hd, b, k0, nk = items[i]
                        pe.wait_ge(exp_ready, items_before(l, m) + i + 1)
                        if i >= 2:
                            pe.wait_ge(probs_placed, items_before(l, m) + i - 1)
                        for y in range(nk // P):
                            last = nc.tensor.transpose(psA[:, i % 2, y * P:(y + 1) * P],
                                                       expS[:, i % 2, y * P:(y + 1) * P], ident[:])
                        last.then_inc(probs_turned, 1)
                    if step >= 2:
                        i = step - 2
                        hd, b, k0, nk = items[i]
                        pe.wait_ge(probs_placed, items_before(l, m) + i + 1)
                        if i >= 2:
                            pe.wait_ge(attn_done, items_before(l, m) + i - 1)
                        v = vcol + (hd // 2) * HD
                        for y in range(nk // P):
                            last = mm(psB[:, 2 + i % 2, 0:HD], expT[:, i % 2, y * P:(y + 1) * P],
                                      mix[:, k0 // P + y, v:v + HD], y == 0, y == nk // P - 1)
                        last.then_inc(values_ready, 1)
                    if step + 1 < n:
                        scores(step + 1)
                    if step < n:
                        for x in range(per):
                            mod_half(l, m * HALVES // 2 + step * per + x)
                last_group = l * MOD_GROUPS + EARLY_GROUPS + (m + 1) * HALVES // 8 - 1
                turn_rows(last_group, 1, psA[:, 3])
                pe.wait_ge(mod_added, last_group + 1)
                pe.wait_ge(attn_done, items_before(l, m) + n)

            def retention(l):
                pe.wait_ge(kdec_ready, l + 1)
                for d, order in enumerate(((2, 3, 0), (3, 2, 1))):
                    for step, b in enumerate(order):
                        for hd in range(NH):
                            last = mm(psB[0:HD, 2 * d + step // 2, (step % 2) * 256 + hd * HD:(step % 2) * 256 + (hd + 1) * HD],
                                      kdec[:, d, b, hd * HD:(hd + 1) * HD], mix[:, b, COL_RV + hd * HD:COL_RV + (hd + 1) * HD])
                last.then_inc(kv_ready, 1)

                def qk(b):
                    if b >= 2:
                        pe.wait_ge(qk_decayed[l], b - 1)
                    for hd in range(NH):
                        last = mm(psA[:, b % 2, hd * P:(hd + 1) * P], headsT[:, NH + hd, b * P:(b + 1) * P],
                                  headsT[:, hd, b * P:(b + 1) * P])
                    last.then_inc(qk_ready[l], 1)

                before = ((1, 2), (2, 1), (None, 0), (0, None))
                qk(0)
                pe.wait_ge(states_ready, l + 1)
                for b in range(blocks_of(l)):
                    if b + 1 < blocks_of(l):
                        qk(b + 1)
                    pe.wait_ge(qk_decayed[l], b + 1)
                    if b >= 2:
                        pe.wait_ge(ret_taken[l], b - 1)
                    for hd in range(NH):
                        last = mm(psA[:, 2 + b % 2, hd * HD:(hd + 1) * HD], expS[:, b % 2, hd * P:(hd + 1) * P],
                                  mix[:, b, COL_RV + hd * HD:COL_RV + (hd + 1) * HD])
                    for d, state in enumerate((stateF, stateB)):
                        if before[b][d] is not None:
                            for hd in range(NH):
                                last = mm(psB[:, b % 2, d * 256 + hd * HD:d * 256 + (hd + 1) * HD],
                                          headsT[:, hd, b * P:(b + 1) * P], state[:, before[b][d], hd * HD:(hd + 1) * HD])
                    last.then_inc(ret_ready[l], 1)

            def feed_forward(k, chunks, T, at_unit, up_done, down_done, beside=False):
                def up_pair(i, first):
                    for s in range(2):
                        if s == 0:
                            pe.wait_ge(down_taken[k], down_done + 2)
                        arrived(i * 2 + (at_unit + s))
                        pe.wait_ge(up_taken[k], i * 2 + (up_done + s + 1))
                        if k == 1 and s == 1:
                            pe.wait_ge(down_taken[0], KC + 2)
                        by_chunk = first and s == 0
                        for j, c in [(j, c) for c in range(KC) for j in range(2)] if by_chunk else \
                                    [(j, c) for j in range(2) for c in range(KC)]:
                            if by_chunk and j == 0:
                                h_arrived(1, c)
                            last = mm3(psA[:, 2 * s + j, 0:T], w(s, (j * KC + c) * P, P), h(c, 0, T), c == 0, c == KC - 1)
                        last.then_inc(w_used, 1)

                if k == 0:
                    up_pair(0, True)
                with pe.Fori(1 if k == 0 else 0, chunks // 2) as i:
                    up_pair(i, False)

                def down_pair(i, first):
                    for s in range(2):
                        if s == 0:
                            pe.wait_ge(up_taken[k], up_done + (chunks + 1))
                        arrived(i * 2 + (at_unit + (chunks + s)))
                        pe.wait_ge(down_taken[k], i * 2 + (down_done + s + 1))
                        for c in range(chunks):
                            if s == 0 and c == chunks - 1:
                                pe.wait_ge(up_taken[k], up_done + (chunks + 2))
                            last = mm3(psA[:, 2 * s, 0:T], w(s, c * P, P),
                                       (hidhi[:, c * T:(c + 1) * T], hidlo[:, c * T:(c + 1) * T]), c == 0, c == chunks - 1)
                        last.then_inc(w_used, 1)
                        if k == 1 and not (first and s == 0):
                            mean_square(2, i * 2 + (s - 1), 1 - s, TOK, first, False)
                        if beside and s == 0:
                            for x in range(2):
                                pe.wait_ge(modf_landed[x], i * 16 + 16)
                                mod_multiply(psB[0:2, 2, x * UC:(x + 1) * UC], modfull[:, x]).then_inc(modf_used, 1)
                        elif beside:
                            turn_rows(i + MOD_GROUPS, 2, psB[:, 1])

                if k == 1:
                    down_pair(0, True)
                with pe.Fori(1 if k == 1 else 0, KC // 2) as i:
                    down_pair(i, False)

            for l in range(DEPTH):
                T = blocks_of(l) * P
                if l:
                    mean_square(2 * l, KC - 1, 1, TOK, False, True)
                norm(2 * l, TOK)
                for u in range(MIX_UNITS):
                    s, blocks = u % 2, mix_blocks(l, u)
                    arrived(first_mix[l] + u)
                    pe.wait_ge(mix_taken[l], u + 1)
                    order = [(b, k) for k in range(KC) for b in range(blocks)] if u == 0 else \
                            [(b, k) for b in range(blocks) for k in range(KC)]
                    for b, k in order:
                        if (u, b) == (0, 0):
                            h_arrived(2 * l, k)
                        last = mm3(psA[:, 2 * s + b // 2, (b % 2) * UC:(b % 2 + 1) * UC], h(k, b * P, (b + 1) * P), w(s, k * UC, UC),
                                   k == 0 and (u != 0 or b % 2 == 0), k == KC - 1 and (u != 0 or b % 2 == 1))
                    last.then_inc(w_used, 1)
                    if u == AFTER_V:
                        pe.wait_ge(late_landed, 16 * (l + 1))
                        for g in range(NH):
                            last = nc.tensor.transpose(psB[:, 0, g * P:(g + 1) * P], wsrow[:, g, :], ident[:])
                        last.then_inc(ws_turned, 1)
                    if u == AFTER_W:
                        pe.wait_ge(ws_copied, l + 1)
                        pe.wait_ge(v_normed, l + 1)
                        for g in range(NH):
                            last = mm(psB[:, 1 + g // 2, (g % 2) * 256:(g % 2) * 256 + T // P * HD], wsT[:, g, :],
                                      mix[:, 0:T // P, COL_V + g * HD:COL_V + (g + 1) * HD])
                        last.then_inc(mlp_mixed, 1)
                pe.wait_ge(mix_taken[l], MIX_UNITS + 2)
                turn_heads(l, 0, 6, COL_WQ)
                pe.wait_ge(mlp_done, l + 1)
                attention(l, 0, COL_WV)
                turn_heads(l, 1, 6, COL_GQ)
                attention(l, 1, COL_GV)
                turn_heads(l, 2, 8, COL_RQ)
                retention(l)
                def turn_branches():
                    pe.wait_ge(branches_ready, l + 1)
                    pe.wait_ge(gates_taken[l], GATES_FIRST + 2)
                    for c in range(KC):
                        if c >= 4:
                            pe.wait_ge(br_lo[l], c - 3)
                        col = OUT_COLS[c // 2] + (c % 2) * P
                        for b in range(T // P):
                            last = nc.tensor.transpose(psA[:, c % 4, b * P:(b + 1) * P], mix[:, b, col:col + P], ident[:])
                        last.then_inc(br_turned[l], 1)
                    pe.wait_ge(br_lo[l], KC)

                def two_groups(i, first):
                    for j in range(2 * GROUP_UNITS):
                        g, u = divmod(j, GROUP_UNITS)
                        if first and j == GATES_FIRST:
                            turn_branches()
                        arrived(i * (2 * GROUP_UNITS) + (first_group[l] + j))
                        if u < NBR:
                            pe.wait_ge(gates_taken[l], i * (2 * NBR) + (g * NBR + u + 1))
                            last = two_chunks(j % 2, u % 2, lambda k: h(k, 0, T), T)
                        else:
                            for c in range(2):
                                for br in range(NBR):
                                    pe.wait_ge(proj_taken[l], i * (4 * NBR) + ((2 * g + c) * NBR + br + 1))
                                    for k in (2 * br, 2 * br + 1):
                                        last = mm3(psB[:, br, 0:T], w(j % 2, k * UC + c * P, P),
                                                   (brhi[:, k, 0:T], brlo[:, k, 0:T]), k == 2 * br, k == 2 * br + 1)
                                    if (c, br) != (1, NBR - 1):
                                        last.then_inc(proj_ready[l], 1)
                        last.then_inc(w_used, 1)

                pe.wait_ge(ret_taken[l], blocks_of(l))
                two_groups(0, True)
                with pe.Fori(1, GROUPS // 2) as i:
                    two_groups(i, False)
                pe.wait_ge(gates_taken[l], GROUPS * NBR + 2)
                for u in range(OUT_UNITS):
                    arrived(first_out[l] + u)
                    pe.wait_ge(out_taken[l], u + 1)
                    for j, k in [(j, k) for k in range(KC) for j in range(2)] if u == 0 else \
                                [(j, k) for j in range(2) for k in range(KC)]:
                        if (u, j) == (0, 0):
                            pe.wait_ge(acc_ready[l], k + 1)
                        last = mm3(psA[:, 2 * (u % 2) + j, 0:T], w(u % 2, k * UC + j * P, P), (acchi[:, k, 0:T], acclo[:, k, 0:T]),
                                   k == 0, k == KC - 1)
                    last.then_inc(w_used, 1)
                    for c in range(max(2 * u - 2, 0), 2 * u if u < OUT_UNITS - 1 else KC):
                        mean_square(2 * l + 1, c, c % 2, T, c == 0, c == KC - 1)
                norm(2 * l + 1, T)
                if l == 0:
                    for k, chunks in enumerate(FFN_PARTS):
                        if k:
                            pe.wait_ge(down_taken[k - 1], KC + 1)
                        feed_forward(k, chunks, T, first_part[k], 0, 0, k == 0)
                else:
                    pe.wait_ge(router_landed, 16 * 7)
                    for k in range(KC):
                        h_arrived(3, k)
                        for b in range(LBLK):
                            last = mm(psB[:, 0, b * NEXP:(b + 1) * NEXP], hf[:, k, b * P:(b + 1) * P], rw[:, k, :],
                                      k == 0 and b == 0, k == KC - 1 and b == LBLK - 1)
                    last.then_inc(router_ready, 1)
                    pe.wait_ge(out_taken[l], OUT_UNITS + 2)
                    for b in range(LBLK):
                        for c in range(KC):
                            last = nc.tensor.transpose(psA[:, 2 * b + c // 4, (c % 4) * P:(c % 4 + 1) * P],
                                                       hf[:, c, b * P:(b + 1) * P], ident[:])
                            if c % 4 == 3:
                                last.then_inc(tok_turned, 1)
                    pe.wait_ge(mask_ready, 1)
                    for b in range(LBLK):
                        for y in range(b + 1):
                            mm(psB[:, 1, 16 + b * NEXP:16 + (b + 1) * NEXP], before[:, 0 if y == b else 1, :],
                               rout[:, 8, y, :], y == 0, y == b)
                    for b in range(LBLK):
                        last = mm(psB[:, 1, 32:32 + NEXP], before[:, 1, :], rout[:, 8, b, :], b == 0, b == LBLK - 1)
                    last.then_inc(counted, 1)
                    pe.wait_ge(tok_lo, 2 * LBLK)
                    pe.wait_ge(most_ready, 1)
                    fullest = pe.value_load(most_i[0:1, 0:1], min_val=0, max_val=SEQ)

                    def turn_routing(rows, turned):
                        for b in range(LBLK):
                            last = nc.tensor.transpose(psB[0:NEXP, 2, b * P:(b + 1) * P], rout[:, rows, b, :], ident[:])
                        last.then_inc(turned, 1)

                    def spread_routing(experts, banks, done):
                        for k, e in enumerate(experts):
                            last = mm(banks[:, k // 2, (k % 2) * SEQ:(k % 2 + 1) * SEQ], pick[:, e, :], combT[:])
                        last.then_inc(done, 1)

                    def gather(half, n):
                        if half == 0:
                            pe.wait_ge(gat_ready, n + 1)
                        if half == 1:
                            pe.wait_ge(gathered_placed, n * 2 + 1)
                        part = (tokhi, toklo)[half]
                        for c in range(KC):
                            for b in range(LBLK):
                                last = mm(psB[:, c // 4, (c % 4) * P:(c % 4 + 1) * P], part[:, b, c * P:(c + 1) * P],
                                          gat[:, b, :], b == 0, b == LBLK - 1)
                        last.then_inc(gathered, 1)
                        if half == 1:
                            for b in range(LBLK):
                                w_ = rout[:, 0, b, ds(n, 1)] if not isinstance(n, int) else rout[:, 0, b, n:n + 1]
                                last = mm(psA[:, 3, 0:1], gat[:, b, :].bitcast(F32), w_, b == 0, b == LBLK - 1)
                            last.then_inc(cw_ready, 1)

                    def scatter(half, n):
                        if half == 0:
                            pe.wait_ge(y_lo_ready, n + 1)
                            pe.wait_ge(sca_ready, n + 1)
                        else:
                            pe.wait_ge(scattered_added, n * 2 + 1)
                        for c in range(4 * half, 4 * half + 4):
                            for k, y in enumerate((yhi, ylo)):
                                last = mm(psB[:, (c % 4) // 2, (c % 2) * SEQ:(c % 2 + 1) * SEQ], y[:, c * P:(c + 1) * P], sca[:],
                                          k == 0, k == 1)
                        last.then_inc(scattered, 1)

                    def arrived3(e, u):
                        pe.wait_ge(elo_ready, e * (2 * GU) + (2 * u + 2))

                    def turn_up(e, i):
                        pe.wait_ge(eup_ready, e * UPS + (i + 1))
                        if not (isinstance(e, int) and e == 0 and i == 0):
                            pe.wait_ge(eupT_lo_ready, e * UPS + i)
                        for y in range(2):
                            last = nc.tensor.transpose(psA[:, 2, y * P:(y + 1) * P], eup[:, i % 2, y * P:(y + 1) * P], ident[:])
                        last.then_inc(eup_turned, 1)

                    def gathered_expert(e):
                        first = isinstance(e, int) and e == 0
                        final = isinstance(e, int) and e == NEXP - 1
                        pe.wait_ge(gathered_placed, e * 2 + 2)
                        for u in range(2 * UPS):
                            i, which = divmod(u, 2)
                            arrived3(e, u)
                            if not (first and i == 0):
                                pe.wait_ge(eup_ready if which else eup_silu, e * UPS + i)
                            for k in range(KC):
                                last = mm3(psA[:, which, 0:UC], (ghi[:, k, :], glo[:, k, :]),
                                           (ehi[:, u % RING, k * UC:(k + 1) * UC], elo[:, u % RING, k * UC:(k + 1) * UC]),
                                           k == 0, k == KC - 1)
                            last.then_inc(ew_used, 1)
                            if which and i:
                                turn_up(e, i - 1)
                            if first and u in (3, 7):
                                half = u // 4
                                pe.wait_ge(pos_placed if half else pos_copied, 1)
                                spread_routing(range(4 * half, 4 * half + 4), psB[:, 2:4, :], pos_spread)
                        if not first:
                            scatter(0, e - 1)
                        for j in range(DOWNS):
                            u = 2 * UPS + j
                            s_ = u % RING
                            arrived3(e, u)
                            pe.wait_ge(eupT_lo_ready, e * UPS + (j + 1))
                            if j == 0 and first:
                                pe.wait_ge(pos_placed, 2)
                            if j == 0 and not first:
                                pe.wait_ge(y_lo_ready, e + 0)
                            for y in range(2):
                                for half in range(2):
                                    col = y * D + half * 512
                                    last = mm3(psB[:, 2 + half, :], (eupT_hi[:, 2 * j + y, :], eupT_lo[:, 2 * j + y, :]),
                                               (ehi[:, s_, col:col + 512], elo[:, s_, col:col + 512]),
                                               j == 0 and y == 0, j == DOWNS - 1 and y == 1)
                            last.then_inc(ew_used, 1)
                            if j == 0 and not first:
                                scatter(1, e - 1)
                            if j == 1:
                                turn_up(e, UPS - 1)
                            if j in (1, 2) and not final:
                                if j == 1 and not first:
                                    pe.wait_ge(scattered_added, e * 2)
                                gather(j - 1, e + 1)

                    with pe.If(fullest < P + 1):
                        turn_routing(9, pos_turned)
                        gather(0, 0)
                        gather(1, 0)
                        gathered_expert(0)
                        with pe.Fori(1, NEXP - 1) as e:
                            gathered_expert(e)
                        gathered_expert(NEXP - 1)
                        for half in range(2):
                            scatter(half, NEXP - 1)
                    with pe.Else():
                        turn_routing(0, combine_turned)
                        pe.wait_ge(combine_copied, 1)
                        spread_routing(range(NEXP), psA, comb_spread)
                        pe.wait_ge(comb_spread, 2)
                        with pe.Fori(0, NEXP) as e:
                            feed_forward(2, EXP_CHUNKS, T, e * EXP_UNITS + first_exp, e * EXP_CHUNKS, e * KC)
            for c in range(KC):
                pe.wait_ge(x_final, c + 1)
                if c >= 4:
                    pe.wait_ge(out_placed, c - 3)
                for b in range(LBLK):
                    last = nc.tensor.transpose(psA[:, c % 4, b * P:(b + 1) * P], xT[:, c, b * P:(b + 1) * P], ident[:])
                last.then_inc(out_turned, 1)

        @block.gpsimd
        def _(pool):
            for l in range(DEPTH):
                w = t["w_mod"][l].rearrange("(c p) n -> p c n", p=P)

                def half_load(pair, slot):
                    c = (slot % 2) * (KC // 2)
                    pool.dma_start(half_raw[slot][:], w[:, c:c + KC // 2, ds(pair * UC + 2 * D, UC)]).then_inc(modh_landed[slot], 16)

                pool.wait_ge(h_split, 2 * l * KC + KC)
                pool.dma_start(wsrow[:], t["mlp_w_s"][l].rearrange("g i j -> i g j")).then_inc(late_landed, 16)
                half_load(0, 0)
                half_load(0, 1)
                pool.wait_ge(mlp_mixed, l + 1)
                half_load(1, 2)
                pool.wait_ge(heads_ready, 3 * l + 3)
                half_load(1, 3)
                with pool.Fori(1, HALVES // HALF_RING) as i:
                    for s in range(HALF_RING):
                        pool.wait_ge(modh_used, i * HALF_RING + (l * HALVES + s + 1 - HALF_RING))
                        half_load(i * 2 + s // 2, s)
                if l == 0:
                    w = t["w_mod"][1].rearrange("(c p) n -> p c n", p=P)
                    pool.wait_ge(h_split, 2 * KC)
                    for s in range(2):
                        pool.dma_start(modfull[:, s], w[:, :, s * UC:(s + 1) * UC]).then_inc(modf_landed[s], 16)
                    with pool.Fori(1, EARLY_UNITS // 2) as i:
                        for s in range(2):
                            pool.wait_ge(modf_used, i * 2 + (s - 1))
                            pool.dma_start(modfull[:, s], w[:, :, ds(i * (2 * UC) + s * UC, UC)]).then_inc(modf_landed[s], 16)
                else:
                    pool.wait_ge(tok_turned, 2 * LBLK)
                    nc.gpsimd.memset(moe[:].rearrange("p c n -> p (c n)"), 0.0).then_inc(moe_zeroed, 1)

        @block.scalar
        def _(act):
            step = Steps(act, act_step)

            def f(out, in_, func, **k):
                return nc.scalar.activation(out, in_, func, **k)

            def hi_part(n, slot):
                for h in UPPER_FIRST:
                    act.wait_ge(raw_landed[slot][h], 8 * n + (16 - 8 * slot))
                    part = slice(h * HALF, (h + 1) * HALF)
                    f(whi[:, slot, part], raw[:, slot, part], ACT.Copy).then_inc(hi_ready, 1)

            def next_hi(n, slot):
                act.wait_ge(w_used, n + 1)
                hi_part(n + 2, slot)

            for l in range(DEPTH):
                act.sem_inc(mix_taken[l], 2)
                act.sem_inc(gates_taken[l], 2)

            act.wait_ge(setup_copied, 1)
            f(siluc[:], rowsT[:, 0:16].rearrange("p (w c) -> p c w", w=2), ACT.Silu).then_inc(silu_ready, 1)
            def square(k, c, slot, T, free):
                if not free:
                    act.wait_ge(meansq, k * KC + (c - 1))
                x = xT[:, c, 0:T] if isinstance(c, int) else xT[:, ds(c, 1), 0:T].rearrange("p o n -> p (o n)")
                f(sqr[:, slot, 0:T], x, ACT.Square).then_inc(squares, 1)

            for c in range(KC):
                act.wait_ge(x_placed, c + 1)
                square(0, c, c % 2, TOK, c < 2)
            act.wait_ge(lg_ready, 1)
            step(f(lgx[:, 1, :], lgx[:, 1, :], ACT.Exp, scale=-1.0))
            f(lgx[:, 1, :], lgx[:, 1, :], ACT.Ln, bias=1.0).then_inc(lg_steps, 1)
            act.wait_ge(lg_ready, 2)
            for k in range(4):
                last = f(expcol[:, k].rearrange("p l d h -> p (l d h)"), lgx[:, 2, :], ACT.Exp, scale=idx[:, k:k + 1])
            last.then_inc(lg_steps, 1)
            for l in range(DEPTH):
                for hd in range(NH):
                    n = l * NH + hd
                    if n >= 2:
                        act.wait_ge(decay_used, n - 1)
                    for d in range(2):
                        col = (l * 2 + d) * NH + hd
                        last = f(tmp[:, n % 2, d * P:(d + 1) * P], rel[:, d, :], ACT.Exp, scale=lgx[:, 2, col:col + 1])
                    last.then_inc(decay_exp, 1)
            hi_part(0, 0)
            hi_part(1, 1)

            def root(k, ap):
                act.wait_ge(ms_ready, k + 1)
                f(ap, ap, ACT.Sqrt).then_inc(root_ready, 1)

            def norm(k, T):
                l, second = divmod(k, 2)
                root(l * ROOTS + (NORM2 if second else NORM1), stat[:, 0, 0:T // P])
                sh = SH2 if second else SH1
                for c in range(KC):
                    act.wait_ge(xn_ready, k * KC + c + 1)
                    for w in range(T // SEQ):
                        part, shift = slice(w * SEQ, (w + 1) * SEQ), mod[:, l, sh, c, w:w + 1]
                        if k == 2 * DEPTH - 1:
                            step(f(hf[:, c, part], hf[:, c, part], ACT.Identity, bias=shift))
                            last = f(hhi[:, c, part], hf[:, c, part], ACT.Copy)
                        else:
                            last = f(hhi[:, c, part], hf[:, c, part], ACT.Identity, bias=shift)
                    last.then_inc(h_ready, 1)

            def place_heads(l, m, heads):
                for j in range(heads):
                    act.wait_ge(head_turned, heads_before(l, m) + j + 1)
                    n = head_blocks(l, j) * P
                    f(headsT[:, j, 0:n], psA[0:HD, j % 4, 0:n], ACT.Copy).then_inc(head_placed, 1)

            def half_high(l, x):
                act.wait_ge(modh_landed[x % HALF_RING], 16 * (l * HALVES // HALF_RING + x // HALF_RING + 1))
                used = l * HALVES + max(x + 1 - high_ring(l), 0)
                if used:
                    act.wait_ge(modh_used, used)
                f(high_place(l, x), half_raw[x % HALF_RING][:], ACT.Copy).then_inc(modh_hi, 1)

            def attention(l, m):
                items = attention_items(l)
                n = len(items)
                per = HALVES // (2 * n)
                if m == 0:
                    act.wait_ge(heads_ready, 3 * l + 3)
                    half_high(l, 0)
                    half_high(l, 1)
                for t_ in range(n + 1):
                    if t_ < n:
                        i = t_
                        hd, b, k0, nk = items[i]
                        act.wait_ge(max_ready, items_before(l, m) + i + 1)
                        if i >= 2:
                            act.wait_ge(probs_turned, items_before(l, m) + i - 1)
                        if m == 0:
                            f(sinkexp[:, i:i + 1], negmax[:, i:i + 1], ACT.Exp, bias=sink[:, l * NH + hd:l * NH + hd + 1])
                        f(expS[:, i % 2, 0:nk], psB[:, i % 2, 0:nk], ACT.Exp, scale=SCALE, bias=negmax[:, i:i + 1],
                          accum_out=rowsum[:, i:i + 1]).then_inc(exp_ready, 1)
                    if t_ >= 1:
                        i = t_ - 1
                        hd, b, k0, nk = items[i]
                        act.wait_ge(probs_turned, items_before(l, m) + i + 1)
                        if i >= 2:
                            act.wait_ge(values_ready, items_before(l, m) + i - 1)
                        f(expT[:, i % 2, 0:nk], psA[:, i % 2, 0:nk], ACT.Copy).then_inc(probs_placed, 1)
                    if t_ < n:
                        for x in halves_ahead(m, t_, per):
                            half_high(l, x)

            def feed_forward(k, chunks, T, at_unit, up_done):
                with act.Fori(0, chunks // 2) as i:
                    for s in range(2):
                        next_hi(i * 2 + (at_unit + s), s)
                        act.wait_ge(up_taken[k], i * 2 + (up_done + (s + 1)))
                        f(tmp[:, s, 0:T], psA[:, 2 * s, 0:T], ACT.Silu).then_inc(up_silu[k], 1)

            def down_his(chunks, at_unit, turns, square_x=False):
                def pair(i, square_x, first):
                    for s in range(2):
                        next_hi(i * 2 + (at_unit + (chunks + s)), s)
                        if square_x:
                            act.wait_ge(down_taken[1], i * 2 + (s + 3))
                            square(2, i * 2 + s, s, TOK, first)

                if square_x:
                    pair(0, True, True)
                with act.Fori(1 if square_x else 0, turns) as i:
                    pair(i, square_x, False)

            for l in range(DEPTH):
                T = blocks_of(l) * P
                norm(2 * l, TOK)
                for u in range(MIX_UNITS):
                    s = u % 2
                    next_hi(first_mix[l] + u, s)
                    func = ACT.Gelu_apprx_tanh if u < 2 else ACT.Silu if u * UC == COL_RG else ACT.Copy
                    n = mix_blocks(l, u)
                    f(mix[:, 0:n, u * UC:(u + 1) * UC], psA[:, 2 * s:2 * s + n // 2, :].rearrange("p a (b n) -> p (a b) n", n=UC),
                      func).then_inc(mix_taken[l], 1)
                    if u == AFTER_V:
                        root(l * ROOTS + ROOT_V, stat[:, 0, 0:T // P * NH])
                    if u in (AFTER_W, AFTER_G):
                        root(l * ROOTS + (ROOT_W if u == AFTER_W else ROOT_G), stat[:, 0, 0:T // P * NH + NBLK * 2])
                place_heads(l, 0, 6)
                attention(l, 0)
                place_heads(l, 1, 6)
                attention(l, 1)
                place_heads(l, 2, 8)
                root(l * ROOTS + ROOT_GN, stat[:, 0, 0:T // P * NH])

                def two_groups(i, first):
                    for j in range(2 * GROUP_UNITS):
                        g, u = divmod(j, GROUP_UNITS)
                        if first and j == GATES_FIRST:
                            for c in range(KC):
                                act.wait_ge(br_turned[l], c + 1)
                                f(brhi[:, c, 0:T], psA[:, c % 4, 0:T], ACT.Copy).then_inc(br_hi[l], 1)
                        next_hi(i * (2 * GROUP_UNITS) + (first_group[l] + j), j % 2)
                        if u == 0:
                            act.wait_ge(gates_used[l], i * 2 + (g + 1))
                        if u < NBR:
                            f(gates[:, u, :, 0:T], psA[:, 2 * (u % 2):2 * (u % 2) + 2, 0:T], ACT.Sigmoid).then_inc(gates_taken[l], 1)

                two_groups(0, True)
                with act.Fori(1, GROUPS // 2) as i:
                    two_groups(i, False)
                if l:
                    act.wait_ge(w_used, first_out[l])
                    act.dma_start(rw[:], t["router_w"][0].rearrange("(c p) e -> p c e", p=P)).then_inc(router_landed, 16)
                    act.dma_start(rb[:], t["router_b"].broadcast_to([P, NEXP])).then_inc(router_landed, 16)
                    act.dma_start(eidx[:], t["k_eidx"]).then_inc(router_landed, 16)
                    act.dma_start(pick[:], t["k_pick"]).then_inc(router_landed, 16)
                    act.dma_start(before[:], t["k_before"]).then_inc(router_landed, 16)
                    act.dma_start(slots[:], t["k_slots"]).then_inc(router_landed, 16)
                    act.dma_start(slot_of[:], t["k_idx"]).then_inc(router_landed, 16)
                for u in range(OUT_UNITS):
                    if l == 0 or u < OUT_UNITS - 2:
                        next_hi(first_out[l] + u, u % 2)
                    act.wait_ge(out_taken[l], u + 3)
                    for c in (2 * u, 2 * u + 1):
                        square(2 * l + 1, c, c % 2, T, u == 0)
                norm(2 * l + 1, T)
                if l == 0:
                    for k, chunks in enumerate(FFN_PARTS):
                        feed_forward(k, chunks, T, first_part[k], 0)
                        down_his(chunks, first_part[k], KC // 2, k == 1)
                else:
                    act.wait_ge(gap_ready, 1)
                    f(stat[:, 0, 4:6], stat[:, 0, 2:4], ACT.Exp).then_inc(gap_exp, 1)
                    for n in range(2 * LBLK):
                        act.wait_ge(tok_turned, n + 1)
                        f(tokhi[:, n // 2, (n % 2) * 512:(n % 2 + 1) * 512], psA[:, n, :], ACT.Copy).then_inc(tok_hi, 1)

                    def ehi_part(e, u):
                        s_ = u % RING
                        for h in UPPER_FIRST:
                            act.wait_ge(eraw_landed[s_][h], e * (16 * GU // RING) + 16 * (u // RING + 1))
                            part = slice(h * HALF, (h + 1) * HALF)
                            f(ehi[:, s_, part], eraw[:, s_, part], ACT.Copy).then_inc(ehi_ready, 1)

                    for u in range(RING):
                        ehi_part(0, u)
                    act.wait_ge(most_ready, 1)
                    fullest = act.value_load(most_i[0:1, 0:1], min_val=0, max_val=SEQ)

                    def place_up(e, i):
                        act.wait_ge(eup_turned, e * UPS + (i + 1))
                        f(eupT_hi[:, 2 * i:2 * i + 2, :].rearrange("p c n -> p (c n)"), psA[:, 2, 0:2 * P], ACT.Copy).then_inc(eupT_hi_ready, 1)

                    def place_gathered(half, n):
                        act.wait_ge(gathered, n * 2 + (half + 1))
                        f((ghi, glo)[half][:].rearrange("p c n -> p (c n)"), psB[:, 0:2, :].rearrange("p a n -> p (a n)"),
                          ACT.Copy).then_inc(gathered_placed, 1)

                    def gathered_expert(e):
                        first = isinstance(e, int) and e == 0
                        final = isinstance(e, int) and e == NEXP - 1
                        for u in range(GU):
                            i, which = divmod(u, 2)
                            act.wait_ge(ew_used, e * GU + (u + 1))
                            if u < 2 * UPS and not which:
                                if not (first and i < 2):
                                    act.wait_ge(eup_ready, e * UPS + (i - 1))
                                f(tmp[:, i % 2, 0:UC], psA[:, 0, 0:UC], ACT.Silu).then_inc(eup_silu, 1)
                            if not (final and u + RING >= GU):
                                ehi_part(e, u + RING)
                            if u < 2 * UPS and which and i:
                                place_up(e, i - 1)
                            if first and u in (4, 8):
                                half = u // 4 - 1
                                act.wait_ge(pos_spread, half + 1)
                                f(posB[:, 4 * half:4 * half + 4].rearrange("p e n -> p (e n)"),
                                  psB[:, 2:4, :].rearrange("p a n -> p (a n)"), ACT.Copy).then_inc(pos_placed, 1)
                            if u == 2 * UPS + 1:
                                place_up(e, UPS - 1)
                            j = u - 2 * UPS
                            if j in (1, 2) and not final:
                                place_gathered(j - 1, e + 1)
                        act.wait_ge(cw_placed, e + 1)
                        c = cw[:, e:e + 1] if isinstance(e, int) else cw[:, ds(e, 1)]
                        f(yhi[:], psB[:, 2:4, :].rearrange("p a n -> p (a n)"), ACT.Copy, scale=c).then_inc(y_hi_ready, 1)

                    with act.If(fullest < P + 1):
                        for half in range(2):
                            place_gathered(half, 0)
                        gathered_expert(0)
                        with act.Fori(1, NEXP - 1) as e:
                            gathered_expert(e)
                        gathered_expert(NEXP - 1)
                    with act.Else():
                        act.wait_ge(comb_spread, 1)
                        f(combB[:].rearrange("p e n -> p (e n)"), psA[:].rearrange("p a n -> p (a n)"), ACT.Copy).then_inc(comb_spread, 1)
                        for s in range(2):
                            hi_part(first_exp + s, s)
                        with act.Fori(0, NEXP - 1) as e:
                            feed_forward(2, EXP_CHUNKS, T, e * EXP_UNITS + first_exp, e * EXP_CHUNKS)
                            down_his(EXP_CHUNKS, e * EXP_UNITS + first_exp, KC // 2)
                        e = NEXP - 1
                        feed_forward(2, EXP_CHUNKS, T, e * EXP_UNITS + first_exp, e * EXP_CHUNKS)
                        down_his(EXP_CHUNKS, e * EXP_UNITS + first_exp, KC // 2 - 1)

        @block.vector
        def _(dve):
            step = Steps(dve, dve_step)
            V = nc.vector

            def tt(out, a, b, op):
                return V.tensor_tensor(out, a, b, op)

            def lo_part(n, slot):
                for k, h in enumerate(UPPER_FIRST):
                    dve.wait_ge(hi_ready, n * 2 + (k + 1))
                    part = slice(h * HALF, (h + 1) * HALF)
                    tt(wlo[:, slot, part], raw[:, slot, part], whi[:, slot, part].bitcast(F32), ALU.subtract).then_inc(lo_ready, 1)

            def split(hi, lo, x):
                step(V.tensor_copy(hi, x))
                return tt(lo, x, hi.bitcast(F32), ALU.subtract)

            V.memset(ones[:], 1.0 / D).then_inc(ones_set, 1)
            for l in range(DEPTH):
                dve.sem_inc(gates_used[l], 1)
                dve.sem_inc(proj_taken[l], NBR)
                dve.sem_inc(out_taken[l], 2)
            for k in range(3):
                dve.sem_inc(up_taken[k], 2)
                dve.sem_inc(down_taken[k], 2)
            dve.wait_ge(setup_turned, 1)
            V.tensor_copy(rowsT[:], psB[:, 0, P:P + 24])
            V.tensor_copy(vecT[:], psB[:, 0, 0:P]).then_inc(setup_copied, 1)
            dve.wait_ge(setup_copied, 1)
            modcols = mod[:].rearrange("p l s c w -> p (l s c) w")

            def copy_rows(n, where, bank):
                V.tensor_copy(modrows[where][:, n % 2 if isinstance(n, int) else 0, :], bank).then_inc(mod_copied, 1)

            def add_bias(n, bank):
                dve.wait_ge(mod_turned, n + 1)
                part = slice(4 * n, 4 * n + 4) if isinstance(n, int) else ds(n * 4, 4)
                tt(modcols[:, part, :], bank[:, 0:8].rearrange("p (n w) -> p n w", w=2),
                   vecT[:, part].unsqueeze(2).broadcast_to([P, 4, 2]), ALU.add).then_inc(mod_added, 1)

            def scales(l, second):
                dve.wait_ge(mod_added, l * MOD_GROUPS + (MOD_GROUPS if second else EARLY_GROUPS))
                w = vecT[:, 96 + 16 * second + 8 * l:96 + 16 * second + 8 * l + 8].unsqueeze(2).broadcast_to([P, KC, 2])
                step(V.tensor_scalar(gsc[:, l, second], mod[:, l, SC2 if second else SC1], 1.0, None, ALU.add))
                step(tt(gsc[:, l, second], gsc[:, l, second], w, ALU.mult))

            def mod_group(g):
                dve.wait_ge(mod_used, 2 * g + 2)
                if g >= 2:
                    dve.wait_ge(mod_turned, g - 1)
                copy_rows(g, 0, psB[0:2, 2 + g % 2, :])
                if g:
                    add_bias(g - 1, psB[:, 1])

            dve.wait_ge(silu_ready, 1)
            step(V.tensor_copy(siluc4[:, :, 0:2], siluc[:]))
            tt(siluc4[:, :, 2:4], siluc[:], siluc4[:, :, 0:2].bitcast(F32), ALU.subtract)
            tt(fold[:], ident[0:4, 0:2], ident[0:4, 2:4], ALU.add)
            mod_group(0)
            mod_group(1)
            for c in range(KC):
                dve.wait_ge(x_turned, c + 1)
                V.tensor_copy(xT[:, c, :], psA[:, c % 4, :]).then_inc(x_placed, 1)
            dve.wait_ge(lg_landed, loaded(lg_landed))
            step(V.tensor_scalar(lgx[:, 1, :], lgx[:, 0, :], -1.0, None, ALU.mult))
            tt(lgx[:, 1, :], lgx[:, 0, :], lgx[:, 1, :], ALU.max).then_inc(lg_ready, 1)
            mod_group(2)
            dve.wait_ge(lg_steps, 1)
            step(V.tensor_scalar(lgx[:, 0, :], lgx[:, 0, :], 0.0, None, ALU.min))
            tt(lgx[:, 2, :], lgx[:, 0, :], lgx[:, 1, :], ALU.subtract).then_inc(lg_ready, 1)
            for n in range(DEPTH * NH):
                l, hd = divmod(n, NH)
                dve.wait_ge(decay_exp, n + 1)
                step(tt(tmp[:, n % 2, 0:2 * P].rearrange("p (d n) -> p d n", d=2), tmp[:, n % 2, 0:2 * P].rearrange("p (d n) -> p d n", d=2),
                        rel[:, 2:4, :], ALU.mult))
                tt(decay[:, l, hd, :], tmp[:, n % 2, 0:P], tmp[:, n % 2, P:2 * P], ALU.add).then_inc(decay_used, 1)
            dve.wait_ge(lg_steps, 2)
            for k, d in ((1, 0), (2, 1)):
                for l in range(DEPTH):
                    step(V.tensor_scalar(expcol[:, k, l, d, :], expcol[:, k, l, d, :], SCALE, None, ALU.mult))
            lo_part(0, 0)
            mod_group(3)
            lo_part(1, 1)
            add_bias(EARLY_GROUPS - 1, psB[:, 1])
            scales(0, 0)
            dve.wait_ge(inputs_landed, loaded(inputs_landed))
            V.tensor_scalar(nsink[:], sink[:], -1.0, None, ALU.mult)

            def norm(k, T):
                l, second = divmod(k, 2)
                nb = T // P
                rinv = stat[:, 0, 0:nb]
                dve.wait_ge(meansq, k * KC + KC)
                V.tensor_scalar(rinv, psB[:, 0, 0:nb], EPS, None, ALU.add).then_inc(ms_ready, 1)
                dve.wait_ge(root_ready, l * ROOTS + (NORM2 if second else NORM1) + 1)
                step(V.reciprocal(rinv, rinv))
                for b in range(nb):
                    last = V.tensor_scalar(tmp[:, 1, b * P:(b + 1) * P], ident[:], stat[:, 0, b:b + 1], float(D), ALU.mult, ALU.mult)
                last.then_inc(spread_ready, 1)
                dve.wait_ge(rinv_spread, k + 1)

                def scaled(c):
                    for w in range(T // SEQ):
                        part = slice(w * SEQ, (w + 1) * SEQ)
                        last = V.scalar_tensor_tensor(out=hf[:, c, part], in0=xT[:, c, part], scalar=gsc[:, l, second, c, w:w + 1],
                                                      in1=psB[:, 1, part], op0=ALU.mult, op1=ALU.mult)
                    last.then_inc(xn_ready, 1)

                def low(c):
                    dve.wait_ge(h_ready, k * KC + c + 1)
                    for w in range(T // SEQ):
                        part = slice(w * SEQ, (w + 1) * SEQ)
                        hi = hhi[:, c, part].bitcast(F32)
                        if k == 2 * DEPTH - 1:
                            last = tt(hlo[:, c, part], hf[:, c, part], hi, ALU.subtract)
                        else:
                            last = V.scalar_tensor_tensor(out=hlo[:, c, part], in0=hf[:, c, part],
                                                          scalar=mod[:, l, SH2 if second else SH1, c, w:w + 1], in1=hi,
                                                          op0=ALU.add, op1=ALU.subtract)
                    last.then_inc(h_split, 1)

                for c in range(KC + 2):
                    if c < KC:
                        scaled(c)
                    if c >= 2:
                        low(c - 2)

            def heads_view(col, heads, nb=NBLK):
                return mix[:, 0:nb, col:col + heads * HD].rearrange("p b (h d) -> p b h d", d=HD)

            def per_head(a, nb, heads, n=HD):
                if a.shape[1] == heads and nb * heads != heads:
                    return a.unsqueeze(1).unsqueeze(3).broadcast_to([P, nb, heads, n])
                return a.rearrange("p (b h) -> p b h", b=nb).unsqueeze(3).broadcast_to([P, nb, heads, n])

            def rms(parts, root):
                n, views = 0, []
                for col, heads, nb in parts:
                    x = heads_view(col, heads, nb)
                    last = tt(scrA[:, n * HD:(n + nb * heads) * HD].rearrange("p (b h d) -> p b h d", b=nb, d=HD), x, x, ALU.mult)
                    views.append((x, stat[:, 0, n:n + nb * heads], nb, heads))
                    n += nb * heads
                step(last)
                step(V.tensor_reduce(stat[:, 0, 0:n], scrA[:, 0:n * HD].rearrange("p (n d) -> p n d", d=HD), AX_X, ALU.add))
                V.tensor_scalar(stat[:, 0, 0:n], stat[:, 0, 0:n], 1.0 / HD, EPS, ALU.mult, ALU.add).then_inc(ms_ready, 1)
                dve.wait_ge(root_ready, root + 1)
                step(V.reciprocal(stat[:, 0, 0:n], stat[:, 0, 0:n]))
                for x, r, nb, heads in views:
                    last = tt(x, x, per_head(r, nb, heads), ALU.mult)
                step(last)

            def rope(col, heads, table, nb):
                x = mix[:, 0:nb, col:col + heads * HD].rearrange("p b (h t d) -> p b h t d", t=2, d=HD // 2)
                x1, x2 = x[:, :, :, 0, :], x[:, :, :, 1, :]
                cos, sin = (table[:, k, 0:nb, :].unsqueeze(2).broadcast_to([P, nb, heads, HD // 2]) for k in range(2))
                n = nb * heads * HD // 2
                a, b = (s[:, 0:n].rearrange("p (b h d) -> p b h d", b=nb, h=heads) for s in (scrA, scrB))
                tt(a, x1, sin, ALU.mult)
                step(tt(b, x2, sin, ALU.mult))
                tt(x1, x1, cos, ALU.mult)
                step(tt(x2, x2, cos, ALU.mult))
                tt(x1, x1, b, ALU.subtract)
                return tt(x2, x2, a, ALU.add)

            def attention_heads(l, m, col, root):
                nb = blocks_of(l)
                parts = ((col, NH, nb), (col + NH * HD, 2, NBLK))
                rms([(col, 6, NBLK)] if nb == NBLK else parts, l * ROOTS + root)
                for k, (c, heads, blocks) in enumerate(parts):
                    x = heads_view(c, heads, blocks)
                    wt = qkw[:, l, 2 * m + k, :].unsqueeze(1).unsqueeze(1).broadcast_to([P, blocks, heads, HD])
                    last = tt(x, x, wt, ALU.mult)
                step(last)
                rope(col, 6, axial, LBLK).then_inc(heads_ready, 1)

            def half_low(l, x):
                dve.wait_ge(modh_hi, l * HALVES + x + 1)
                tt(half_lo[x % HALF_RING][:], half_raw[x % HALF_RING][:], high_place(l, x).bitcast(F32), ALU.subtract).then_inc(modh_lo, 1)

            def attention(l, m):
                items = attention_items(l)
                n = len(items)
                per = HALVES // (2 * n)
                if m == 0:
                    half_low(l, 0)
                    half_low(l, 1)
                groups = l * MOD_GROUPS + EARLY_GROUPS + m * HALVES // 8

                def lows(t_):
                    for x in halves_ahead(m, t_ - 1, per):
                        half_low(l, x)

                for t_ in range(n + 2):
                    if t_ < n:
                        i = t_
                        hd, b, k0, nk = items[i]
                        dve.wait_ge(scores_ready, items_before(l, m) + i + 1)
                        s = psB[:, i % 2, 0:nk]
                        if m == 0 and b < LBLK:
                            other = psB[:, i % 2, (1 - b) * P:(2 - b) * P]
                            step(tt(other, other, wmask[:, b, :], ALU.add))
                        step(V.tensor_reduce(negmax[:, i:i + 1], s, AX_X, ALU.max))
                        if m == 0:
                            V.tensor_scalar(negmax[:, i:i + 1], negmax[:, i:i + 1], -SCALE, nsink[:, l * NH + hd:l * NH + hd + 1],
                                            ALU.mult, ALU.min).then_inc(max_ready, 1)
                        else:
                            V.tensor_scalar(negmax[:, i:i + 1], negmax[:, i:i + 1], -SCALE, None, ALU.mult).then_inc(max_ready, 1)
                    if 1 <= t_ <= n:
                        lows(t_)
                    if t_ >= 2:
                        i = t_ - 2
                        hd, b, k0, nk = items[i]
                        dve.wait_ge(values_ready, items_before(l, m) + i + 1)
                        if m == 0:
                            step(tt(rowsum[:, i:i + 1], rowsum[:, i:i + 1], sinkexp[:, i:i + 1], ALU.add))
                        step(V.reciprocal(rowsum[:, i:i + 1], rowsum[:, i:i + 1]))
                        col = OUT_COLS[m + 1] + hd * HD
                        V.tensor_scalar(mix[:, b, col:col + HD], psB[:, 2 + i % 2, 0:HD], rowsum[:, i:i + 1], None,
                                        ALU.mult).then_inc(attn_done, 1)
                    done = (t_ + 1) * per
                    if t_ < n and done % 4 == 0:
                        g = groups + done // 4 - 1
                        if g > groups:
                            add_bias(g - 1, psA[:, 3])
                        dve.wait_ge(modh_used, l * HALVES + m * HALVES // 2 + done)
                        copy_rows(g, 1, psA[0:4, 2, :])
                add_bias(groups + HALVES // 8 - 1, psA[:, 3])

            def retention(l):
                nb = blocks_of(l)
                k = heads_view(COL_RK, NH)
                for d, e in enumerate((1, 2)):
                    kd = kdec[:, d].rearrange("p b (h d) -> p b h d", d=HD)
                    last = tt(kd, k, per_head(expcol[:, e, l, d, :], NBLK, NH), ALU.mult)
                last.then_inc(kdec_ready, 1)
                dve.wait_ge(kv_ready, l + 1)
                for d, state in enumerate((stateF, stateB)):
                    cd = expcol[0:HD, 3, l, d, :].unsqueeze(2).broadcast_to([HD, NH, HD])
                    kv = psB[0:HD, 2 * d:2 * d + 2, :].rearrange("p a (b n) -> p (a b) n", b=2)
                    step(V.tensor_copy(state[:, 0, :], kv[:, 0, :]))
                    for n in (1, 2):
                        new, old = (state[:, x, :].rearrange("p (h d) -> p h d", h=NH) for x in (n, n - 1))
                        step(tt(new, old, cd, ALU.mult))
                        step(tt(state[:, n, :], state[:, n, :], kv[:, n, :], ALU.add))
                dve.sem_inc(states_ready, 1)

                def decayed(b):
                    dve.wait_ge(qk_ready[l], b + 1)
                    if b >= 2:
                        dve.wait_ge(ret_ready[l], b - 1)
                    tt(expS[:, b % 2, :], psA[:, b % 2, :], decay[:, l].rearrange("p h n -> p (h n)"), ALU.mult).then_inc(qk_decayed[l], 1)

                decayed(0)
                for b in range(nb):
                    if b + 1 < nb:
                        decayed(b + 1)
                    dve.wait_ge(ret_ready[l], b + 1)
                    inter = [psB[:, b % 2, d * 256:(d + 1) * 256].rearrange("p (h d) -> p h d", h=NH) for d in range(2)]
                    o = mix[:, b, COL_RQ:COL_RQ + 256]
                    terms = [psA[:, 2 + b % 2, 0:256]]
                    for d, skip in enumerate((2, 3)):
                        if b != skip:
                            scr = (scrA, scrB)[d][:, (b % 3) * 256:(b % 3 + 1) * 256]
                            last = tt(scr.rearrange("p (h d) -> p h d", h=NH), inter[d],
                                      expcol[:, d, l, d, :].unsqueeze(2).broadcast_to([P, NH, HD]), ALU.mult)
                            terms.append(scr)
                    step(last)
                    last = tt(o, terms[0], terms[1], ALU.add)
                    if len(terms) > 2:
                        step(last)
                        last = tt(o, o, terms[2], ALU.add)
                    last.then_inc(ret_taken[l], 1)
                dve.wait_ge(ret_taken[l], nb)
                x, n = heads_view(COL_RQ, NH, nb), nb * NH
                flat = mix[:, 0:nb, COL_RQ:COL_RQ + NH * HD]
                sq = scrA[:, 0:n * HD].rearrange("p (b h d) -> p b h d", b=nb, d=HD)
                step(V.tensor_reduce(stat[:, 1, 0:n].rearrange("p (b h) -> p b h", b=nb), x, AX_X, ALU.add))
                step(V.tensor_scalar(stat[:, 1, 0:n], stat[:, 1, 0:n], 1.0 / HD, None, ALU.mult))
                step(tt(x, x, per_head(stat[:, 1, 0:n], nb, NH), ALU.subtract))
                step(tt(sq, x, x, ALU.mult))
                step(V.tensor_reduce(stat[:, 0, 0:n], scrA[:, 0:n * HD].rearrange("p (n d) -> p n d", d=HD), AX_X, ALU.add))
                V.tensor_scalar(stat[:, 0, 0:n], stat[:, 0, 0:n], 1.0 / HD, EPS, ALU.mult, ALU.add).then_inc(ms_ready, 1)
                dve.wait_ge(root_ready, l * ROOTS + ROOT_GN + 1)
                step(V.reciprocal(stat[:, 0, 0:n], stat[:, 0, 0:n]))
                step(tt(x, x, per_head(stat[:, 0, 0:n], nb, NH), ALU.mult))
                step(tt(flat, flat, gn[:, l, :].unsqueeze(1).broadcast_to([P, nb, NH * HD]), ALU.mult))
                tt(flat, flat, mix[:, 0:nb, COL_RG:COL_RG + NH * HD], ALU.mult).then_inc(branches_ready, 1)

            def add_to_x(l, gate, oc, bank, T):
                for w in range(T // SEQ):
                    x = xT[:, oc, w * SEQ:(w + 1) * SEQ] if isinstance(oc, int) else \
                        xT[:, ds(oc, 1), w * SEQ:(w + 1) * SEQ].rearrange("p o n -> p (o n)")
                    g = mod[:, l, gate, oc, w:w + 1] if isinstance(oc, int) else \
                        mod[:, l, gate, ds(oc, 1), w:w + 1].rearrange("p o n -> p (o n)")
                    last = V.scalar_tensor_tensor(out=x, in0=bank[:, w * SEQ:(w + 1) * SEQ], scalar=g, in1=x,
                                                  op0=ALU.mult, op1=ALU.add)
                return last

            def next_lo(n, slot):
                lo_part(n + 2, slot)

            UP_STEPS = 2

            def ups(k, chunks, T, at_unit, up_done, turns_done):
                with dve.Fori(0, chunks // 2) as i:
                    step.loop(turns_done + i, 2 * UP_STEPS)
                    for s in range(2):
                        next_lo(i * 2 + (at_unit + s), s)
                        dve.wait_ge(up_silu[k], i * 2 + (up_done + (s + 1)))
                        x = tmp[:, s, 0:T]
                        step(tt(x, x, psA[:, 2 * s + 1, 0:T], ALU.mult))
                        split(hidhi[:, ds(i * (2 * T) + s * T, T)], hidlo[:, ds(i * (2 * T) + s * T, T)], x).then_inc(up_taken[k], 1)

            for l in range(DEPTH):
                T = blocks_of(l) * P
                norm(2 * l, TOK)
                nb = T // P
                for u in range(MIX_UNITS):
                    next_lo(first_mix[l] + u, u % 2)
                    if u in (AFTER_V, AFTER_W, AFTER_G, AFTER_R):
                        dve.wait_ge(mix_taken[l], u + 3)
                    if u == AFTER_V:
                        rms([(COL_V, NH, nb)], l * ROOTS + ROOT_V)
                        v = mix[:, 0:nb, COL_V:COL_V + NH * HD]
                        tt(v, v, gv[:, l, :].unsqueeze(1).broadcast_to([P, nb, NH * HD]), ALU.mult).then_inc(v_normed, 1)
                        dve.wait_ge(ws_turned, l + 1)
                        V.tensor_copy(wsT[:].rearrange("p g n -> p (g n)"), psB[:, 0, :]).then_inc(ws_copied, 1)
                    elif u == AFTER_W:
                        attention_heads(l, 0, COL_WQ, ROOT_W)
                    elif u == AFTER_W + 1:
                        dve.wait_ge(mlp_mixed, l + 1)
                        for g in range(NH):
                            x = mix[:, 0:nb, COL_U + g * HD:COL_U + (g + 1) * HD]
                            mixed = psB[:, 1 + g // 2, (g % 2) * 256:(g % 2) * 256 + nb * HD].rearrange("p (b d) -> p b d", d=HD)
                            last = V.scalar_tensor_tensor(out=x, in0=mixed, scalar=rowsT[:, 16 + l * NH + g:17 + l * NH + g], in1=x,
                                                          op0=ALU.add, op1=ALU.mult)
                        last.then_inc(mlp_done, 1)
                    elif u == AFTER_G:
                        dve.wait_ge(heads_ready, 3 * l + 1)
                        attention_heads(l, 1, COL_GQ, ROOT_G)
                    elif u == AFTER_R:
                        dve.wait_ge(heads_ready, 3 * l + 2)
                        step(rope(COL_RQ, NH, rot, nb))
                        rope(COL_RK, NH, rot, NBLK).then_inc(heads_ready, 1)
                attention(l, 0)
                attention(l, 1)
                scales(l, 1)
                dve.wait_ge(attn_done, items_before(l, 1) + len(attention_items(l)))
                dve.wait_ge(heads_ready, 3 * l + 3)
                retention(l)
                STEPS = 4 * NBR
                READY = 2 * NBR - 1
                total, new = tmp[:, 0, 0:T], tmp[:, 1, 0:T]

                def two_groups(i, first):
                    for j in range(2 * GROUP_UNITS):
                        g, u = divmod(j, GROUP_UNITS)
                        if first and j == GATES_FIRST:
                            for c in range(KC):
                                dve.wait_ge(br_hi[l], c + 1)
                                tt(brlo[:, c, 0:T], psA[:, c % 4, 0:T], brhi[:, c, 0:T].bitcast(F32), ALU.subtract).then_inc(br_lo[l], 1)
                        n = i * (2 * GROUP_UNITS) + (first_group[l] + j)
                        if u < NBR:
                            next_lo(n, j % 2)
                            continue
                        for c in range(2):
                            for br in range(NBR):
                                if (c, br) == (1, NBR - 1):
                                    dve.wait_ge(w_used, n + 1)
                                    next_lo(n, j % 2)
                                else:
                                    dve.wait_ge(proj_ready[l], i * (2 * READY) + (g * READY + c * NBR + br + 1))
                                if (c, br) == (0, 0):
                                    dve.wait_ge(gates_taken[l], i * (2 * NBR) + ((g + 1) * NBR + 2))
                                out = total if br == 0 else new
                                ins = tt(out, psB[:, br, 0:T], gates[:, br, c, 0:T], ALU.mult)
                                ins.then_inc(proj_taken[l], 1)
                                dve.wait_ge(proj_taken[l], i * (4 * NBR) + ((2 * g + c) * NBR + br + 1 + NBR))
                                if br:
                                    step(tt(total, total, new, ALU.add))
                            oc = i * (2 * UC // P) + (g * 2 + c)
                            hi, lo = (a[:, ds(oc, 1), 0:T].rearrange("p o n -> p (o n)") for a in (acchi, acclo))
                            step(V.tensor_copy(hi, total))
                            tt(lo, total, hi.bitcast(F32), ALU.subtract).then_inc(acc_ready[l], 1)
                            dve.wait_ge(acc_ready[l], i * (2 * UC // P) + (g * 2 + c + 1))
                        dve.sem_inc(gates_used[l], 1)

                two_groups(0, True)
                with dve.Fori(1, GROUPS // 2) as i:
                    step.loop(i - 1, STEPS)
                    two_groups(i, False)
                step.end(GROUPS // 2 - 1, STEPS)
                def out_pair(i, more):
                    for s in range(2):
                        n = i * 2 + (first_out[l] + s)
                        if more:
                            next_lo(n, s)
                        dve.wait_ge(w_used, n + 1)
                        for j in range(2):
                            last = add_to_x(l, G1, i * 4 + (2 * s + j), psA[:, 2 * s + j], T)
                        last.then_inc(out_taken[l], 1)

                with dve.Fori(0, OUT_UNITS // 2 - l) as i:
                    out_pair(i, True)
                if l:
                    out_pair(OUT_UNITS // 2 - 1, False)
                norm(2 * l + 1, T)
                if l == 0:
                    for k, chunks in enumerate(FFN_PARTS):
                        ups(k, chunks, T, first_part[k], 0, 0)
                        step.end(chunks // 2, 2 * UP_STEPS)
                        with dve.Fori(0, KC // 2) as i:
                            for s in range(2):
                                n = i * 2 + (first_part[k] + chunks + s)
                                next_lo(n, s)
                                dve.wait_ge(w_used, n + 1)
                                add_to_x(0, G2, i * 2 + s, psA[:, 2 * s], T).then_inc(down_taken[k], 1)
                                if k == 0 and s == 0:
                                    dve.wait_ge(modf_used, i * 2 + 2)
                                    copy_rows(i + MOD_GROUPS, 2, psB[0:2, 2, :])
                                elif k == 0:
                                    add_bias(i + MOD_GROUPS, psB[:, 1])
                        dve.wait_ge(down_taken[k], KC + 2)
                    scales(1, 0)
                    continue
                dve.wait_ge(router_landed, 16 * 7)
                dve.wait_ge(router_ready, 1)
                R = [rout[:, k] for k in range(12)]
                spread = [P, LBLK, NEXP]
                def over(col):
                    return stat[:, 0, col:col + LBLK].unsqueeze(2).broadcast_to(spread)
                step(tt(R[1], psB[:, 0, 0:LBLK * NEXP].rearrange("p (b e) -> p b e", b=LBLK),
                        rb[:].unsqueeze(1).broadcast_to(spread), ALU.add))
                for n, logits in enumerate((R[1], R[5])):
                    top = (8, 10)[n]
                    step(V.tensor_reduce(stat[:, 0, top:top + LBLK], logits, AX_X, ALU.max))
                    step(tt(R[2], logits, over(top), ALU.is_equal))
                    step(V.scalar_tensor_tensor(out=R[3], in0=R[2], scalar=-float(NEXP), in1=eidx[:].unsqueeze(1).broadcast_to(spread),
                                                op0=ALU.mult, op1=ALU.add))
                    step(V.tensor_reduce(stat[:, 0, 12:14], R[3], AX_X, ALU.min))
                    step(tt(R[6 + n], R[3], over(12), ALU.is_equal))
                    if n == 0:
                        step(V.scalar_tensor_tensor(out=R[5], in0=R[6], scalar=-BIG, in1=R[1], op0=ALU.mult, op1=ALU.add))
                tt(stat[:, 0, 2:4], stat[:, 0, 10:12], stat[:, 0, 8:10], ALU.subtract).then_inc(gap_ready, 1)
                dve.wait_ge(gap_exp, 1)
                step(V.tensor_scalar(stat[:, 0, 6:8], stat[:, 0, 4:6], 1.0, None, ALU.add))
                step(V.reciprocal(stat[:, 0, 6:8], stat[:, 0, 6:8]))
                step(tt(R[0], R[7], over(4), ALU.mult))
                step(tt(R[0], R[0], R[6], ALU.add))
                step(tt(R[0], R[0], over(6), ALU.mult))
                tt(R[8], R[6], R[7], ALU.add).then_inc(mask_ready, 1)
                dve.wait_ge(counted, 1)
                step(V.scalar_tensor_tensor(out=R[9], in0=psB[:, 1, 16:16 + LBLK * NEXP].rearrange("p (b e) -> p b e", b=LBLK),
                                            scalar=1.0, in1=R[8], op0=ALU.add, op1=ALU.mult))
                step(V.tensor_scalar(R[9], R[9], -1.0, None, ALU.add))
                step(V.tensor_reduce(most[:], psB[:, 1, 32:32 + NEXP], AX_X, ALU.max))
                V.tensor_copy(most_i[:], most[:]).then_inc(most_ready, 1)
                for n in range(2 * LBLK):
                    dve.wait_ge(tok_hi, n + 1)
                    part = slice((n % 2) * 512, (n % 2 + 1) * 512)
                    tt(toklo[:, n // 2, part], psA[:, n, :], tokhi[:, n // 2, part].bitcast(F32), ALU.subtract).then_inc(tok_lo, 1)
                dve.wait_ge(most_ready, 1)
                fullest = dve.value_load(most_i[0:1, 0:1], min_val=0, max_val=SEQ)

                def elo_part(e, u):
                    s_ = u % RING
                    for k, h in enumerate(UPPER_FIRST):
                        dve.wait_ge(ehi_ready, e * (2 * GU) + (2 * u + k + 1))
                        part = slice(h * HALF, (h + 1) * HALF)
                        tt(elo[:, s_, part], eraw[:, s_, part], ehi[:, s_, part].bitcast(F32), ALU.subtract).then_inc(elo_ready, 1)

                def build_gather(n):
                    for b in range(LBLK):
                        at_ = R[9][:, b, ds(n, 1)] if not isinstance(n, int) else R[9][:, b, n:n + 1]
                        last = V.tensor_scalar(gat[:, b, :], slots[:], at_, None, ALU.is_equal)
                    last.then_inc(gat_ready, 1)

                def place_up_lo(e, i):
                    dve.wait_ge(eupT_hi_ready, e * UPS + (i + 1))
                    hi, lo = (a[:, 2 * i:2 * i + 2, :].rearrange("p c n -> p (c n)") for a in (eupT_hi, eupT_lo))
                    tt(lo, psA[:, 2, 0:2 * P], hi.bitcast(F32), ALU.subtract).then_inc(eupT_lo_ready, 1)

                def add_scattered(half, n):
                    dve.wait_ge(moe_zeroed, 1)
                    dve.wait_ge(scattered, n * 2 + (half + 1))
                    m = moe[:, 4 * half:4 * half + 4, :].rearrange("p c n -> p (c n)")
                    tt(m, m, psB[:, 0:2, :].rearrange("p a n -> p (a n)"), ALU.add).then_inc(scattered_added, 1)

                def weights_of_slots(n):
                    dve.wait_ge(cw_ready, n + 1)
                    c = cw[:, n:n + 1] if isinstance(n, int) else cw[:, ds(n, 1)]
                    V.tensor_copy(c, psA[:, 3, 0:1]).then_inc(cw_placed, 1)

                def gathered_expert(e):
                    first = isinstance(e, int) and e == 0
                    final = isinstance(e, int) and e == NEXP - 1
                    if not final:
                        dve.wait_ge(cw_ready, e + 1)
                        build_gather(e + 1)
                    for u in range(GU):
                        i, which = divmod(u, 2)
                        if u < 2 * UPS and which:
                            dve.wait_ge(eup_silu, e * UPS + (i + 1))
                            dve.wait_ge(ew_used, e * GU + (u + 1))
                            if not (first and i < 2):
                                dve.wait_ge(eup_turned, e * UPS + (i - 1))
                            tt(eup[:, i % 2, :], tmp[:, i % 2, 0:UC], psA[:, 1, 0:UC], ALU.mult).then_inc(eup_ready, 1)
                        if u == 2 * UPS - 1 and not first:
                            add_scattered(0, e - 1)
                        if u == 2 * UPS and not first:
                            add_scattered(1, e - 1)
                        if not (final and u + RING >= GU):
                            elo_part(e, u + RING)
                        if u < 2 * UPS and which and i:
                            place_up_lo(e, i - 1)
                        if u == 2 * UPS + 1:
                            place_up_lo(e, UPS - 1)
                        if u == 2 * UPS + 2 and not final:
                            weights_of_slots(e + 1)
                    if first:
                        dve.wait_ge(pos_placed, 2)
                    at_ = posB[:, e, :] if isinstance(e, int) else posB[:, ds(e, 1), :].rearrange("p o n -> p (o n)")
                    V.tensor_scalar(sca[:], at_, slot_of[:, 2:3], None, ALU.is_equal).then_inc(sca_ready, 1)
                    dve.wait_ge(y_hi_ready, e + 1)
                    c = cw[:, e:e + 1] if isinstance(e, int) else cw[:, ds(e, 1)]
                    V.scalar_tensor_tensor(out=ylo[:], in0=psB[:, 2:4, :].rearrange("p a n -> p (a n)"), scalar=c,
                                           in1=yhi[:].bitcast(F32), op0=ALU.mult, op1=ALU.subtract).then_inc(y_lo_ready, 1)

                with dve.If(fullest < P + 1):
                    dve.wait_ge(pos_turned, 1)
                    V.tensor_copy(combT[:], psB[0:NEXP, 2, 0:SEQ]).then_inc(pos_copied, 1)
                    build_gather(0)
                    for u in range(RING):
                        elo_part(0, u)
                    weights_of_slots(0)
                    gathered_expert(0)
                    with dve.Fori(1, NEXP - 1) as e:
                        gathered_expert(e)
                    gathered_expert(NEXP - 1)
                    for half in range(2):
                        add_scattered(half, NEXP - 1)
                    dve.wait_ge(scattered_added, 2 * NEXP)
                with dve.Else():
                    dve.wait_ge(ehi_ready, 2 * RING)
                    dve.wait_ge(combine_turned, 1)
                    V.tensor_copy(combT[:], psB[0:NEXP, 2, 0:SEQ]).then_inc(combine_copied, 1)
                    dve.wait_ge(comb_spread, 2)
                    dve.wait_ge(moe_zeroed, 1)
                    for s in range(2):
                        lo_part(first_exp + s, s)
                    start = step.n

                    def expert(e, last_turns):
                        at_unit = e * EXP_UNITS + first_exp
                        per = EXP_CHUNKS * UP_STEPS + KC
                        with dve.Fori(0, EXP_CHUNKS // 2) as i:
                            step.n, step.base = start, e * per + i * (2 * UP_STEPS)
                            for s in range(2):
                                next_lo(i * 2 + (at_unit + s), s)
                                dve.wait_ge(up_silu[2], i * 2 + (e * EXP_CHUNKS + (s + 1)))
                                x = tmp[:, s, 0:T]
                                step(tt(x, x, psA[:, 2 * s + 1, 0:T], ALU.mult))
                                split(hidhi[:, ds(i * (2 * T) + s * T, T)], hidlo[:, ds(i * (2 * T) + s * T, T)], x).then_inc(up_taken[2], 1)

                        def down_pair(i, more):
                            step.n, step.base = start, e * per + (i * 2 + EXP_CHUNKS * UP_STEPS)
                            for s in range(2):
                                n = i * 2 + (at_unit + (EXP_CHUNKS + s))
                                if more:
                                    next_lo(n, s)
                                dve.wait_ge(w_used, n + 1)
                                x = tmp[:, s, SEQ:2 * SEQ]
                                c = combB[:, ds(e, 1), :].rearrange("p o n -> p (o n)")
                                m = moe[:, ds(i * 2 + s, 1), :].rearrange("p o n -> p (o n)")
                                step(tt(x, psA[:, 2 * s, 0:T], c, ALU.mult))
                                tt(m, m, x, ALU.add).then_inc(down_taken[2], 1)

                        with dve.Fori(0, last_turns) as i:
                            down_pair(i, True)
                        if last_turns < KC // 2:
                            down_pair(last_turns, False)

                    with dve.Fori(0, NEXP - 1) as e:
                        expert(e, KC // 2)
                    expert(NEXP - 1, KC // 2 - 1)
                    dve.wait_ge(down_taken[2], NEXP * KC + 2)
                for c in range(KC):
                    V.scalar_tensor_tensor(out=xT[:, c, 0:T], in0=moe[:, c, :], scalar=mod[:, l, G2, c, 0:1], in1=xT[:, c, 0:T],
                                           op0=ALU.mult, op1=ALU.add).then_inc(x_final, 1)
            dve.wait_ge(x_final, KC)
            for c in range(KC):
                dve.wait_ge(out_turned, c + 1)
                V.tensor_copy(xrows[:, 0:LBLK, c * P:(c + 1) * P], psA[:, c % 4, 0:LBLK * P].rearrange("p (b n) -> p b n", n=P)).then_inc(out_placed, 1)


INPUTS = ("x", "c", "ctx", "c_ctx", "w_mod", "b_mod", "g_norm1", "g_norm2", "w_in", "mlp_g_v", "mlp_w_s", "mlp_b_s",
          "win_q_norm", "win_k_norm", "win_sink", "glb_q_norm", "glb_k_norm", "ret_decay", "ret_gn", "w_branch", "w_out",
          "ffn_w1", "ffn_w3", "ffn_w2", "router_w", "router_b", "moe_w1", "moe_w3", "moe_w2")
GRID_W = 64
ROPE_BASE = 10000.0


def shape_constants():
    f = np.float32
    i, j = np.arange(P, dtype=f)[:, None], np.arange(P, dtype=f)[None, :]
    wmask = np.stack([np.where(j <= i, f(0), f(-BIG)), np.where(j >= i, f(0), f(-BIG))], 1)
    rel = np.stack([np.maximum(j - i, 0), np.maximum(i - j - 1, 0), np.where(j >= i, SCALE, 0), np.where(i > j, SCALE, 0)], 1)
    idx = np.concatenate([i + 1, P - 1 - i, i, np.full_like(i, P)], 1)

    def by_block(ang):
        tab = np.stack([np.cos(ang), np.sin(ang)], 0).astype(f)
        return np.ascontiguousarray(tab.reshape(2, -1, P, HD // 2).transpose(2, 0, 1, 3))

    pos = np.arange(SEQ)
    inv = (ROPE_BASE ** (-np.arange(HD // 4, dtype=f) / f(HD // 4))).astype(f)
    axial = np.concatenate([(pos // GRID_W).astype(f)[:, None] * inv, (pos % GRID_W).astype(f)[:, None] * inv], 1)
    inv = (ROPE_BASE ** (-np.arange(HD // 2, dtype=f) / f(HD // 2))).astype(f)
    place = np.concatenate([CTX + np.arange(SEQ), np.arange(CTX)]).astype(f)
    pick = np.zeros((NEXP, NEXP, P), f)
    pick[np.arange(NEXP), np.arange(NEXP)] = 1
    return {"k_ident": np.eye(P, dtype=f), "k_wmask": wmask.astype(f), "k_rel": rel.astype(f), "k_idx": idx.astype(f),
            "k_axial": by_block(axial), "k_rot": by_block(place[:, None] * inv), "k_pick": pick,
            "k_before": np.stack([(i < j), np.ones((P, P), bool)], 1).astype(f), "k_slots": np.tile(j, (P, 1)), "k_eidx": np.tile(np.arange(NEXP, dtype=f), (P, 1))}


def kernel(**inputs):
    import concourse.bacc as bacc
    from concourse.bass_utils import run_bass_kernel_spmd

    nc = bacc.Bacc("TRN2", target_bir_lowering=False, num_devices=1)
    arrays = {name: np.ascontiguousarray(inputs[name]) for name in INPUTS}
    arrays.update(shape_constants())
    tensors = {name: nc.dram_tensor(name, a.shape, mybir.dt.from_np(a.dtype), kind="ExternalInput").ap()
               for name, a in arrays.items()}
    tensors["out"] = nc.dram_tensor("out", (1, SEQ, D), F32, kind="ExternalOutput").ap()
    build_program(nc, tensors)
    return run_bass_kernel_spmd(nc, [arrays], core_ids=[0]).results[0]["out"]
```
